# Optimizing a Trainium2 kernel written in Bass

```python
import math
import jax, jax.numpy as jnp
from jax import lax
import numpy as np

D_MODEL = 1024
BATCH = 1
SEQ = 512
DEPTH = 1
DEC_BATCH = 8
DEC_SEQ = 8
PAST_LEN = 2048
PAGE_SIZE = 128

N_MEM = 256
GLA_HEADS = 4
GLA_DV = D_MODEL // (2 * GLA_HEADS)
GLA_DK = GLA_DV // 2
GLA_GATE_RANK = 16
GLA_TAU = 16.0
GLA_CHUNK = 64
MLA_HEADS = 8
MLA_V = D_MODEL // (2 * MLA_HEADS)
MLA_NOPE = MLA_V
MLA_ROPE = MLA_V // 2
MLA_Q_RANK = 3 * D_MODEL // 8
MLA_KV_RANK = D_MODEL // 4
ROPE_THETA = 10000.0
Q_BLOCK = 128
X_HEADS = 4
X_DIM = D_MODEL // 8
D_FF = 4 * D_MODEL
EPS = 1e-6

GLA_WIDTH = GLA_HEADS * GLA_DV
MLA_WIDTH = MLA_HEADS * MLA_V
MIX_WIDTH = GLA_WIDTH + MLA_WIDTH
IN_SIZES = (GLA_HEADS * GLA_DK, GLA_HEADS * GLA_DK, GLA_WIDTH, GLA_WIDTH, GLA_GATE_RANK,
            MLA_Q_RANK, MLA_KV_RANK, MLA_ROPE)
SPLIT_POINTS = tuple(int(v) for v in np.cumsum(IN_SIZES)[:-1])
D_IN = sum(IN_SIZES)
MLA_SCALE = (MLA_NOPE + MLA_ROPE) ** -0.5

kernel_name = 'hymba_gla_mla_memory_decoder_step'

def rms_norm(x, g):
    xf = x.astype(jnp.float32)
    y = xf * lax.rsqrt(jnp.mean(xf * xf, axis=-1, keepdims=True) + EPS)
    return (y * g.astype(jnp.float32)).astype(x.dtype)

def rope(x, pos):
    half = x.shape[-1] // 2
    inv = ROPE_THETA ** (-jnp.arange(half, dtype=jnp.float32) / half)
    ang = pos.astype(jnp.float32)[:, None] * inv[None, :]
    cos = jnp.cos(ang)[None, :, None, :]
    sin = jnp.sin(ang)[None, :, None, :]
    xf = x.astype(jnp.float32)
    x1, x2 = xf[..., :half], xf[..., half:]
    return jnp.concatenate([x1 * cos - x2 * sin, x2 * cos + x1 * sin], axis=-1).astype(x.dtype)

def gla_recurrence(q, k, v, log_a, s0):
    B, T = q.shape[:2]
    c = math.gcd(T, GLA_CHUNK)
    n = T // c

    def to_chunks(t):
        return jnp.moveaxis(t.reshape(B, n, c, *t.shape[2:]), 1, 0).astype(jnp.float32)

    qc, kc, vc, ac = to_chunks(q), to_chunks(k), to_chunks(v), to_chunks(log_a)
    causal = jnp.tril(jnp.ones((c, c), dtype=bool))[None, :, :, None, None]

    def step(s, inp):
        qi, ki, vi, ai = inp
        b = jnp.cumsum(ai, axis=1)
        o_inter = jnp.einsum('bthk,bhkv->bthv', qi * jnp.exp(b), s)
        diff = jnp.where(causal, b[:, :, None] - b[:, None, :], -jnp.inf)
        att = jnp.einsum('bthk,bshk,btshk->bhts', qi, ki, jnp.exp(diff))
        o_intra = jnp.einsum('bhts,bshv->bthv', att, vi)
        b_last = b[:, -1]
        s_new = s * jnp.exp(b_last)[..., None] + jnp.einsum(
            'bshk,bshv->bhkv', ki * jnp.exp(b_last[:, None] - b), vi)
        return s_new, o_inter + o_intra

    s_fin, o = lax.scan(step, s0.astype(jnp.float32), (qc, kc, vc, ac))
    o = jnp.moveaxis(o, 0, 1).reshape(B, T, GLA_HEADS, GLA_DV)
    return o, s_fin

def mix_inputs(h, pos, lp):
    B, T, _ = h.shape
    z = h @ lp['w_in']
    q, k, v, r, a, qa, kva, kpe = jnp.split(z, SPLIT_POINTS, axis=-1)
    q = q.reshape(B, T, GLA_HEADS, GLA_DK) * (GLA_DK ** -0.5)
    k = k.reshape(B, T, GLA_HEADS, GLA_DK)
    v = v.reshape(B, T, GLA_HEADS, GLA_DV)
    gate_pre = (a @ lp['w_gla_a2'] + lp['b_gla_a']).astype(jnp.float32)
    log_a = (jax.nn.log_sigmoid(gate_pre) / GLA_TAU).reshape(B, T, GLA_HEADS, GLA_DK)
    qf = (rms_norm(qa, lp['g_mla_qa']) @ lp['w_mla_qb']).reshape(B, T, MLA_HEADS, MLA_NOPE + MLA_ROPE)
    qn = rms_norm(qf[..., :MLA_NOPE], lp['g_q_nope'])
    qp = rope(rms_norm(qf[..., MLA_NOPE:], lp['g_q_rope']), pos)
    ckv = rms_norm(kva, lp['g_mla_kva'])
    kp = rope(rms_norm(kpe, lp['g_k_rope'])[:, :, None, :], pos)[:, :, 0]
    return (q, k, v, r, log_a), (qn, qp, ckv, kp)

def mla_decompress(ckv, lp):
    B, S, _ = ckv.shape
    kv = (ckv @ lp['w_mla_kvb']).reshape(B, S, MLA_HEADS, MLA_NOPE + MLA_V)
    kn = rms_norm(kv[..., :MLA_NOPE], lp['g_k_nope'])
    return kn, kv[..., MLA_NOPE:]

def mla_scores(qn, qp, kn, kp):
    s = jnp.einsum('bthd,bshd->bhts', qn, kn) + jnp.einsum('bthd,bsd->bhts', qp, kp)
    return s.astype(jnp.float32) * MLA_SCALE

def mla_prompt_attention(qn, qp, kn, kp, v):
    B, T = qn.shape[:2]
    qb = math.gcd(T, Q_BLOCK)
    nb = T // qb
    qn_b = qn.reshape(B, nb, qb, MLA_HEADS, MLA_NOPE).swapaxes(0, 1)
    qp_b = qp.reshape(B, nb, qb, MLA_HEADS, MLA_ROPE).swapaxes(0, 1)
    kpos = jnp.arange(T)

    def block(args):
        i, qn_i, qp_i = args
        s = mla_scores(qn_i, qp_i, kn, kp)
        qpos = i * qb + jnp.arange(qb)
        s = jnp.where(kpos[None, :] <= qpos[:, None], s, -jnp.inf)
        p = jax.nn.softmax(s, axis=-1).astype(v.dtype)
        return jnp.einsum('bhts,bshd->bthd', p, v)

    o = lax.map(block, (jnp.arange(nb), qn_b, qp_b))
    return o.swapaxes(0, 1).reshape(B, T, MLA_HEADS, MLA_V)

def online_update(carry, s, v):
    m, l, acc = carry
    m_new = jnp.maximum(m, jnp.max(s, axis=-1))
    corr = jnp.exp(m - m_new)
    p = jnp.exp(s - m_new[..., None])
    l = l * corr + jnp.sum(p, axis=-1)
    acc = acc * corr[..., None] + jnp.einsum('bhts,bshd->bhtd', p, v.astype(jnp.float32))
    return (m_new, l, acc)

def mla_sample_attention(qn, qp, ckv_new, kp_new, pool_ckv, pool_kpe, page_table, lp):
    B, T = qn.shape[:2]
    carry = (jnp.full((B, MLA_HEADS, T), -jnp.inf, jnp.float32),
             jnp.zeros((B, MLA_HEADS, T), jnp.float32),
             jnp.zeros((B, MLA_HEADS, T, MLA_V), jnp.float32))

    def page_step(c, pages):
        ckv = pool_ckv[pages]
        kp = pool_kpe[pages]
        kn, v = mla_decompress(ckv, lp)
        return online_update(c, mla_scores(qn, qp, kn, kp), v), None

    carry, _ = lax.scan(page_step, carry, page_table.T)
    kn, v = mla_decompress(ckv_new, lp)
    s = mla_scores(qn, qp, kn, kp_new)
    s = jnp.where(jnp.tril(jnp.ones((T, T), dtype=bool)), s, -jnp.inf)
    m, l, acc = online_update(carry, s, v)
    o = acc / l[..., None]
    return o.transpose(0, 2, 1, 3).astype(qn.dtype)

def mix_output(o_gla, r, o_mla, lp):
    B, T = r.shape[:2]
    og = rms_norm(o_gla.astype(r.dtype), lp['g_gla_o']).reshape(B, T, GLA_WIDTH) * jax.nn.silu(r)
    om = o_mla.reshape(B, T, MLA_WIDTH)
    return jnp.concatenate([og, om], axis=-1) @ lp['w_out']

def memory_kv(mem, lp):
    B, N, _ = mem.shape
    m = rms_norm(mem, lp['g_mem'])
    k = rms_norm((m @ lp['w_xk']).reshape(B, N, X_HEADS, X_DIM), lp['g_xk'])
    v = (m @ lp['w_xv']).reshape(B, N, X_HEADS, X_DIM)
    return k, v

def cross_attend(h, mk, mv, lp):
    B, T, _ = h.shape
    q = rms_norm((h @ lp['w_xq']).reshape(B, T, X_HEADS, X_DIM), lp['g_xq'])
    s = jnp.einsum('bthd,bnhd->bhtn', q, mk).astype(jnp.float32) * (X_DIM ** -0.5)
    p = jax.nn.softmax(s, axis=-1).astype(mv.dtype)
    o = jnp.einsum('bhtn,bnhd->bthd', p, mv).reshape(B, T, X_HEADS * X_DIM)
    return o @ lp['w_xo']

def ffn(h, lp):
    u = jnp.maximum(h @ lp['w_ff1'], 0)
    return (u * u) @ lp['w_ff2']

def prompt_layer(x, mem, lp):
    B, T, _ = x.shape
    pos = jnp.arange(T)
    h = rms_norm(x, lp['g_mix'])
    (q, k, v, r, log_a), (qn, qp, ckv, kp) = mix_inputs(h, pos, lp)
    s0 = jnp.zeros((B, GLA_HEADS, GLA_DK, GLA_DV), jnp.float32)
    o_gla, s_gla = gla_recurrence(q, k, v, log_a, s0)
    kn, vm = mla_decompress(ckv, lp)
    o_mla = mla_prompt_attention(qn, qp, kn, kp, vm)
    x = x + mix_output(o_gla, r, o_mla, lp)
    mk, mv = memory_kv(mem, lp)
    x = x + cross_attend(rms_norm(x, lp['g_x']), mk, mv, lp)
    x = x + ffn(rms_norm(x, lp['g_ff']), lp)
    return x, ckv, kp, mk, mv, s_gla.astype(x.dtype)

def sample_layer(x, pool_ckv, pool_kpe, page_table, mk, mv, s_prev, lp):
    B, T, _ = x.shape
    pos = PAST_LEN + jnp.arange(T)
    h = rms_norm(x, lp['g_mix'])
    (q, k, v, r, log_a), (qn, qp, ckv, kp) = mix_inputs(h, pos, lp)
    o_gla, s_gla = gla_recurrence(q, k, v, log_a, s_prev)
    o_mla = mla_sample_attention(qn, qp, ckv, kp, pool_ckv, pool_kpe, page_table, lp)
    x = x + mix_output(o_gla, r, o_mla, lp)
    x = x + cross_attend(rms_norm(x, lp['g_x']), mk, mv, lp)
    x = x + ffn(rms_norm(x, lp['g_ff']), lp)
    return x, ckv, kp, s_gla.astype(x.dtype)

def setup_inputs(seed: int = 0) -> dict:
    key = jax.random.key(seed)
    ks = iter(jax.random.split(key, 48))

    def nrm(shape, scale=1.0):
        return jax.random.normal(next(ks), shape, jnp.float32) * scale

    def gain(n):
        return 1.0 + nrm((DEPTH, n), 0.02)

    def lin(fi, fo):
        return nrm((DEPTH, fi, fo), fi ** -0.5)

    n_pages = PAST_LEN // PAGE_SIZE
    n_used = DEC_BATCH * n_pages
    n_pool = n_used + n_used // 4
    x_prompt = nrm((BATCH, SEQ, D_MODEL))
    x_sample = nrm((DEC_BATCH, DEC_SEQ, D_MODEL))
    mem_prompt = nrm((BATCH, N_MEM, D_MODEL))
    cache_ckv = nrm((DEPTH, n_pool, PAGE_SIZE, MLA_KV_RANK))
    cache_kpe = nrm((DEPTH, n_pool, PAGE_SIZE, MLA_ROPE))
    cache_mem_k = nrm((DEPTH, DEC_BATCH, N_MEM, X_HEADS, X_DIM))
    cache_mem_v = nrm((DEPTH, DEC_BATCH, N_MEM, X_HEADS, X_DIM))
    state_gla = nrm((DEPTH, DEC_BATCH, GLA_HEADS, GLA_DK, GLA_DV), 0.5)
    page_table = jax.random.permutation(next(ks), n_pool)[:n_used].reshape(DEC_BATCH, n_pages).astype(jnp.int32)
    return {
        'x_prompt': x_prompt, 'x_sample': x_sample, 'mem_prompt': mem_prompt,
        'cache_ckv': cache_ckv, 'cache_kpe': cache_kpe,
        'cache_mem_k': cache_mem_k, 'cache_mem_v': cache_mem_v,
        'state_gla': state_gla, 'page_table': page_table,
        'g_mix': gain(D_MODEL), 'w_in': lin(D_MODEL, D_IN),
        'w_gla_a2': lin(GLA_GATE_RANK, GLA_HEADS * GLA_DK), 'b_gla_a': nrm((DEPTH, GLA_HEADS * GLA_DK), 0.01),
        'g_gla_o': gain(GLA_DV),
        'g_mla_qa': gain(MLA_Q_RANK), 'w_mla_qb': lin(MLA_Q_RANK, MLA_HEADS * (MLA_NOPE + MLA_ROPE)),
        'g_mla_kva': gain(MLA_KV_RANK), 'w_mla_kvb': lin(MLA_KV_RANK, MLA_HEADS * (MLA_NOPE + MLA_V)),
        'g_q_nope': gain(MLA_NOPE), 'g_k_nope': gain(MLA_NOPE),
        'g_q_rope': gain(MLA_ROPE), 'g_k_rope': gain(MLA_ROPE),
        'w_out': lin(MIX_WIDTH, D_MODEL),
        'g_x': gain(D_MODEL), 'g_mem': gain(D_MODEL),
        'w_xq': lin(D_MODEL, X_HEADS * X_DIM), 'w_xk': lin(D_MODEL, X_HEADS * X_DIM),
        'w_xv': lin(D_MODEL, X_HEADS * X_DIM), 'g_xq': gain(X_DIM), 'g_xk': gain(X_DIM),
        'w_xo': lin(X_HEADS * X_DIM, D_MODEL),
        'g_ff': gain(D_MODEL), 'w_ff1': lin(D_MODEL, D_FF), 'w_ff2': lin(D_FF, D_MODEL),
    }

def reference(x_prompt, x_sample, mem_prompt, cache_ckv, cache_kpe, cache_mem_k, cache_mem_v,
              state_gla, page_table, g_mix, w_in, w_gla_a2, b_gla_a, g_gla_o, g_mla_qa, w_mla_qb,
              g_mla_kva, w_mla_kvb, g_q_nope, g_k_nope, g_q_rope, g_k_rope, w_out, g_x, g_mem,
              w_xq, w_xk, w_xv, g_xq, g_xk, w_xo, g_ff, w_ff1, w_ff2):
    yp, ys = x_prompt, x_sample
    ckv_p, kpe_p, mk_p, mv_p, gla_p = [], [], [], [], []
    ckv_s, kpe_s, gla_s = [], [], []
    for l in range(DEPTH):
        lp = {
            'g_mix': g_mix[l], 'w_in': w_in[l], 'w_gla_a2': w_gla_a2[l], 'b_gla_a': b_gla_a[l],
            'g_gla_o': g_gla_o[l], 'g_mla_qa': g_mla_qa[l], 'w_mla_qb': w_mla_qb[l],
            'g_mla_kva': g_mla_kva[l], 'w_mla_kvb': w_mla_kvb[l], 'g_q_nope': g_q_nope[l],
            'g_k_nope': g_k_nope[l], 'g_q_rope': g_q_rope[l], 'g_k_rope': g_k_rope[l],
            'w_out': w_out[l], 'g_x': g_x[l], 'g_mem': g_mem[l], 'w_xq': w_xq[l], 'w_xk': w_xk[l],
            'w_xv': w_xv[l], 'g_xq': g_xq[l], 'g_xk': g_xk[l], 'w_xo': w_xo[l],
            'g_ff': g_ff[l], 'w_ff1': w_ff1[l], 'w_ff2': w_ff2[l],
        }
        yp, c1, c2, c3, c4, c5 = prompt_layer(yp, mem_prompt, lp)
        ckv_p.append(c1); kpe_p.append(c2); mk_p.append(c3); mv_p.append(c4); gla_p.append(c5)
        ys, d1, d2, d3 = sample_layer(ys, cache_ckv[l], cache_kpe[l], page_table,
                                      cache_mem_k[l], cache_mem_v[l], state_gla[l], lp)
        ckv_s.append(d1); kpe_s.append(d2); gla_s.append(d3)
    return (yp, ys, jnp.stack(ckv_p), jnp.stack(kpe_p), jnp.stack(mk_p), jnp.stack(mv_p), jnp.stack(gla_p),
            jnp.stack(ckv_s), jnp.stack(kpe_s), jnp.stack(gla_s))


_drawn_inputs = setup_inputs


def setup_inputs(seed=0):
    import zlib

    import numpy as np

    out = dict(_drawn_inputs(seed))
    spreads = {}
    factors = {'cache_kpe': 4.201,
     'b_gla_a': 8.0,
     'g_gla_o': 6.589,
     'g_mla_qa': 8.0,
     'g_mla_kva': 2.718,
     'g_q_nope': 8.0,
     'g_k_nope': 8.0,
     'g_q_rope': 8.0,
     'g_k_rope': 4.453,
     'g_x': 8.0,
     'g_mem': 2.843,
     'g_xq': 8.0,
     'g_xk': 2.891,
     'g_ff': 3.347}
    for name, (base, spread) in spreads.items():
        noise = np.random.default_rng([zlib.crc32(name.encode()), seed]).standard_normal(out[name].shape)
        drawn = base * np.exp(spread * noise) if base else spread * noise
        out[name] = __import__('jax').numpy.asarray(drawn.astype(out[name].dtype))
    for name, factor in factors.items():
        out[name] = (out[name] * factor).astype(out[name].dtype)
    return out
```

```python
from contextlib import ExitStack

import numpy as np
import concourse.bass as bass
from concourse import mybir

F32 = mybir.dt.float32
I32 = mybir.dt.int32
ALU = mybir.AluOpType
ACT = mybir.ActivationFunctionType
AX = mybir.AxisListType

P = 128
D = 1024
KD = D // P
TP = 512
NB = 8
TS = 8
NS = NB * TS
NT = TP + NS
HALF = NT // 2
TILES = 5
PAST = 2048
PAGE = 128
NPG = PAST // PAGE
GH, DK, DV = 4, 64, 128
MH, MV, ROPE = 8, 64, 32
MQ = MV + ROPE
QR, KR = 384, 256
KQ, KC = QR // P, KR // P
MLA_SCALE = float(MQ) ** -0.5
XH, XD = 4, 128
NM = 256
FF = 4 * D
KF = FF // P
EPS = 1e-6
NEG = -1.0e30
CLAMP = 80.0 * 16.0
TAU = 16.0

W_XK, W_XV, W_QK, W_R, W_V, W_KVA, W_AKPE, W_QA, W_OUT, W_XQ, W_XO, W_F1, W_F2, W_END = (
    0, 4, 8, 12, 16, 20, 22, 23, 26, 34, 38, 42, 74, 106)
SLOTS = 8

C_ID, C_ONE, C_TRI, C_CAUS, C_SMASK, C_SNEG, C_SEQ, C_SCAN, C_ROPE, C_EPS, C_LNX, C_END = (
    0, 128, 256, 384, 512, 576, 640, 648, 1224, 1384, 1385, 1386)
G_MIX, G_X, G_FF, G_MEM, G_QA, G_GLA, G_XQ, G_BA, G_END = 0, 8, 16, 24, 32, 35, 36, 37, 39
R_KVA, R_QN, R_KN, R_QR, R_KR, R_XK, R_END = 0, 256, 320, 384, 416, 448, 576


def make_plan():
    used = [0] * 8
    fills = {}

    def fill(key, bank):
        used[bank] += 1
        fills[key] = (bank, used[bank])

    rot = [0]

    def turn(key):
        fill(key, rot[0] % 8)
        rot[0] += 1

    for j in range(4):
        turn(("memT", j))
    turn("ms_mem")
    for t in range(2):
        turn(("xk", t))
    for t in range(2):
        turn(("xv", t))
    for k in range(KD):
        turn(("xT", k))
    turn("xTs")
    for h in range(2):
        turn(("ms_mix", h))
    for n in range(2):
        turn(("kmT", n))
    for j in range(8):
        for h in range(2):
            turn(("z", j, h))
    for t in range(TILES):
        turn(("v", t))
    for t in range(TILES):
        turn(("kva", t))
    for j in range(8, 12):
        for h in range(2):
            turn(("z", j, h))
    for p in range(2):
        for h in range(2):
            turn(("gate", p, h))
    for p in range(2):
        turn(("klt", p))
    turn("klts")
    for t in range(4):
        turn(("att", t))
    turn("atts")
    for t in range(4):
        turn(("go", t))
        turn(("st", t))
    turn("gos")
    for b in range(NB):
        turn(("sst", b))
    for h in range(GH):
        for c in range(2):
            turn(("ms_gla", h, c))
    for c in range(2):
        turn(("ms_qa", c))
    for n in range(4):
        turn(("wkT", n))
    for t in range(TILES):
        for c in range(2):
            turn(("qf", t, c))
    for k in range(KC):
        turn(("ckT", k))
    turn("ckTs")
    for t in range(TILES):
        turn(("krp", t))
    for t in range(4):
        turn(("vp", t))
    for h in range(MH):
        turn(("qT", h))
    turn("qTs")
    for k in range(KC):
        turn(("qabs", k))
    turn("qpd")
    for h in range(MH):
        turn(("kT", h))
    for t in range(4):
        for h in range(MH):
            n = t * MH + h
            fill(("s", t, h), n % 3)
            fill(("pT", t, h), (3, 6)[n % 2])
        fill(("po", t), 4 + t % 2)
        fill(("poT", t), 7)
    base = list(used)
    for n in range(8):
        fills[("ct", n)] = (n % 2, base[n % 2] + n // 2 + 1)
    for j in range(NPG):
        fills[("kr", j)] = (2 + j % 2, base[2 + j % 2] + j // 2 + 1)
    for g in range(4):
        fills[("sc", g)] = (4 + g % 2, base[4 + g % 2] + g // 2 + 1)
    fills["scn"] = (6, base[6] + 1)
    fills["pv"] = (6, base[6] + 2)
    fills["kpt"] = (7, base[7] - 2)
    fills["kpt0"] = (7, base[7] + 1)
    fills["mt"] = (7, base[7] + 3)
    fills["mb"] = (7, base[7] + 4)
    fills["pct"] = (7, base[7] + 5)
    for name in ("mt", "mb", "pct"):
        fills[name + "_last"] = (7, fills[name][1] - 1)
    stride = [4, 4, 8, 8, 2, 2, 2, 4]
    for b in range(8):
        used[b] += NB * stride[b]
    rot[0] = 0
    turn("oms")
    for j in range(KD):
        for c in range(2):
            turn(("wo", j, c))
    for c in range(2):
        turn(("ms_x", c))
    for j in range(XH):
        for c in range(2):
            turn(("xq", j, c))
    for j in range(XH):
        for c in range(2):
            turn(("ms_xq", j, c))
    pairs = [(t, u) for t in range(4) for u in range(2)]
    for n in range(len(pairs) + 2):
        if n < len(pairs):
            turn(("cs", *pairs[n]))
        if n >= 2:
            turn(("cp", *pairs[n - 2]))
    for h in range(XH):
        turn(("co", h))
    rot[0] = 0
    for b in range(NB):
        for n in range(2):
            fill(("ck", b, n), (b * 2 + n) % 4)
    fill("css", 4)
    fill("cmt", 5)
    fill("cmb", 6)
    fill("cl", 7)
    fill("cos", 4)
    for j in range(KD):
        for c in range(2):
            turn(("xo", j, c))
    for c in range(2):
        turn(("ms_ff", c))
    rot[0] = 0
    base = list(used)
    for j in range(8):
        for c in range(2):
            n = 2 * j + c
            fills[("f1", j, c)] = (n % 8, base[n % 8] + n // 8 + 1)
    for b in range(8):
        used[b] += 2 * (KF // 8)
    base = list(used)
    for j in range(2):
        for c in range(2):
            fills[("f2", j, c)] = (2 * j + c, base[2 * j + c] + 1)
    for b in range(4):
        used[b] += KD // 2
    rot[0] = 4
    for t in range(TILES):
        for c in range(2):
            turn(("y", t, c))
    return fills, stride


PLAN, SEQ_STRIDE = make_plan()


def build(nc, x, xs, mem, consts, gains, rows, ring_w, w_kvb_d, w_qb_d, w_a2_d, cache_ckv, cache_kpe,
          cache_mk, cache_mv, state, pages, y_p, y_s, ckv_p, kpe_p, mk_p, mv_p, gla_p, ckv_s, kpe_s,
          gla_s):
    with ExitStack() as ctx:
        def sb(name, shape, dt=F32):
            return ctx.enter_context(nc.sbuf_tensor(name, shape, dt))

        sems = {}

        def S(name):
            if name not in sems:
                sems[name] = ctx.enter_context(nc.semaphore(name))
            return sems[name]

        cst = sb("cst", [P, C_END])
        gn = sb("gn", [P, G_END])
        row = sb("row", [P, R_END])
        xT = sb("xT", [P, KD, NT])
        hT = sb("hT", [P, KD * NT])
        mixT = sb("mixT", [P, KD, NT])
        ring = sb("ring", [P, SLOTS, KD, P])
        w_kvb = sb("w_kvb", [P, KC, 2 * MH * MV])
        w_a2 = sb("w_a2", [16, GH * DK])
        vm_p = sb("vm_p", [P, 2, XH * XD])
        kmT = sb("kmT", [P, 2, XH, P])
        rstd = sb("rstd", [P, NT])
        stat = sb("stat", [P, 640])
        page_sb = sb("page_sb", [1, NB * NPG], I32)
        ARENA = 23440
        arena = sb("arena", [P, ARENA])
        bank = [ctx.enter_context(nc.psum_tensor(f"bank{b}", [P, 512], F32)) for b in range(8)]

        def view(base, at, *shape):
            n = int(np.prod(shape))
            assert at + n <= base.shape[1], (at, shape)
            v = base[:, at:at + n]
            if len(shape) > 1:
                names = "abcd"[:len(shape)]
                v = v.rearrange(f"p ({' '.join(names)}) -> p {' '.join(names)}", **dict(zip(names, shape)))
            return v

        def spread(ap, axis, n):
            v = ap.unsqueeze(axis)
            return v.broadcast_to([*v.shape[:axis], n, *v.shape[axis + 1:]])

        ident = cst[:, C_ID:C_ID + P]
        ones = cst[:, C_ONE:C_ONE + P]
        tri = cst[:, C_TRI:C_TRI + P]
        causal = cst[:, C_CAUS:C_CAUS + P]
        smask = cst[0:NS, C_SMASK:C_SMASK + NS]
        sneg = cst[0:NS, C_SNEG:C_SNEG + NS]
        seqm = cst[0:NS, C_SEQ:C_SEQ + NB]
        scanm = cst[:, C_SCAN:C_SCAN + NT]
        cosn = view(cst, C_ROPE, TILES, ROPE // 2)
        sinn = view(cst, C_ROPE + 80, TILES, ROPE // 2)
        epsc = cst[:, C_EPS:C_EPS + 1]
        lnxc = cst[:, C_LNX:C_LNX + 1]
        hTk = view(hT, 0, KD, NT)
        mix_flat = mixT[:, :, :].rearrange("p a b -> p (a b)")

        zT = view(arena, 0, 12, NT)
        vtok = view(arena, 6912, TILES, GH * DV)
        kv = view(arena, 9472, TILES, KR + ROPE)
        sq1 = view(arena, 10912, KD, NT)
        memx = view(arena, 15520, 2, D)
        memT = view(arena, 17568, KD, NM)
        hmT = view(arena, 19616, KD, NM)
        xin_s = view(arena, 21664, D)
        xin = mix_flat[:, 0:4 * D].rearrange("p (t d) -> p t d", t=4)
        km_p = view(hT, 0, 2, XH * XD)
        gb = view(arena, 10912, 2, NT)
        eb = view(arena, 12064, 2, NT)
        ek = view(arena, 13216, 2, NT)
        qz = view(arena, 14368, 2, 2, NT)
        qi = view(arena, 16672, 2, 2, NT)
        klt = view(arena, 18976, TILES, 2, P)
        st = view(arena, 20256, 2, DV)
        st_s = view(arena, 20512, NB, 2, DV)
        att = view(hT, 0, 4, GH, P)
        atts = view(hT, 2048, GH, NS)
        klm = view(hT, 2304, 2, 2, P)
        kl = hTk[:, 6:8, :]
        dq, dl, eq = hTk[:, 0:2, :], hTk[:, 2:4, :], hTk[:, 4:6, :]
        sqg = view(arena, 14368, GH, NT)
        rs = view(arena, 16672, GH, NT)
        qf = view(arena, 0, TILES, MH * MQ)
        qT = view(arena, 4608, MH, TP)
        qTs = view(arena, 8704, MH, NS)
        qabs = view(arena, 10912, KC, NB, MH * TS)
        qpd = view(arena, 11936, NB, 4, MH * TS)
        ckT = view(arena, 13984, KC, NT)
        cknT = view(arena, 22500, KC, P)
        kpnT = view(arena, 22760, P)
        ckn = view(arena, 15136, KR + 1)
        sqf = view(arena, 15396, TILES, MH * MQ)
        w_qb = view(arena, 19236, KQ, MH * MQ)
        sqa = view(hT, 0, KQ, NT)
        qp4 = view(hT, 0, MH, P)
        w_kT = view(hT, 1728, MH, KR)
        sqk = view(hT, 3776, 512)
        kfull = view(arena, 19236, 4, MH * MQ)
        kT = view(arena, 0, MH, TP)
        vp = view(arena, 15396, 4, MH * MV)
        gq2 = view(arena, 22400, MV)
        gqr = view(arena, 22464, ROPE)
        pr = view(hT, 0, 3, 512)
        prT = view(hT, 1536, 2, 512)
        ot = view(hT, 2560, 2, 512)
        cpg = [view(arena, 17444, NPG, KR + 1), view(arena, 0, NPG, KR + 1)]
        kpg = [view(arena, 21556, NPG * ROPE), view(arena, 4112, NPG * ROPE)]
        sc = view(arena, 4624, NPG + 1, MH * TS)
        pb = view(arena, 5712, NPG + 1, MH * TS)
        pcs = view(arena, 6800, KR)
        pcT = view(arena, 7056, KC, MH, NS)
        mx = view(arena, 8080, P)
        dg = view(arena, 8208, 64)
        cT = view(hT, 0, 2, 2, KC, P)
        sqs = view(hT, 1024, 2, 512)
        kpT = view(hT, 2048, 4, P)
        vmc = view(arena, 0, NB, 2, XH * XD)
        kmc = view(arena, 8192, 2, 2, XH * XD)
        kmcT = view(arena, 10240, 2, 2, XH, P)
        xqT = view(arena, 12288, XH, NT)
        xoT = view(arena, 14592, XH, NT)
        pcx = view(arena, 16896, 2, 2, NM)
        pcxT = view(arena, 17920, XH, 2, TP)
        scs = view(arena, 22016, 2, NB * XH * TS)
        mxc = view(arena, 22528, NB * XH * TS)
        dgc = view(arena, 22784, 2, P)
        lrc = view(arena, 23040, NB * XH * TS)
        uT = view(arena, 0, KF, NT)
        ytok = view(hT, 0, 2, D)

        bank_full = [S(f"bank_full{b}") for b in range(8)]
        bank_free = [S(f"bank_free{b}") for b in range(8)]
        LOOP_COUNT = {}

        def at(key, turn=0, stride=0):
            b, n = PLAN[key]
            return b, (n if isinstance(turn, int) and turn == 0 else turn * stride + n)

        def full(eng, key, turn=0, stride=0):
            b, n = at(key, turn, stride)
            eng.wait_ge(bank_full[b], n)
            return bank[b]

        def freed(ins, key):
            return ins.then_inc(bank_free[PLAN[key][0]], 1)

        def reopen(pe, key, turn=0, stride=0):
            b, n = at(key, turn, stride)
            if not (isinstance(n, int) and n == 1):
                pe.wait_ge(bank_free[b], n - 1)
            return bank[b]

        def filled(ins, key):
            return ins.then_inc(bank_full[PLAN[key][0]], 1)

        def meet(eng, n):
            eng.drain().then_inc(S("phase_end"), 1)
            eng.wait_ge(S("phase_end"), 4 * n)

        def cols(t):
            return (t * P, P) if t < 4 else (TP, NS)

        def w_k(k):
            return w_kvb[:, k, :].rearrange("p (h c) -> p h c", h=MH)[:, :, 0:MV]

        def w_v(k):
            return w_kvb[:, k, :].rearrange("p (h c) -> p h c", h=MH)[:, :, MV:2 * MV]

        class Chain:

            def __init__(self, eng, name):
                self.eng, self.sem, self.n = eng, S(name), 0

            def __call__(self, ins):
                self.n += 1
                ins.then_inc(self.sem, 1)
                self.eng.wait_ge(self.sem, self.n)

        def wait_prT_free(eng, n, steps):
            if n >= 2:
                t, h = steps[n - 2]
                if h < MH - 1:
                    eng.wait_ge(S("prT_used"), (n - 2) - t)
                else:
                    full(eng, ("po", t))

        last_read = {}
        for j in range(4):
            last_read[W_XK + j], last_read[W_XV + j] = ("xk", 1), ("xv", 1)
            last_read[W_QK + j], last_read[W_R + j] = ("z", j, 1), ("z", 4 + j, 1)
            last_read[W_V + j], last_read[W_XQ + j] = ("v", 4), ("xq", j, 1)
            last_read[W_XO + j] = ("xo", 2 * j + 1, 1)
        for j in range(2):
            last_read[W_KVA + j] = ("kva", 4)
        last_read[W_AKPE] = ("z", 11, 1)
        for j in range(3):
            last_read[W_QA + j] = ("z", 8 + j, 1)
        for j in range(KD):
            last_read[W_OUT + j] = ("wo", j, 1)

        slot_in = [S(f"slot_in{s}") for s in range(SLOTS)]

        def slot(pe, tile):
            pe.wait_ge(slot_in[tile % SLOTS], 16 * (tile // SLOTS + 1))
            return tile % SLOTS

        squares = {"mem": 0, "mix": KD, "x": 2 * KD, "ff": 3 * KD}
        rstds = {"mem": 0, "mix": 1, "qa": 2, "x": 3, "ff": 4}
        normed = {"mem": 0, "mix": KD, "qa": 2 * KD, "x": 2 * KD + KQ, "ff": 3 * KD + KQ}

        block = ctx.enter_context(nc.Block())

        @block.sync
        def _(sp):
            def load_tile(n):
                if n >= SLOTS:
                    b, c = PLAN[last_read[n - SLOTS]]
                    sp.wait_ge(bank_full[b], c)
                sp.dma_start(ring[:, n % SLOTS, :, :].rearrange("p a b -> p (a b)"), ring_w[n]).then_inc(
                    slot_in[n % SLOTS], 16)

            sp.dma_start(cst[:, :], consts).then_inc(S("const_in"), 16)
            sp.dma_start(memx, mem.rearrange("a (t p) d -> p (a t) d", p=P)).then_inc(S("mem_in"), 16)
            sp.dma_start(gn[:, :], gains).then_inc(S("const_in"), 16)
            sp.dma_start(row[:, :], rows.broadcast_to([P, R_END])).then_inc(S("const_in"), 16)
            for n in range(W_XK, W_XV):
                load_tile(n)
            sp.dma_start(xin, x.rearrange("a (t p) d -> p (a t) d", p=P)).then_inc(S("x_in"), 16)
            sp.dma_start(xin_s[0:NS, :], xs.rearrange("b t d -> (b t) d")).then_inc(S("x_in"), 16)
            for n in range(W_XV, W_QK):
                load_tile(n)
            sp.dma_start(page_sb[:, :], pages.rearrange("(o b) n -> o (b n)", o=1)).then_inc(S("page_in"), 16)
            sp.dma_start(w_a2[:, :], w_a2_d[0]).then_inc(S("wa2_in"), 16)
            sp.dma_start(w_kvb[:, :, :], w_kvb_d[0].rearrange("(k p) n -> p k n", p=P)).then_inc(S("wkvb_in"), 16)
            for n in range(W_QK, W_OUT):
                load_tile(n)
            sp.wait_ge(S("phase_end"), 4 * 1)
            sp.dma_start(st_s, state[0].rearrange("b (q h) k v -> (h k) b q v", q=2)).then_inc(S("state_in"), 16)
            for n in range(W_OUT, W_XQ):
                if last_read[n - SLOTS][0] in ("z", "kva", "v"):
                    load_tile(n)
            sp.wait_ge(S("phase_end"), 4 * 2)
            sp.dma_start(w_qb, w_qb_d[0].rearrange("(k p) n -> p k n", p=P)).then_inc(S("wqb_in"), 16)
            sp.wait_ge(S("page_in"), 16)

            def load_pages(b, par):
                for j in range(NPG):
                    where = page_sb[0:1, bass.ds(b * NPG + j, 1)]
                    page = sp.value_load(where, min_val=0, max_val=cache_ckv.shape[1] - 1)
                    sp.dma_start(cpg[par][:, j, 0:KR], cache_ckv[0, bass.ds(page, 1), :, :].rearrange(
                        "a p c -> p (a c)")).then_inc(S(f"page_c{par}_{j // 4}"), 16)
                    sp.dma_start(kpg[par][:, j * ROPE:(j + 1) * ROPE], cache_kpe[0, bass.ds(page, 1), :, :].rearrange(
                        "a p c -> p (a c)")).then_inc(S(f"page_k{par}"), 16)

            sp.wait_ge(S("phase_end"), 4 * 3)
            load_pages(0, 0)
            sp.wait_ge(S("phase_end"), 4 * 4)
            load_pages(1, 1)
            with sp.Fori(0, (NB - 2) // 2) as i:
                for par in range(2):
                    b = i * 2 + (2 + par)
                    sp.wait_ge(S("pv_out"), b - 1)
                    load_pages(b, par)
            sp.wait_ge(S("phase_end"), 4 * 5)
            mk = cache_mk[0].rearrange("b (n p) h d -> b p n (h d)", p=P)
            mv = cache_mv[0].rearrange("b (n p) h d -> b p n (h d)", p=P)
            for b in range(2):
                sp.dma_start(kmc[:, b, :, :], mk[b]).then_inc(S(f"kmc_in{b}"), 16)
            for b in range(NB):
                sp.dma_start(vmc[:, b, :, :], mv[b]).then_inc(S("vmc_in"), 16)
            for n in range(W_XQ, W_F1):
                load_tile(n)
            for n in range(W_F1, W_F1 + SLOTS - 4):
                load_tile(n)
            for b in range(2, NB):
                bk, c = PLAN[("ck", b - 2, 1)]
                sp.wait_ge(bank_full[bk], c)
                sp.dma_start(kmc[:, b % 2, :, :], mk[b]).then_inc(S(f"kmc_in{b % 2}"), 16)
            for n in range(W_F1 + SLOTS - 4, W_F1 + SLOTS):
                load_tile(n)
            with sp.Fori(0, KF // 8 - 1) as i:
                for j in range(8):
                    b, c = at(("f1", j, 1), i, 2)
                    sp.wait_ge(bank_full[b], c)
                    sp.dma_start(ring[:, (W_F1 + j) % SLOTS, :, :].rearrange("p a b -> p (a b)"),
                                 ring_w[bass.ds(i * 8 + (W_F1 + 8 + j), 1)].rearrange("a p c -> p (a c)")
                                 ).then_inc(slot_in[(W_F1 + j) % SLOTS], 16)
            for j in range(8):
                b, c = at(("f1", j, 1), KF // 8 - 1, 2)
                sp.wait_ge(bank_full[b], c)
                n = W_F2 + j
                sp.dma_start(ring[:, n % SLOTS, :, :].rearrange("p a b -> p (a b)"), ring_w[n]).then_inc(
                    slot_in[n % SLOTS], 16)
            with sp.Fori(0, KD // 2 - 1) as i:
                for j in range(8):
                    if j % 4 < 3:
                        sp.wait_ge(S("f2_used"), i * 6 + (j // 4 * 3 + j % 4 + 1))
                    else:
                        b, c = at(("f2", j // 4, 1), i, 1)
                        sp.wait_ge(bank_full[b], c)
                    sp.dma_start(ring[:, (W_F2 + j) % SLOTS, :, :].rearrange("p a b -> p (a b)"),
                                 ring_w[bass.ds(i * 8 + (W_F2 + 8 + j), 1)].rearrange("a p c -> p (a c)")
                                 ).then_inc(slot_in[(W_F2 + j) % SLOTS], 16)

        @block.tensor
        def _(pe):
            mm, tr = nc.tensor.matmul, nc.tensor.transpose

            def sums(name, keys, sq, n_k, width=HALF):
                outs = [reopen(pe, key) for key in keys]
                for k in range(n_k):
                    if name in squares:
                        pe.wait_ge(S("squares"), squares[name] + k + 1)
                    for c, key in enumerate(keys):
                        ins = mm(outs[c][:, 0:width], ones, sq[:, k, c * width:(c + 1) * width],
                                 start=(k == 0), stop=(k == n_k - 1))
                        if k == n_k - 1:
                            filled(ins, key)

            def project(key, lhsT, src, n_k, m=P):
                outs = [reopen(pe, (*key, c)) for c in range(2)]
                for k in range(n_k):
                    for c in range(2):
                        ins = mm(outs[c][0:m, 0:HALF], lhsT(k), src[:, k, c * HALF:(c + 1) * HALF],
                                 start=(k == 0), stop=(k == n_k - 1))
                        if k == n_k - 1:
                            filled(ins, (*key, c))

            pe.wait_ge(S("const_in"), 48)
            pe.wait_ge(S("mem_in"), 16)
            for j in range(4):
                o = reopen(pe, ("memT", j))
                for kk in range(2):
                    for t in range(2):
                        ins = tr(o[:, (kk * 2 + t) * P:(kk * 2 + t + 1) * P],
                                 memx[:, t, (2 * j + kk) * P:(2 * j + kk + 1) * P], ident)
                filled(ins, ("memT", j))
            sums("mem", ["ms_mem"], sq1, KD, width=NM)
            pe.wait_ge(S("normed"), normed["mem"] + KD)
            for name, w0 in (("xk", W_XK), ("xv", W_XV)):
                for j in range(4):
                    slot(pe, w0 + j)
                for t in range(2):
                    o = reopen(pe, (name, t))
                    for k in range(KD):
                        ins = mm(o[:, :], hmT[:, k, t * P:(t + 1) * P], ring[:, w0 % SLOTS:w0 % SLOTS + 4, k, :],
                                 start=(k == 0), stop=(k == KD - 1))
                    filled(ins, (name, t))
            pe.wait_ge(S("x_in"), 32)
            for k in range(KD):
                o = reopen(pe, ("xT", k))
                for t in range(4):
                    ins = tr(o[:, t * P:(t + 1) * P], xin[:, t, k * P:(k + 1) * P], ident)
                filled(ins, ("xT", k))
            o = reopen(pe, "xTs")
            for k in range(KD):
                ins = tr(o[:, k * NS:(k + 1) * NS], xin_s[0:NS, k * P:(k + 1) * P], ident[0:NS, 0:NS])
            filled(ins, "xTs")
            sums("mix", [("ms_mix", 0), ("ms_mix", 1)], sq1, KD)
            pe.wait_ge(S("km"), 1)
            for n in range(2):
                o = reopen(pe, ("kmT", n))
                for h in range(XH):
                    ins = tr(o[:, h * P:(h + 1) * P], km_p[:, n, h * XD:(h + 1) * XD], ident)
                filled(ins, ("kmT", n))
            pe.wait_ge(S("normed"), normed["mix"] + KD)
            for j in range(8):
                s = slot(pe, W_QK + j)
                project(("z", j), lambda k: ring[:, s, k, :], hTk, KD)
            for name, w0, n_w in (("v", W_V, 4), ("kva", W_KVA, 3)):
                for j in range(n_w):
                    slot(pe, w0 + j)
                for t in range(TILES):
                    c0, m = cols(t)
                    o = reopen(pe, (name, t))
                    s0 = w0 % SLOTS
                    n_out = GH * DV if name == "v" else KR
                    for k in range(KD):
                        ins = mm(o[0:m, 0:n_out], hTk[:, k, c0:c0 + m], ring[:, s0:s0 + n_out // P, k, :],
                                 start=(k == 0), stop=(k == KD - 1))
                    if name == "kva":
                        for k in range(KD):
                            ins = mm(o[0:m, KR:KR + ROPE], hTk[:, k, c0:c0 + m],
                                     ring[:, W_AKPE % SLOTS, k, 16:16 + ROPE], start=(k == 0), stop=(k == KD - 1))
                    filled(ins, (name, t))
            for j in range(8, 11):
                s = slot(pe, W_QA + j - 8)
                project(("z", j), lambda k: ring[:, s, k, :], hTk, KD)
            project(("z", 11), lambda k: ring[:, W_AKPE % SLOTS, k, 0:16], hTk, KD, m=16)
            meet(pe, 1)

            pe.wait_ge(S("wa2_in"), 16)
            for p in range(2):
                for c in range(2):
                    o = reopen(pe, ("gate", p, c))
                    filled(mm(o[:, 0:HALF], w_a2[:, p * P:(p + 1) * P], zT[0:16, 11, c * HALF:(c + 1) * HALF],
                              start=True, stop=True), ("gate", p, c))
            pe.wait_ge(S("kl"), 1)
            for p in range(2):
                o = reopen(pe, ("klt", p))
                for t in range(4):
                    ins = tr(o[:, t * P:(t + 1) * P], kl[:, p, t * P:(t + 1) * P], ident)
                filled(ins, ("klt", p))
            o = reopen(pe, "klts")
            for p in range(2):
                ins = tr(o[0:NS, p * P:(p + 1) * P], kl[:, p, TP:NT], ident)
            filled(ins, "klts")
            pe.wait_ge(S("kd"), 1)
            pe.wait_ge(S("qz"), 8)
            for t in range(4):
                o = reopen(pe, ("att", t))
                for h in range(GH):
                    ins = mm(o[:, h * P:(h + 1) * P], ek[:, h // 2, t * P:(t + 1) * P],
                             qz[:, h // 2, h % 2, t * P:(t + 1) * P], start=True, stop=True)
                filled(ins, ("att", t))
            o = reopen(pe, "atts")
            for h in range(GH):
                ins = mm(o[0:NS, h * NS:(h + 1) * NS], ek[:, h // 2, TP:NT], qz[:, h // 2, h % 2, TP:NT],
                         start=True, stop=True)
            filled(ins, "atts")
            pe.wait_ge(S("klt"), 3)
            for t in range(4):
                o = reopen(pe, ("go", t))
                pe.wait_ge(S("att"), t + 1)
                if t:
                    pe.wait_ge(S("gla_state"), 4 * t)
                for h in range(GH):
                    ins = mm(o[:, h * P:(h + 1) * P], vtok[:, t, h * DV:(h + 1) * DV], att[:, t, h, :],
                             start=True, stop=(t == 0))
                    if t:
                        ins = mm(o[:, h * P:(h + 1) * P], st[:, h // 2, :], qi[:, h // 2, h % 2, t * P:(t + 1) * P],
                                 start=False, stop=True)
                filled(ins, ("go", t))
                o = reopen(pe, ("st", t))
                for p in range(2):
                    ins = mm(o[:, p * 256:(p + 1) * 256], klt[:, t, p, :], vtok[:, t, p * 256:(p + 1) * 256],
                             start=True, stop=True)
                filled(ins, ("st", t))
            pe.wait_ge(S("att"), 5)
            pe.wait_ge(S("state_in"), 16)
            o = reopen(pe, "gos")
            for h in range(GH):
                mm(o[:, h * NS:(h + 1) * NS], vtok[0:NS, 4, h * DV:(h + 1) * DV], atts[0:NS, h, :],
                   start=True, stop=False, skip_group_check=True)
                for b in range(NB):
                    ins = mm(o[:, h * NS + b * TS:h * NS + (b + 1) * TS], st_s[:, b, h // 2, :],
                             qi[:, h // 2, h % 2, TP + b * TS:TP + (b + 1) * TS], start=False, stop=True,
                             skip_group_check=True)
            filled(ins, "gos")
            for b in range(NB):
                o = reopen(pe, ("sst", b))
                pe.wait_ge(S("klm"), b + 1)
                for p in range(2):
                    ins = mm(o[:, p * 256:(p + 1) * 256], klm[0:NS, b % 2, p, :],
                             vtok[0:NS, 4, p * 256:(p + 1) * 256], start=True, stop=True)
                filled(ins, ("sst", b))
            pe.wait_ge(S("sq_gla"), 1)
            for h in range(GH):
                for c in range(2):
                    o = reopen(pe, ("ms_gla", h, c))
                    filled(mm(o[:, 0:HALF], ones, sqg[:, h, c * HALF:(c + 1) * HALF], start=True, stop=True),
                           ("ms_gla", h, c))
            meet(pe, 2)

            pe.wait_ge(S("sq_qa"), 1)
            sums("qa", [("ms_qa", 0), ("ms_qa", 1)], sqa, KQ)
            pe.wait_ge(S("wkvb_in"), 16)
            for n in range(4):
                o = reopen(pe, ("wkT", n))
                for e in range(2):
                    for k in range(KC):
                        h = 2 * n + e
                        ins = tr(o[0:MV, (e * 2 + k) * P:(e * 2 + k + 1) * P],
                                 w_kvb[:, k, h * P:h * P + MV], ident)
                filled(ins, ("wkT", n))
            pe.wait_ge(S("wqb_in"), 16)
            pe.wait_ge(S("normed"), normed["qa"] + KQ)
            for t in range(TILES):
                c0, m = cols(t)
                for c in range(2):
                    o = reopen(pe, ("qf", t, c))
                    for k in range(KQ):
                        ins = mm(o[0:m, 0:384], zT[:, 8 + k, c0:c0 + m], w_qb[:, k, c * 384:(c + 1) * 384],
                                 start=(k == 0), stop=(k == KQ - 1))
                    filled(ins, ("qf", t, c))
            pe.wait_ge(S("ckv"), 1)
            for k in range(KC):
                o = reopen(pe, ("ckT", k))
                for t in range(4):
                    ins = tr(o[:, t * P:(t + 1) * P], kv[:, t, k * P:(k + 1) * P], ident)
                filled(ins, ("ckT", k))
            o = reopen(pe, "ckTs")
            for k in range(KC):
                tr(o[:, k * NS:(k + 1) * NS], kv[0:NS, 4, k * P:(k + 1) * P], ident[0:NS, 0:NS])
            filled(tr(o[0:ROPE, P:P + NS], kv[0:NS, 4, KR:KR + ROPE], ident[0:NS, 0:NS]), "ckTs")
            pe.wait_ge(S("ckT"), 3)
            for t in range(TILES):
                c0, m = cols(t)
                o = reopen(pe, ("krp", t))
                for k in range(KC):
                    ins = mm(o[0:m, :], ckT[:, k, c0:c0 + m], w_k(k), start=(k == 0), stop=(k == KC - 1))
                filled(ins, ("krp", t))
            for t in range(4):
                o = reopen(pe, ("vp", t))
                for k in range(KC):
                    ins = mm(o[:, :], ckT[:, k, t * P:(t + 1) * P], w_v(k), start=(k == 0), stop=(k == KC - 1))
                filled(ins, ("vp", t))
            pe.wait_ge(S("q_ready"), 1)
            for h in range(MH):
                o = reopen(pe, ("qT", h))
                for t in range(4):
                    ins = tr(o[0:MQ, t * P:(t + 1) * P], qf[:, t, h * MQ:(h + 1) * MQ], ident)
                filled(ins, ("qT", h))
            o = reopen(pe, "qTs")
            for h in range(MH):
                ins = tr(o[0:MQ, h * NS:(h + 1) * NS], qf[0:NS, 4, h * MQ:(h + 1) * MQ], ident[0:NS, 0:NS])
            filled(ins, "qTs")
            pe.wait_ge(S("qTs"), 1)
            pe.wait_ge(S("w_kT"), 4)
            for k in range(KC):
                o = reopen(pe, ("qabs", k))
                for h in range(MH):
                    ins = mm(o[:, h * NS:(h + 1) * NS], w_kT[0:MV, h, k * P:(k + 1) * P], qTs[0:MV, h, :],
                             start=True, stop=True)
                filled(ins, ("qabs", k))
            pe.wait_ge(S("qp4"), 1)
            o = reopen(pe, "qpd")
            for h in range(MH):
                ins = tr(o[:, h * NS:(h + 1) * NS], qp4[0:NS, h, :], ident[0:NS, 0:NS])
            filled(ins, "qpd")
            pe.wait_ge(S("kfull"), 2)
            for h in range(MH):
                o = reopen(pe, ("kT", h))
                for t in range(4):
                    ins = tr(o[0:MQ, t * P:(t + 1) * P], kfull[:, t, h * MQ:(h + 1) * MQ], ident)
                filled(ins, ("kT", h))
            meet(pe, 3)

            steps = [(t, h) for t in range(4) for h in range(MH)]

            def out_rows(t):
                pe.wait_ge(S("ot"), t + 1)
                o = reopen(pe, ("poT", t))
                for j in range(4):
                    ins = tr(o[:, j * P:(j + 1) * P], ot[:, t % 2, j * P:(j + 1) * P], ident)
                filled(ins, ("poT", t))

            for n in range(len(steps) + 5):
                if n < len(steps):
                    t, h = steps[n]
                    o = reopen(pe, ("s", t, h))
                    filled(mm(o[:, 0:(t + 1) * P], qT[0:MQ, h, t * P:(t + 1) * P], kT[0:MQ, h, 0:(t + 1) * P],
                              start=True, stop=True), ("s", t, h))
                if 2 <= n < len(steps) + 2:
                    t, h = steps[n - 2]
                    pe.wait_ge(S("pr"), n - 1)
                    o = reopen(pe, ("pT", t, h))
                    for s in range(t + 1):
                        ins = tr(o[:, s * P:(s + 1) * P], pr[:, (n - 2) % 3, s * P:(s + 1) * P], ident)
                    filled(ins, ("pT", t, h))
                if 3 <= n < len(steps) + 3:
                    t, h = steps[n - 3]
                    pe.wait_ge(S(f"prT{(n - 3) % 2}"), (n - 3) // 2 + 1)
                    if h == 0:
                        reopen(pe, ("po", t))
                    o = bank[PLAN[("po", t)][0]]
                    for s in range(t + 1):
                        ins = mm(o[:, h * MV:(h + 1) * MV], prT[:, (n - 3) % 2, s * P:(s + 1) * P],
                                 vp[:, s, h * MV:(h + 1) * MV], start=(s == 0), stop=(s == t))
                    if h < MH - 1:
                        ins.then_inc(S("prT_used"), 1)
                    else:
                        filled(ins, ("po", t))
                if n >= 5 and steps[n - 5][1] == MH - 1:
                    out_rows(steps[n - 5][0])
            meet(pe, 4)

            def uses(b):
                return b // 2 + 1 if isinstance(b, int) else b[0] + (b[1] + 1)

            def transposed_pages(par, n, b):
                if n % 2 == 0:
                    pe.wait_ge(S(f"page_c{par}_{n // 2}"), (uses(b)) * 64)
                bb = b if isinstance(b, int) else b[2]
                o = reopen(pe, ("ct", n), bb, 4)
                for e in range(2):
                    for k in range(KC):
                        ins = tr(o[:, (e * KC + k) * P:(e * KC + k + 1) * P],
                                 cpg[par][:, 2 * n + e, k * P:(k + 1) * P], ident)
                filled(ins, ("ct", n))

            def softmax_max(b, last=""):
                pe.wait_ge(S("mx"), b + 1)
                o = reopen(pe, "mt" + last, b, 4)
                filled(tr(o[:, 0:P], mx, ident), "mt")

            def softmax_spread(b, last=""):
                pe.wait_ge(S("dg"), b + 1)
                o = reopen(pe, "mb" + last, b, 4)
                filled(mm(o[:, 0:64], ones[0:64, :], dg[0:64, :], start=True, stop=True), "mb")

            def weighted(b, par):
                pe.wait_ge(S("pb"), b + 1)
                o = reopen(pe, "pv", b, 2)
                for j in range(NPG):
                    mm(o[0:64, 0:KR + 1], pb[:, j, :], cpg[par][:, j, :], start=(j == 0), stop=False)
                filled(mm(o[0:64, 0:KR + 1], pb[0:NS, NPG, :], ckn[0:NS, :], start=False, stop=True), "pv")

            def weighted_T(b, last=""):
                pe.wait_ge(S("pcs"), b + 1)
                o = reopen(pe, "pct" + last, b, 4)
                for k in range(KC):
                    ins = tr(o[:, k * P:(k + 1) * P], pcs[:, k * P:(k + 1) * P], ident)
                filled(ins, "pct")

            def sequence(b, par, half, first=False):
                tb = b if isinstance(b, int) else (half[0], half[1], b)
                prev = None if first else b - 1
                pe.wait_ge(S(f"page_k{par}"), uses(tb) * (16 * NPG))
                o = reopen(pe, "kpt0") if first else reopen(pe, "kpt", b, 4)
                for g in range(4):
                    ins = tr(o[:, g * P:(g + 1) * P], kpg[par][:, g * P:(g + 1) * P], ident)
                filled(ins, "kpt")
                transposed_pages(par, 0, tb)
                for n in range(8):
                    if n < 7:
                        transposed_pages(par, n + 1, tb)
                    pe.wait_ge(S("cT"), b * 8 + (n + 1))
                    for e in range(2):
                        j = 2 * n + e
                        o = reopen(pe, ("kr", j), b, 8)
                        for k in range(KC):
                            ins = mm(o[:, :], cT[:, n % 2, e, k, :], w_k(k), start=(k == 0), stop=(k == KC - 1))
                        filled(ins, ("kr", j))
                        g, i = j // 4, j % 4
                        if i == 0:
                            reopen(pe, ("sc", g), b, 2)
                        o = bank[PLAN[("sc", g)][0]]
                        for k in range(KC):
                            ins = mm(o[:, i * 64:(i + 1) * 64], cT[:, n % 2, e, k, :],
                                     qabs[:, k, bass.ds(b, 1), :].rearrange("p a c -> p (a c)"),
                                     start=(k == 0), stop=(k == KC - 1))
                        if i < 3 and e == 1:
                            ins.then_inc(S("cT_used"), 1)
                        if i == 3:
                            if g == 0:
                                pe.wait_ge(S("kpT"), b + 1)
                            filled(mm(o[:, 256:512], kpT[:, g, :],
                                      qpd[:, bass.ds(b, 1), :, :].rearrange("p a q c -> p (a q c)"),
                                      start=True, stop=True), ("sc", g))
                        if prev is not None:
                            if j == 1:
                                softmax_max(prev)
                            if j == 3:
                                softmax_spread(prev)
                            if j == 6:
                                weighted(prev, 1 - par)
                            if j == 9:
                                weighted_T(prev)
                o = reopen(pe, "scn", b, 2)
                for k in range(KC):
                    mm(o[:, 0:64], cknT[:, k, :], qabs[:, k, bass.ds(b, 1), :].rearrange("p a c -> p (a c)"),
                       start=(k == 0), stop=(k == KC - 1))
                filled(mm(o[:, 64:128], kpnT,
                          qpd[:, bass.ds(b, 1), 0, :].rearrange("p a c -> p (a c)"),
                          start=True, stop=True), "scn")

            pe.wait_ge(S("page_one"), 2)
            sequence(0, 0, None, first=True)
            with pe.Fori(0, (NB - 2) // 2) as i:
                sequence(i * 2 + 1, 1, (i, 0))
                sequence(i * 2 + 2, 0, (i, 1))
            sequence(NB - 1, 1, None)
            softmax_max(NB - 1, "_last")
            softmax_spread(NB - 1, "_last")
            weighted(NB - 1, 1)
            weighted_T(NB - 1, "_last")
            pe.wait_ge(S("pcT"), NB)
            o = reopen(pe, "oms")
            for h in range(MH):
                for k in range(KC):
                    ins = mm(o[MV * (h % 2):MV * (h % 2 + 1), (h // 2) * NS:(h // 2 + 1) * NS],
                             w_kvb[:, k, h * P + MV:(h + 1) * P], pcT[:, k, h, :], start=(k == 0), stop=(k == KC - 1))
            filled(ins, "oms")
            meet(pe, 5)

            for j in range(KD):
                s = slot(pe, W_OUT + j)
                project(("wo", j), lambda k: ring[:, s, k, :], mixT, KD)
            sums("x", [("ms_x", 0), ("ms_x", 1)], mixT, KD)
            pe.wait_ge(S("normed"), normed["x"] + KD)
            for j in range(XH):
                s = slot(pe, W_XQ + j)
                project(("xq", j), lambda k: ring[:, s, k, :], hTk, KD)
            for j in range(XH):
                pe.wait_ge(S("sq_xq"), j + 1)
                for c in range(2):
                    o = reopen(pe, ("ms_xq", j, c))
                    filled(mm(o[:, 0:HALF], ones, mixT[:, j, c * HALF:(c + 1) * HALF], start=True, stop=True),
                           ("ms_xq", j, c))
            pe.wait_ge(S("xq"), XH)
            pairs = [(t, u) for t in range(4) for u in range(2)]
            for n in range(len(pairs) + 2):
                if n < len(pairs):
                    t, u = pairs[n]
                    o = reopen(pe, ("cs", t, u))
                    for e in range(2):
                        h = 2 * u + e
                        ins = mm(o[:, e * NM:(e + 1) * NM], xqT[:, h, t * P:(t + 1) * P], kmT[:, :, h, :],
                                 start=True, stop=True)
                    filled(ins, ("cs", t, u))
                if n >= 2:
                    t, u = pairs[n - 2]
                    pe.wait_ge(S("pcx"), n - 1)
                    o = reopen(pe, ("cp", t, u))
                    for e in range(2):
                        for m in range(2):
                            ins = tr(o[:, (e * 2 + m) * P:(e * 2 + m + 1) * P],
                                     pcx[:, (n - 2) % 2, e, m * P:(m + 1) * P], ident)
                    filled(ins, ("cp", t, u))
            pe.wait_ge(S("pcxT"), 8)
            for h in range(XH):
                o = reopen(pe, ("co", h))
                for m in range(2):
                    ins = mm(o[:, :], vm_p[:, m, h * XD:(h + 1) * XD], pcxT[:, h, m, :], start=(m == 0), stop=(m == 1))
                filled(ins, ("co", h))
            css = bank[PLAN["css"][0]]
            for b in range(NB + 1):
                if b < NB:
                    pe.wait_ge(S(f"kmc_in{b % 2}"), 16 * (b // 2 + 1))
                    for m in range(2):
                        o = reopen(pe, ("ck", b, m))
                        for h in range(XH):
                            ins = tr(o[:, h * P:(h + 1) * P], kmc[:, b % 2, m, h * XD:(h + 1) * XD], ident)
                        filled(ins, ("ck", b, m))
                if b:
                    q = b - 1
                    pe.wait_ge(S("kmcT"), 2 * q + 2)
                    if q == 0:
                        reopen(pe, "css")
                    for m in range(2):
                        for h in range(XH):
                            c0 = ((m * NB + q) * XH + h) * TS
                            ins = mm(css[:, c0:c0 + TS], kmcT[:, q % 2, m, h, :],
                                     xqT[:, h, TP + q * TS:TP + (q + 1) * TS], start=True, stop=True)
                    if q < NB - 1:
                        ins.then_inc(S("kmcT_used"), 1)
            filled(ins, "css")
            pe.wait_ge(S("mxc"), 1)
            o = reopen(pe, "cmt")
            for e in range(2):
                ins = tr(o[:, e * P:(e + 1) * P], mxc[:, e * P:(e + 1) * P], ident)
            filled(ins, "cmt")
            pe.wait_ge(S("dgc"), 2)
            o = reopen(pe, "cmb")
            for e in range(2):
                ins = mm(o[:, e * P:(e + 1) * P], ones, dgc[:, e, :], start=True, stop=True)
            filled(ins, "cmb")
            pe.wait_ge(S("scs"), 1)
            o = reopen(pe, "cl")
            for m in range(2):
                ins = mm(o[:, 0:256], ones, scs[:, m, :], start=(m == 0), stop=(m == 1))
            filled(ins, "cl")
            pe.wait_ge(S("vmc_in"), 16 * NB)
            o = reopen(pe, "cos")
            for b in range(NB):
                for h in range(XH):
                    c0 = (b * XH + h) * TS
                    for m in range(2):
                        ins = mm(o[:, c0:c0 + TS], vmc[:, b, m, h * XD:(h + 1) * XD], scs[:, m, c0:c0 + TS],
                                 start=(m == 0), stop=(m == 1))
            filled(ins, "cos")
            pe.wait_ge(S("xoT_p"), XH)
            pe.wait_ge(S("xoT_s"), 1)
            for j in range(KD):
                s = slot(pe, W_XO + j // 2)
                project(("xo", j), lambda k: ring[:, s, (j % 2) * 4 + k, :], xoT, XH)
            sums("ff", [("ms_ff", 0), ("ms_ff", 1)], mixT, KD)
            pe.wait_ge(S("normed"), normed["ff"] + KD)
            meet(pe, 6)

            with pe.Fori(0, KF // 8) as i:
                for j in range(8):
                    n = W_F1 + j
                    s = n % SLOTS
                    pe.wait_ge(slot_in[s], i * 16 + 16 * (n // SLOTS + 1))
                    outs = [reopen(pe, ("f1", j, c), i, 2) for c in range(2)]
                    for k in range(KD):
                        for c in range(2):
                            ins = mm(outs[c][:, 0:HALF], ring[:, s, k, :], hTk[:, k, c * HALF:(c + 1) * HALF],
                                     start=(k == 0), stop=(k == KD - 1))
                            if k == KD - 1:
                                filled(ins, ("f1", j, c))
            pe.wait_ge(S("uT"), 2 * KF)
            with pe.Fori(0, KD // 2) as i:
                for j in range(2):
                    outs = [reopen(pe, ("f2", j, c), i, 1) for c in range(2)]
                    for q in range(4):
                        n = W_F2 + 4 * j + q
                        s = n % SLOTS
                        pe.wait_ge(slot_in[s], i * 16 + 16 * (n // SLOTS + 1))
                        for k in range(8):
                            for c in range(2):
                                ins = mm(outs[c][:, 0:HALF], ring[:, s, k, :],
                                         uT[:, q * 8 + k, c * HALF:(c + 1) * HALF],
                                         start=(q == 0 and k == 0), stop=(q == 3 and k == 7))
                                if q == 3 and k == 7:
                                    filled(ins, ("f2", j, c))
                        if q < 3:
                            ins.then_inc(S("f2_used"), 1)
            pe.wait_ge(S("y_T"), 2 * KD)
            for t in range(TILES):
                c0, m = cols(t)
                for c in range(2):
                    o = reopen(pe, ("y", t, c))
                    for k in range(4):
                        ins = tr(o[0:m, k * P:(k + 1) * P], xT[:, 4 * c + k, c0:c0 + m], ident)
                    filled(ins, ("y", t, c))

        @block.scalar
        def _(act):
            link = Chain(act, "act_step")
            A = nc.scalar.activation

            def rsqrt_sums(keys, scale, width=HALF, extra=None):
                for c, key in enumerate(keys):
                    o = full(act, key)
                    freed(A(rstd[:, c * width:(c + 1) * width], o[:, 0:width], ACT.Ln, bias=epsc, scale=scale), key)
                for key in keys:
                    b, n = PLAN[key]
                    act.wait_ge(bank_free[b], n)
                w = width * len(keys)
                A(rstd[:, 0:w], rstd[:, 0:w], ACT.Exp, scale=-0.5,
                  **({} if extra is None else {"bias": extra})).then_inc(S("rstd"), 1)

            act.wait_ge(S("const_in"), 48)
            for j in (0, 2):
                o = full(act, ("memT", j))
                freed(nc.scalar.copy(memT[:, 2 * j:2 * j + 2, :], o[:, :].rearrange("p (a b) -> p a b", a=2)), ("memT", j))
            for k in range(KD):
                b, n = PLAN[("memT", k // 2)]
                act.wait_ge(bank_free[b], n)
                A(sq1[:, k, 0:NM], memT[:, k, :], ACT.Square).then_inc(S("squares"), 1)
            rsqrt_sums(["ms_mem"], 1.0 / D, width=NM)
            for t in range(2):
                o = full(act, ("xk", t))
                link(nc.scalar.copy(km_p[:, t, :], o[:, :]))
                freed(A(sq1[:, 4 + t, 0:512], o[:, :], ACT.Square), ("xk", t))
            act.wait_ge(S("ss_km"), 1)
            link(A(stat[:, 8:16], stat[:, 0:8], ACT.Ln, bias=epsc, scale=1.0 / XD))
            A(stat[:, 8:16], stat[:, 8:16], ACT.Exp, scale=-0.5).then_inc(S("r_km"), 1)
            act.wait_ge(S("r_km"), 1)
            for k in range(0, KD, 2):
                o = full(act, ("xT", k))
                freed(nc.scalar.copy(xT[:, k, 0:TP], o[:, :]), ("xT", k))
            o = full(act, "xTs")
            freed(nc.scalar.copy(xT[:, :, TP:NT], o[:, :].rearrange("p (k c) -> p k c", k=KD)), "xTs")
            b, n = PLAN["xTs"]
            act.wait_ge(bank_free[b], n)
            act.wait_ge(S("km"), 1)
            for k in range(KD):
                b, n = PLAN[("xT", k)]
                act.wait_ge(bank_free[b], n)
                A(sq1[:, k, :], xT[:, k, :], ACT.Square).then_inc(S("squares"), 1)
            rsqrt_sums([("ms_mix", 0), ("ms_mix", 1)], 1.0 / D)
            o = full(act, ("kmT", 0))
            freed(nc.scalar.copy(kmT[:, 0, :, :].rearrange("p a b -> p (a b)"), o[:, :]), ("kmT", 0))
            for j in range(12):
                if j == 8:
                    for t in (0, 2, 4):
                        m = cols(t)[1]
                        o = full(act, ("v", t))
                        freed(nc.scalar.copy(vtok[0:m, t, :], o[0:m, :]), ("v", t))
                    for t in (0, 2, 4):
                        m = cols(t)[1]
                        o = full(act, ("kva", t))
                        freed(nc.scalar.copy(kv[0:m, t, :], o[0:m, 0:KR + ROPE]), ("kva", t))
                m = P if j < 11 else 16
                o = full(act, ("z", j, 0))
                freed(nc.scalar.copy(zT[0:m, j, 0:HALF], o[0:m, 0:HALF]), ("z", j, 0))
            meet(act, 1)

            for p in range(2):
                for c in range(2):
                    o = full(act, ("gate", p, c))
                    freed(A(eb[:, p, c * HALF:(c + 1) * HALF], o[:, 0:HALF], ACT.Identity,
                            bias=gn[:, G_BA + p:G_BA + p + 1]), ("gate", p, c))
            for p in range(2):
                for c in range(2):
                    b, n = PLAN[("gate", p, c)]
                    act.wait_ge(bank_free[b], n)
            link(A(ek, eb, ACT.Abs))
            link(A(ek, ek, ACT.Exp, scale=-1.0))
            A(ek, ek, ACT.Ln, bias=1.0).then_inc(S("softplus"), 1)
            act.wait_ge(S("dq"), 3)
            link(A(eq, dq, ACT.Exp, scale=1.0 / TAU))
            A(ek, dq, ACT.Exp, scale=-1.0 / TAU).then_inc(S("e_k"), 1)
            A(eb, gb, ACT.Exp, scale=1.0 / TAU).then_inc(S("e_b"), 1)
            act.wait_ge(S("dl"), 4)
            A(dl, dl, ACT.Exp, scale=1.0 / TAU).then_inc(S("e_l"), 1)
            o = full(act, ("klt", 0))
            freed(nc.scalar.copy(klt[:, 0:4, 0, :], o[:, :].rearrange("p (t c) -> p t c", t=4)), ("klt", 0))
            b, n = PLAN[("klt", 0)]
            act.wait_ge(bank_free[b], n)
            o = full(act, "klts")
            link(nc.scalar.copy(klt[0:NS, 4, :, :], o[0:NS, 0:256].rearrange("p (q c) -> p q c", q=2)))
            act.nop().then_inc(bank_free[PLAN["klts"][0]], 1)
            act.nop().then_inc(S("klt"), 2)
            for t in range(4):
                o = full(act, ("go", t))
                freed(nc.scalar.copy(mixT[:, 0:GH, t * P:(t + 1) * P], o[:, :].rearrange("p (h c) -> p h c", h=GH)),
                      ("go", t))
            o = full(act, "gos")
            freed(nc.scalar.copy(mixT[:, 0:GH, TP:NT], o[:, 0:GH * NS].rearrange("p (h c) -> p h c", h=GH)), "gos")
            for key in [("go", t) for t in range(4)] + ["gos"]:
                b, n = PLAN[key]
                act.wait_ge(bank_free[b], n)
            A(sqg, mixT[:, 0:GH, :], ACT.Square).then_inc(S("sq_gla"), 1)
            A(rs, zT[:, 4:8, :], ACT.Sigmoid).then_inc(S("sig_r"), 1)
            for h in range(GH):
                for c in range(2):
                    o = full(act, ("ms_gla", h, c))
                    freed(A(sqg[:, h, c * HALF:(c + 1) * HALF], o[:, 0:HALF], ACT.Ln, bias=epsc, scale=1.0 / DV),
                          ("ms_gla", h, c))
            for h in range(GH):
                for c in range(2):
                    b, n = PLAN[("ms_gla", h, c)]
                    act.wait_ge(bank_free[b], n)
            A(sqg, sqg, ACT.Exp, scale=-0.5).then_inc(S("rstd_gla"), 1)
            meet(act, 2)

            A(sqa, zT[:, 8:11, :], ACT.Square).then_inc(S("sq_qa"), 1)
            act.wait_ge(S("pads"), 6)
            A(sqf[:, :, 0:KR + ROPE], kv, ACT.Square).then_inc(S("sq_kv"), 1)
            rsqrt_sums([("ms_qa", 0), ("ms_qa", 1)], 1.0 / QR)
            for n in (0, 2):
                o = full(act, ("wkT", n))
                freed(nc.scalar.copy(w_kT[0:MV, 2 * n:2 * n + 2, :].rearrange("p a b -> p (a b)"), o[0:MV, :]),
                      ("wkT", n))
                b, c = PLAN[("wkT", n)]
                act.wait_ge(bank_free[b], c)
                act.nop().then_inc(S("w_kT"), 1)
            act.wait_ge(S("ss_kv"), 2)
            link(A(stat[:, 16:21], stat[:, 0:5], ACT.Ln, bias=epsc, scale=1.0 / KR))
            link(A(stat[:, 21:26], stat[:, 5:10], ACT.Ln, bias=epsc, scale=1.0 / ROPE))
            A(stat[:, 16:26], stat[:, 16:26], ACT.Exp, scale=-0.5).then_inc(S("r_kv"), 1)
            for t in range(TILES):
                m = cols(t)[1]
                o = full(act, ("qf", t, 0))
                freed(nc.scalar.copy(qf[0:m, t, 0:384], o[0:m, 0:384]), ("qf", t, 0))
            for t in range(TILES):
                for c in range(2):
                    b, n = PLAN[("qf", t, c)]
                    act.wait_ge(bank_free[b], n)
            act.wait_ge(S("ckv"), 1)
            A(sqf, qf, ACT.Square).then_inc(S("sq_qf"), 1)
            o = full(act, ("ckT", 0))
            freed(nc.scalar.copy(ckT[:, 0, 0:TP], o[:, :]), ("ckT", 0))
            o = full(act, "ckTs")
            nc.scalar.copy(ckT[:, :, TP:NT], o[:, 0:P].rearrange("p (k c) -> p k c", k=KC))
            act.wait_ge(S("pads"), 6)
            nc.scalar.copy(cknT[:, :, 0:NS], o[:, 0:P].rearrange("p (k c) -> p k c", k=KC))
            link(nc.scalar.copy(kpnT[0:ROPE, 0:NS], o[0:ROPE, P:P + NS]))
            act.nop().then_inc(bank_free[PLAN["ckTs"][0]], 1)
            act.nop().then_inc(S("ckT"), 2)
            for t in range(TILES):
                m = cols(t)[1]
                o = full(act, ("krp", t))
                if t < 4:
                    link(nc.scalar.copy(kfull[:, t, :].rearrange("p (h c) -> p h c", h=MH)[:, :, 0:MV],
                                        o[:, :].rearrange("p (h c) -> p h c", h=MH)))
                if t:
                    act.wait_ge(S("ss_kr"), t)
                A(sqk[0:m, :], o[0:m, :], ACT.Square).then_inc(S("sq_kr"), 1)
                act.wait_ge(S("sq_kr"), t + 1)
                act.nop().then_inc(bank_free[PLAN[("krp", t)][0]], 1)
            act.wait_ge(S("ss_q"), 2)
            link(A(stat[:, 112:152], stat[:, 32:72], ACT.Ln, bias=epsc, scale=1.0 / MV))
            link(A(stat[:, 152:192], stat[:, 72:112], ACT.Ln, bias=epsc, scale=1.0 / ROPE))
            A(stat[:, 112:192], stat[:, 112:192], ACT.Exp, scale=-0.5).then_inc(S("r_q"), 1)
            act.wait_ge(S("ss_kr"), 5)
            link(A(stat[:, 232:272], stat[:, 192:232], ACT.Ln, bias=epsc, scale=1.0 / MV))
            A(stat[:, 232:272], stat[:, 232:272], ACT.Exp, scale=-0.5).then_inc(S("r_kr"), 1)
            for h in range(0, MH, 2):
                o = full(act, ("qT", h))
                freed(nc.scalar.copy(qT[0:MQ, h, :], o[0:MQ, :]), ("qT", h))
            o = full(act, "qTs")
            freed(nc.scalar.copy(qTs[0:MQ, :, :].rearrange("p h c -> p (h c)"), o[0:MQ, :]), "qTs")
            b, n = PLAN["qTs"]
            act.wait_ge(bank_free[b], n)
            act.nop().then_inc(S("qTs"), 1)
            for h in range(0, MH, 2):
                o = full(act, ("kT", h))
                freed(nc.scalar.copy(kT[0:MQ, h, :], o[0:MQ, :]), ("kT", h))
            meet(act, 3)

            steps = [(t, h) for t in range(4) for h in range(MH)]
            for n in range(len(steps) + 5):
                if n < len(steps):
                    t, h = steps[n]
                    o = bank[PLAN[("s", t, h)][0]]
                    act.wait_ge(S("row_max"), n + 1)
                    if n >= 3:
                        full(act, ("pT", *steps[n - 3]))
                    A(pr[:, n % 3, 0:(t + 1) * P], o[:, 0:(t + 1) * P], ACT.Exp, bias=stat[:, 32 + n:33 + n],
                      accum_out=stat[:, 64 + n:65 + n]).then_inc(S("pr"), 1)
                    act.wait_ge(S("pr"), n + 1)
                    act.nop().then_inc(bank_free[PLAN[("s", t, h)][0]], 1)
                if 2 <= n < len(steps) + 2 and n % 2 == 1:
                    t, h = steps[n - 2]
                    o = full(act, ("pT", t, h))
                    wait_prT_free(act, n - 2, steps)
                    nc.scalar.copy(prT[:, 1, 0:(t + 1) * P], o[:, 0:(t + 1) * P]).then_inc(S("prT1"), 1)
                    act.wait_ge(S("prT1"), (n - 2) // 2 + 1)
                    act.nop().then_inc(bank_free[PLAN[("pT", t, h)][0]], 1)
                if n >= 5 and steps[n - 5][1] == MH - 1:
                    t = steps[n - 5][0]
                    o = full(act, ("poT", t))
                    freed(nc.scalar.copy(mixT[:, 4:8, t * P:(t + 1) * P], o[:, :].rearrange("p (j c) -> p j c", j=4)),
                          ("poT", t))
            meet(act, 4)

            def page_square(b, j):
                o = full(act, ("kr", j), b, 8)
                if isinstance(b, int) and b == 0 and j < 2:
                    pass
                else:
                    act.wait_ge(S("ss_pg"), b * NPG + (j - 1))
                freed(A(sqs[:, j % 2, :], o[:, :], ACT.Square), ("kr", j))

            def inverse_norms(b, g):
                act.wait_ge(S("ss_pg"), b * NPG + (4 * g + 4))
                r = stat[:, 128 + 32 * (g % 2):160 + 32 * (g % 2)]
                s = stat[:, 64 + 32 * (g % 2):96 + 32 * (g % 2)]
                if not (isinstance(b, int) and b == 0 and g < 2):
                    act.wait_ge(S("sc_done"), b * 4 + (g - 1))
                A(r, s, ACT.Ln, bias=epsc, scale=1.0 / MV).then_inc(S("ln_pg"), 1)
                act.wait_ge(S("ln_pg"), b * 4 + (g + 1))
                A(r, r, ACT.Exp, scale=-0.5).then_inc(S("r_pg"), 1)

            def rope_keys(b, first):
                o = full(act, "kpt0") if first else full(act, "kpt", b, 4)
                nc.scalar.copy(kpT.rearrange("p a b -> p (a b)"), o[:, :]).then_inc(S("kpT"), 1)
                act.wait_ge(S("kpT"), b + 1)
                act.nop().then_inc(bank_free[7], 1)

            def exponentials(b):
                act.wait_ge(S("sc_minus_max"), b + 1)
                A(pb, pb, ACT.Exp).then_inc(S("pb"), 1)

            def sequence(b, first=False):
                rope_keys(b, first)
                for j in range(NPG):
                    page_square(b, j)
                    if j % 4 == 0 and j:
                        inverse_norms(b, j // 4 - 1)
                    if j == 4 and not first:
                        exponentials(b - 1)
                inverse_norms(b, 3)

            sequence(0, True)
            with act.Fori(0, (NB - 2) // 2) as i:
                sequence(i * 2 + 1)
                sequence(i * 2 + 2)
            sequence(NB - 1)
            exponentials(NB - 1)
            o = full(act, "oms")
            freed(nc.scalar.copy(mixT[:, 4:8, TP:NT], o[:, 0:256].rearrange("p (j c) -> p j c", j=4)), "oms")
            meet(act, 5)

            for k in range(KD):
                act.wait_ge(S("x_mix"), 2 * k + 2)
                if k == 0:
                    full(act, ("wo", KD - 1, 1))
                A(mixT[:, k, :], xT[:, k, :], ACT.Square).then_inc(S("squares"), 1)
            rsqrt_sums([("ms_x", 0), ("ms_x", 1)], 1.0 / D)
            for j in range(XH):
                for c in range(2):
                    o = full(act, ("xq", j, c))
                    freed(nc.scalar.copy(xqT[:, j, c * HALF:(c + 1) * HALF], o[:, 0:HALF]), ("xq", j, c))
                for c in range(2):
                    b, n = PLAN[("xq", j, c)]
                    act.wait_ge(bank_free[b], n)
                A(mixT[:, j, :], xqT[:, j, :], ACT.Square).then_inc(S("sq_xq"), 1)
            for j in range(XH):
                for c in range(2):
                    o = full(act, ("ms_xq", j, c))
                    freed(A(mixT[:, 4 + j, c * HALF:(c + 1) * HALF], o[:, 0:HALF], ACT.Ln, bias=epsc,
                            scale=1.0 / XD), ("ms_xq", j, c))
                for c in range(2):
                    b, n = PLAN[("ms_xq", j, c)]
                    act.wait_ge(bank_free[b], n)
                A(mixT[:, 4 + j, :], mixT[:, 4 + j, :], ACT.Exp, scale=-0.5, bias=lnxc).then_inc(S("r_xq"), 1)
            pairs = [(t, u) for t in range(4) for u in range(2)]
            for n in range(len(pairs) + 2):
                if n < len(pairs):
                    t, u = pairs[n]
                    o = bank[PLAN[("cs", t, u)][0]]
                    act.wait_ge(S("cmax"), n + 1)
                    if n >= 2:
                        full(act, ("cp", *pairs[n - 2]))
                    for e in range(2):
                        A(pcx[:, n % 2, e, :], o[:, e * NM:(e + 1) * NM], ACT.Exp,
                          bias=stat[:, 2 * n + e:2 * n + e + 1],
                          accum_out=stat[:, 16 + 2 * n + e:17 + 2 * n + e]).then_inc(S("pcx_raw"), 1)
                    act.wait_ge(S("pcx_raw"), 2 * n + 2)
                    act.nop().then_inc(bank_free[PLAN[("cs", t, u)][0]], 1)
                if n >= 2:
                    t, u = pairs[n - 2]
                    o = full(act, ("cp", t, u))
                    nc.scalar.copy(pcxT[:, 2 * u:2 * u + 2, :, t * P:(t + 1) * P],
                                   o[:, :].rearrange("p (e m c) -> p e m c", e=2, m=2)).then_inc(S("pcxT"), 1)
                    act.wait_ge(S("pcxT"), n - 1)
                    act.nop().then_inc(bank_free[PLAN[("cp", t, u)][0]], 1)
            for h in range(XH):
                o = full(act, ("co", h))
                nc.scalar.copy(xoT[:, h, 0:TP], o[:, :]).then_inc(S("xoT_p"), 1)
                act.wait_ge(S("xoT_p"), h + 1)
                act.nop().then_inc(bank_free[PLAN[("co", h)][0]], 1)
            for b in range(NB):
                for m in range(2):
                    o = full(act, ("ck", b, m))
                    if b >= 2 and m == 0:
                        act.wait_ge(S("kmcT_used"), b - 1)
                    nc.scalar.copy(kmcT[:, b % 2, m, :, :].rearrange("p a b -> p (a b)"), o[:, :]).then_inc(S("kmcT"), 1)
                    act.wait_ge(S("kmcT"), 2 * b + m + 1)
                    act.nop().then_inc(bank_free[PLAN[("ck", b, m)][0]], 1)
            act.wait_ge(S("scs_raw"), 2)
            A(scs, scs, ACT.Exp).then_inc(S("scs"), 1)
            for k in range(KD):
                act.wait_ge(S("x_cross"), 2 * k + 2)
                A(mixT[:, k, :], xT[:, k, :], ACT.Square).then_inc(S("squares"), 1)
            rsqrt_sums([("ms_ff", 0), ("ms_ff", 1)], 1.0 / D)
            meet(act, 6)

            with act.Fori(0, KF // 8) as i:
                for j in range(8):
                    for c in range(2):
                        o = full(act, ("f1", j, c), i, 2)
                        freed(A(uT[:, bass.ds(i * 8 + j, 1), c * HALF:(c + 1) * HALF].rearrange("p a c -> p (a c)"),
                                o[:, 0:HALF], ACT.Relu), ("f1", j, c))
            for t in range(TILES):
                m = cols(t)[1]
                o = full(act, ("y", t, 0))
                if t >= 2:
                    act.wait_ge(S(f"y_out{t % 2}"), 16 * (t // 2))
                nc.scalar.copy(ytok[0:m, t % 2, 0:512], o[0:m, :]).then_inc(S("ytok_left"), 1)
                act.wait_ge(S("ytok_left"), t + 1)
                act.nop().then_inc(bank_free[PLAN[("y", t, 0)][0]], 1)

        @block.vector
        def _(dve):
            link = Chain(dve, "dve_step")
            V = nc.vector

            def scaled(name, src, dst, g0, n_k, width=NT):
                dve.wait_ge(S("rstd"), rstds[name] + 1)
                for k in range(n_k):
                    V.scalar_tensor_tensor(out=dst[:, k, 0:width], in0=src[:, k, 0:width],
                                           scalar=gn[:, g0 + k:g0 + k + 1], in1=rstd[:, 0:width],
                                           op0=ALU.mult, op1=ALU.mult).then_inc(S("normed"), 1)

            dve.wait_ge(S("const_in"), 48)
            for j in (1, 3):
                o = full(dve, ("memT", j))
                freed(V.tensor_copy(memT[:, 2 * j:2 * j + 2, :], o[:, :].rearrange("p (a b) -> p a b", a=2)), ("memT", j))
            for j in range(4):
                b, n = PLAN[("memT", j)]
                dve.wait_ge(bank_free[b], n)
            scaled("mem", memT, hmT, G_MEM, KD, width=NM)
            b, n = PLAN[("xk", 1)]
            dve.wait_ge(bank_free[b], n)
            V.tensor_reduce(stat[:, 0:8].rearrange("p (t h) -> p t h", t=2),
                            sq1[:, 4:6, 0:512].rearrange("p t (h d) -> p t h d", h=XH), AX.X, ALU.add).then_inc(S("ss_km"), 1)
            for t in range(2):
                o = full(dve, ("xv", t))
                V.tensor_copy(vm_p[:, t, :], o[:, :]).then_inc(S("vm"), 1)
                dve.wait_ge(S("vm"), t + 1)
                dve.nop().then_inc(bank_free[PLAN[("xv", t)][0]], 1)
            dve.wait_ge(S("r_km"), 1)
            km8 = km_p.rearrange("p t (h d) -> p (t h) d", h=XH)
            link(V.tensor_tensor(km8, km8, spread(stat[:, 8:16], 2, XD), ALU.mult))
            V.tensor_tensor(km8, km8, spread(row[:, R_XK:R_XK + XD], 1, 8), ALU.mult).then_inc(S("km"), 1)
            for k in range(1, KD, 2):
                o = full(dve, ("xT", k))
                freed(V.tensor_copy(xT[:, k, 0:TP], o[:, :]), ("xT", k))
            for key in [("xT", k) for k in range(KD)] + ["xTs"]:
                b, n = PLAN[key]
                dve.wait_ge(bank_free[b], n)
            full(dve, ("kmT", 1))
            dve.wait_ge(S("mk_out"), 16)
            scaled("mix", xT, hTk, G_MIX, KD)
            o = full(dve, ("kmT", 1))
            freed(V.tensor_copy(kmT[:, 1, :, :].rearrange("p a b -> p (a b)"), o[:, :]), ("kmT", 1))
            for j in range(12):
                if j == 8:
                    for t in (1, 3):
                        o = full(dve, ("v", t))
                        freed(V.tensor_copy(vtok[:, t, :], o[:, :]), ("v", t))
                    for t in (1, 3):
                        o = full(dve, ("kva", t))
                        freed(V.tensor_copy(kv[:, t, :], o[:, 0:KR + ROPE]), ("kva", t))
                m = P if j < 11 else 16
                o = full(dve, ("z", j, 1))
                freed(V.tensor_copy(zT[0:m, j, HALF:NT], o[0:m, 0:HALF]), ("z", j, 1))
            meet(dve, 1)

            dve.wait_ge(S("softplus"), 1)
            link(V.scalar_tensor_tensor(out=ek, in0=eb, scalar=0.0, in1=ek, op0=ALU.min, op1=ALU.subtract))
            for p in range(2):
                link(V.tensor_tensor_scan(gb[:, p, :], scanm, ek[:, p, :], 0.0, ALU.mult, ALU.add))

            def chunks(ap, p, prompt=True):
                return (ap[:, p, 0:TP].rearrange("p (c t) -> p c t", c=4) if prompt
                        else ap[:, p, TP:NT].rearrange("p (c t) -> p c t", c=NB))

            for p in range(2):
                g = chunks(gb, p)
                V.tensor_tensor(chunks(dq, p), g, g[:, :, 63:64].broadcast_to([P, 4, P]), ALU.subtract).then_inc(S("dq"), 1)
            link(V.tensor_copy(dq[:, :, TP:NT], gb[:, :, TP:NT]))
            dve.wait_ge(S("dq"), 2)
            V.tensor_scalar(dq, dq, CLAMP, -CLAMP, ALU.min, ALU.max).then_inc(S("dq"), 1)
            for p in range(2):
                g, gs = chunks(gb, p), chunks(gb, p, False)
                V.tensor_tensor(chunks(dl, p), g[:, :, P - 1:P].broadcast_to([P, 4, P]), g, ALU.subtract).then_inc(S("dl"), 1)
                V.tensor_tensor(chunks(dl, p, False), gs[:, :, TS - 1:TS].broadcast_to([P, NB, TS]), gs,
                                ALU.subtract).then_inc(S("dl"), 1)
            dve.wait_ge(S("pads2"), 2)
            for dst, e, sem in ((qz, eq, "e_k"), (qi, eb, "e_b")):
                dve.wait_ge(S(sem), 1)
                for h in range(2):
                    for p in range(2):
                        r = slice(64 * h, 64 * h + 64)
                        V.scalar_tensor_tensor(out=dst[r, p, h, :], in0=zT[r, p, :], scalar=float(DK) ** -0.5,
                                               in1=e[r, p, :], op0=ALU.mult, op1=ALU.mult).then_inc(S("qz"), 1)
            o = full(dve, ("klt", 1))
            V.tensor_copy(klt[:, 0:4, 1, :], o[:, :].rearrange("p (t c) -> p t c", t=4)).then_inc(S("klt"), 1)
            dve.wait_ge(S("klt"), 3)
            dve.nop().then_inc(bank_free[PLAN[("klt", 1)][0]], 1)
            for t in range(4):
                o = full(dve, ("att", t))
                V.tensor_tensor(att[:, t, :, :], o[:, :].rearrange("p (h c) -> p h c", h=GH), spread(tri, 1, GH),
                                ALU.mult).then_inc(S("att"), 1)
                dve.wait_ge(S("att"), t + 1)
                dve.nop().then_inc(bank_free[PLAN[("att", t)][0]], 1)
            o = full(dve, "atts")
            V.tensor_tensor(atts[0:NS, :, :], o[0:NS, 0:256].rearrange("p (h c) -> p h c", h=GH),
                            spread(smask, 1, GH), ALU.mult).then_inc(S("att"), 1)
            dve.wait_ge(S("att"), 5)
            dve.nop().then_inc(bank_free[PLAN["atts"][0]], 1)

            def masked_keys(b):
                V.tensor_scalar(klm[0:NS, b % 2, :, :], klt[0:NS, 4, :, :], seqm[:, b:b + 1], None,
                                ALU.mult).then_inc(S("klm"), 1)

            dve.wait_ge(S("qz"), 8)
            for t in range(4):
                o = full(dve, ("st", t))
                for h in range(2):
                    for p in range(2):
                        r = slice(64 * h, 64 * h + 64)
                        upd = o[r, p * 256 + h * P:p * 256 + (h + 1) * P]
                        if t == 0:
                            ins = V.tensor_copy(st[r, p, :], upd)
                        else:
                            ins = V.scalar_tensor_tensor(out=st[r, p, :], in0=st[r, p, :],
                                                         scalar=eb[r, p, t * P + P - 1:(t + 1) * P], in1=upd,
                                                         op0=ALU.mult, op1=ALU.add)
                        ins.then_inc(S("gla_state"), 1)
                dve.wait_ge(S("gla_state"), 4 * t + 4)
                dve.nop().then_inc(bank_free[PLAN[("st", t)][0]], 1)
            masked_keys(0)
            masked_keys(1)
            dve.wait_ge(S("state_in"), 16)
            for b in range(NB):
                o = full(dve, ("sst", b))
                for h in range(2):
                    for p in range(2):
                        r = slice(64 * h, 64 * h + 64)
                        c = TP + b * TS + TS - 1
                        V.scalar_tensor_tensor(out=st_s[r, b, p, :], in0=st_s[r, b, p, :], scalar=eb[r, p, c:c + 1],
                                               in1=o[r, p * 256 + h * P:p * 256 + (h + 1) * P],
                                               op0=ALU.mult, op1=ALU.add).then_inc(S("gla_state_s"), 1)
                dve.wait_ge(S("gla_state_s"), 4 * b + 4)
                dve.nop().then_inc(bank_free[PLAN[("sst", b)][0]], 1)
                if b + 2 < NB:
                    masked_keys(b + 2)
            dve.wait_ge(S("rstd_gla"), 1)
            link(V.scalar_tensor_tensor(out=mixT[:, 0:GH, :], in0=mixT[:, 0:GH, :], scalar=gn[:, G_GLA:G_GLA + 1],
                                        in1=sqg, op0=ALU.mult, op1=ALU.mult))
            dve.wait_ge(S("rs"), 1)
            V.tensor_tensor(mixT[:, 0:GH, :], mixT[:, 0:GH, :], rs, ALU.mult)
            meet(dve, 2)

            def rotate(v, c, s, n, tmp):
                a, b = v[..., 0:16], v[..., 16:32]
                link(V.tensor_tensor(tmp[0], a, c, ALU.mult))
                link(V.tensor_tensor(tmp[1], b, s, ALU.mult))
                link(V.tensor_tensor(tmp[2], b, c, ALU.mult))
                link(V.tensor_tensor(tmp[3], a, s, ALU.mult))
                link(V.tensor_tensor(a, tmp[0], tmp[1], ALU.subtract))
                return V.tensor_tensor(b, tmp[2], tmp[3], ALU.add)

            link(V.tensor_scalar(gq2, row[:, R_QN:R_QN + MV], MLA_SCALE, None, ALU.mult))
            link(V.tensor_tensor(gq2, gq2, row[:, R_KN:R_KN + MV], ALU.mult))
            link(V.tensor_scalar(gqr, row[:, R_QR:R_QR + ROPE], MLA_SCALE, None, ALU.mult))
            dve.wait_ge(S("sq_kv"), 1)
            V.tensor_reduce(stat[:, 0:5], sqf[:, :, 0:KR], AX.X, ALU.add).then_inc(S("ss_kv"), 1)
            V.tensor_reduce(stat[:, 5:10], sqf[:, :, KR:KR + ROPE], AX.X, ALU.add).then_inc(S("ss_kv"), 1)
            scaled("qa", zT[:, 8:11, :], zT[:, 8:11, :], G_QA, KQ)
            for n in (1, 3):
                o = full(dve, ("wkT", n))
                link(V.tensor_copy(w_kT[0:MV, 2 * n:2 * n + 2, :].rearrange("p a b -> p (a b)"), o[0:MV, :]))
                dve.nop().then_inc(S("w_kT"), 1)
                dve.nop().then_inc(bank_free[PLAN[("wkT", n)][0]], 1)
            dve.wait_ge(S("r_kv"), 1)
            lat, kpe = kv[:, :, 0:KR], kv[:, :, KR:KR + ROPE]
            link(V.tensor_tensor(lat, lat, spread(stat[:, 16:21], 2, KR), ALU.mult))
            link(V.tensor_tensor(lat, lat, spread(row[:, R_KVA:R_KVA + KR], 1, TILES), ALU.mult))
            link(V.tensor_tensor(kpe, kpe, spread(stat[:, 21:26], 2, ROPE), ALU.mult))
            link(V.tensor_tensor(kpe, kpe, spread(row[:, R_KR:R_KR + ROPE], 1, TILES), ALU.mult))
            ktmp = [view(stat, 272 + 80 * n, TILES, 16) for n in range(4)]
            rotate(kpe, cosn, sinn, None, ktmp).then_inc(S("ckv"), 1)
            for t in range(TILES):
                m = cols(t)[1]
                o = full(dve, ("qf", t, 1))
                freed(V.tensor_copy(qf[0:m, t, 384:768], o[0:m, 0:384]), ("qf", t, 1))
            o = full(dve, ("ckT", 1))
            V.tensor_copy(ckT[:, 1, 0:TP], o[:, :]).then_inc(S("ckT"), 1)
            dve.drain()
            dve.nop().then_inc(bank_free[PLAN[("ckT", 1)][0]], 1)
            dve.wait_ge(S("sq_qf"), 1)
            s8 = sqf.rearrange("p t (h c) -> p (t h) c", h=MH)
            q8 = qf.rearrange("p t (h c) -> p (t h) c", h=MH)
            V.tensor_reduce(stat[:, 32:72], s8[:, :, 0:MV], AX.X, ALU.add).then_inc(S("ss_q"), 1)
            V.tensor_reduce(stat[:, 72:112], s8[:, :, MV:MQ], AX.X, ALU.add).then_inc(S("ss_q"), 1)

            def key_sums(t):
                m = cols(t)[1]
                dve.wait_ge(S("sq_kr"), t + 1)
                V.tensor_reduce(stat[0:m, 192 + 8 * t:200 + 8 * t], sqk[0:m, :].rearrange("p (h c) -> p h c", h=MH),
                                AX.X, ALU.add).then_inc(S("ss_kr"), 1)

            for t in range(TILES):
                key_sums(t)
            dve.wait_ge(S("r_q"), 1)
            link(V.tensor_tensor(q8[:, :, 0:MV], q8[:, :, 0:MV], spread(stat[:, 112:152], 2, MV), ALU.mult))
            link(V.tensor_tensor(q8[:, :, 0:MV], q8[:, :, 0:MV], spread(gq2, 1, 40), ALU.mult))
            link(V.tensor_tensor(q8[:, :, MV:MQ], q8[:, :, MV:MQ], spread(stat[:, 152:192], 2, ROPE), ALU.mult))
            link(V.tensor_tensor(q8[:, :, MV:MQ], q8[:, :, MV:MQ], spread(gqr, 1, 40), ALU.mult))
            qr = qf.rearrange("p t (h c) -> p t h c", h=MH)[:, :, :, MV:MQ]
            qtmp = [view(arena, 15396 + 640 * n, TILES, MH, 16) for n in range(4)]
            rotate(qr, spread(cosn, 2, MH), spread(sinn, 2, MH), None, qtmp).then_inc(S("q_ready"), 1)
            dve.wait_ge(S("q_ready"), 1)
            full(dve, ("ms_qa", 1))
            V.tensor_copy(qp4[0:NS, :, :].rearrange("p h (q c) -> p h q c", q=4),
                          spread(qf[0:NS, 4, :].rearrange("p (h c) -> p h c", h=MH)[:, :, MV:MQ], 2, 4)
                          ).then_inc(S("qp4"), 1)
            for t in range(4):
                o = full(dve, ("vp", t))
                freed(V.tensor_copy(vp[:, t, :], o[:, :]), ("vp", t))
            dve.wait_ge(S("r_kr"), 1)
            k8 = kfull.rearrange("p t (h c) -> p (t h) c", h=MH)
            V.tensor_tensor(k8[:, :, 0:MV], k8[:, :, 0:MV], spread(stat[:, 232:264], 2, MV), ALU.mult).then_inc(
                S("kfull"), 1)
            for h in range(1, MH, 2):
                o = full(dve, ("qT", h))
                freed(V.tensor_copy(qT[0:MQ, h, :], o[0:MQ, :]), ("qT", h))
            for k in range(KC):
                o = full(dve, ("qabs", k))
                freed(V.tensor_copy(qabs[:, k, :, :].rearrange("p b (h t) -> p h b t", h=MH),
                                    o[:, :].rearrange("p (h b t) -> p h b t", h=MH, b=NB)), ("qabs", k))
            dve.wait_ge(S("pads"), 6)
            o = full(dve, "qpd")
            for q in range(4):
                r = slice(32 * q, 32 * q + 32)
                ins = V.tensor_copy(qpd[r, :, q, :].rearrange("p b (h t) -> p h b t", h=MH),
                                    o[r, :].rearrange("p (h b t) -> p h b t", h=MH, b=NB))
            link(ins)
            dve.nop().then_inc(bank_free[PLAN["qpd"][0]], 1)
            for h in range(1, MH, 2):
                o = full(dve, ("kT", h))
                freed(V.tensor_copy(kT[0:MQ, h, :], o[0:MQ, :]), ("kT", h))
            V.tensor_copy(stat[0:NS, 264 + 16:264 + 24], stat[0:NS, 264:272])
            meet(dve, 3)

            steps = [(t, h) for t in range(4) for h in range(MH)]
            for n in range(len(steps) + 5):
                if n < len(steps):
                    t, h = steps[n]
                    o = full(dve, ("s", t, h))
                    link(V.tensor_tensor(o[:, t * P:(t + 1) * P], o[:, t * P:(t + 1) * P], causal, ALU.add))
                    V.tensor_reduce(stat[:, 32 + n:33 + n], o[:, 0:(t + 1) * P], AX.X, ALU.max, negate=True).then_inc(
                        S("row_max"), 1)
                if 2 <= n < len(steps) + 2 and n % 2 == 0:
                    t, h = steps[n - 2]
                    o = full(dve, ("pT", t, h))
                    wait_prT_free(dve, n - 2, steps)
                    V.tensor_copy(prT[:, 0, 0:(t + 1) * P], o[:, 0:(t + 1) * P]).then_inc(S("prT0"), 1)
                    dve.wait_ge(S("prT0"), (n - 2) // 2 + 1)
                    dve.nop().then_inc(bank_free[PLAN[("pT", t, h)][0]], 1)
                if 4 <= n < len(steps) + 4 and steps[n - 4][1] == MH - 1:
                    t = steps[n - 4][0]
                    o = full(dve, ("po", t))
                    dve.wait_ge(S("pr"), 8 * t + 8)
                    link(V.reciprocal(stat[:, 0:8], stat[:, 64 + 8 * t:72 + 8 * t]))
                    if t >= 2:
                        full(dve, ("poT", t - 2))
                    V.tensor_tensor(ot[:, t % 2, :].rearrange("p (h c) -> p h c", h=MH),
                                    o[:, :].rearrange("p (h c) -> p h c", h=MH), spread(stat[:, 0:8], 2, MV),
                                    ALU.mult).then_inc(S("ot"), 1)
                    dve.wait_ge(S("ot"), t + 1)
                    dve.nop().then_inc(bank_free[PLAN[("po", t)][0]], 1)
            meet(dve, 4)

            V.memset(mx, 0.0)
            V.memset(pcs, 0.0)
            link(V.memset(sc[:, NPG, :], NEG))

            def turned(b, n):
                o = full(dve, ("ct", n), b, 4)
                if not (isinstance(b, int) and b == 0 and n < 2):
                    m = n - 2 if n >= 2 else n + 6
                    bb = b if n >= 2 else b - 1
                    if m % 2 == 0:
                        dve.wait_ge(S("cT_used"), bb * 4 + (m // 2 + 1))
                    else:
                        full(dve, ("sc", m // 2), bb, 2)
                V.tensor_copy(cT[:, n % 2, :, :, :].rearrange("p a b c -> p (a b c)"), o[:, :]).then_inc(S("cT"), 1)
                dve.wait_ge(S("cT"), b * 8 + (n + 1))
                dve.nop().then_inc(bank_free[n % 2], 1)

            def page_sums(b, j):
                o = bank_free[2 + j % 2]
                dve.wait_ge(o, b * 8 + (PLAN[("kr", j)][1]))
                g = (j // 4) % 2
                V.tensor_reduce(stat[:, 64 + 32 * g + 8 * (j % 4):72 + 32 * g + 8 * (j % 4)],
                                sqs[:, j % 2, :].rearrange("p (h c) -> p h c", h=MH), AX.X, ALU.add).then_inc(
                    S("ss_pg"), 1)

            def group_scores(b, g):
                o = full(dve, ("sc", g), b, 2)
                dve.wait_ge(S("r_pg"), b * 4 + (g + 1))
                s4 = sc[:, 4 * g:4 * g + 4, :]
                r = stat[:, 128 + 32 * (g % 2):160 + 32 * (g % 2)]
                V.tensor_tensor(s4.rearrange("p j (h t) -> p (j h) t", h=MH),
                                o[:, 0:256].rearrange("p (j t) -> p j t", t=TS), spread(r, 2, TS), ALU.mult).then_inc(
                    S("sc_done"), 1)
                dve.wait_ge(S("sc_done"), b * 4 + (g + 1))
                V.tensor_tensor(s4.rearrange("p j c -> p (j c)"), s4.rearrange("p j c -> p (j c)"), o[:, 256:512],
                                ALU.add).then_inc(S("sc_sum"), 1)
                dve.wait_ge(S("sc_sum"), b * 4 + (g + 1))
                dve.nop().then_inc(bank_free[4 + g % 2], 1)

            def new_scores(b):
                o = full(dve, "scn", b, 2)
                sn = sc[0:NS, NPG, :]
                V.tensor_tensor(sn.rearrange("p (h t) -> p h t", h=MH), o[0:NS, 0:64].rearrange("p (h t) -> p h t", h=MH),
                                spread(stat[0:NS, 280:288], 2, TS), ALU.mult).then_inc(S("scn_a"), 1)
                dve.wait_ge(S("scn_a"), b + 1)
                V.tensor_tensor(sn, sn, o[0:NS, 64:128], ALU.add).then_inc(S("scn_b"), 1)
                dve.wait_ge(S("scn_b"), b + 1)
                dve.nop().then_inc(bank_free[6], 1)
                V.tensor_tensor(sn.rearrange("p (h t) -> p h t", h=MH), sn.rearrange("p (h t) -> p h t", h=MH),
                                spread(sneg[:, bass.ds(b * TS, TS)], 1, MH), ALU.add).then_inc(S("scn_c"), 1)
                dve.wait_ge(S("scn_c"), b + 1)
                dve.wait_ge(S("sc_sum"), b * 4 + 4)
                V.tensor_reduce(mx[:, 0:64], sc.rearrange("p j c -> p c j"), AX.X, ALU.max).then_inc(S("mx"), 1)

            def row_max(b, last=""):
                o = full(dve, "mt" + last, b, 4)
                V.tensor_reduce(stat[0:64, 200:201], o[0:64, 0:P], AX.X, ALU.max, negate=True).then_inc(S("nmx"), 1)
                dve.wait_ge(S("nmx"), b + 1)
                dve.nop().then_inc(bank_free[7], 1)
                V.tensor_scalar(dg[0:64, :], ident[0:64, 0:64], stat[0:64, 200:201], None, ALU.mult).then_inc(S("dg"), 1)

            def minus_max(b, last=""):
                o = full(dve, "mb" + last, b, 4)
                if not (isinstance(b, int) and b == 0):
                    dve.wait_ge(S("pv_out"), b)
                V.tensor_tensor(pb, sc, spread(o[:, 0:64], 1, NPG + 1), ALU.add).then_inc(S("sc_minus_max"), 1)
                dve.wait_ge(S("sc_minus_max"), b + 1)
                dve.nop().then_inc(bank_free[7], 1)

            def divide(b):
                o = full(dve, "pv", b, 2)
                V.reciprocal(stat[0:64, 201:202], o[0:64, KR:KR + 1]).then_inc(S("pv_r"), 1)
                dve.wait_ge(S("pv_r"), b + 1)
                if not (isinstance(b, int) and b == 0):
                    dve.wait_ge(S("pcT"), b)
                V.tensor_scalar(pcs[0:64, :], o[0:64, 0:KR], stat[0:64, 201:202], None, ALU.mult).then_inc(S("pcs"), 1)
                dve.wait_ge(S("pcs"), b + 1)
                dve.nop().then_inc(bank_free[6], 1)
                dve.nop().then_inc(S("pv_out"), 1)

            def keep(b, last=""):
                o = full(dve, "pct" + last, b, 4)
                V.tensor_copy(pcT[:, :, :, bass.ds(b * TS, TS)],
                              o[:, 0:KC * P].rearrange("p (k h t) -> p k h t", k=KC, h=2 * MH)[:, :, 0:MH, :]).then_inc(S("pcT"), 1)
                dve.wait_ge(S("pcT"), b + 1)
                dve.nop().then_inc(bank_free[7], 1)

            def sequence(b, first=False):
                turned(b, 0)
                for n in range(8):
                    if n < 7:
                        turned(b, n + 1)
                    if n == 2:
                        if not first:
                            pass
                    page_sums(b, 2 * n)
                    if not first and n == 1:
                        row_max(b - 1)
                    page_sums(b, 2 * n + 1)
                    if not first and n == 1:
                        minus_max(b - 1)
                    if n in (2, 4, 6):
                        group_scores(b, n // 2 - 1)
                    if not first and n == 4:
                        divide(b - 1)
                    if not first and n == 5:
                        keep(b - 1)
                group_scores(b, 3)
                new_scores(b)

            sequence(0, True)
            with dve.Fori(0, (NB - 2) // 2) as i:
                sequence(i * 2 + 1)
                sequence(i * 2 + 2)
            sequence(NB - 1)
            row_max(NB - 1, "_last")
            minus_max(NB - 1, "_last")
            divide(NB - 1)
            keep(NB - 1, "_last")
            meet(dve, 5)

            def add_to_x(name, sem):
                for j in range(KD):
                    for c in range(2):
                        o = full(dve, (name, j, c))
                        r = xT[:, j, c * HALF:(c + 1) * HALF]
                        V.tensor_tensor(r, r, o[:, 0:HALF], ALU.add).then_inc(S(sem), 1)
                        dve.wait_ge(S(sem), 2 * j + c + 1)
                        dve.nop().then_inc(bank_free[PLAN[(name, j, c)][0]], 1)

            add_to_x("wo", "x_mix")
            scaled("x", xT, hTk, G_X, KD)
            for j in range(XH):
                dve.wait_ge(S("r_xq"), j + 1)
                V.scalar_tensor_tensor(out=xqT[:, j, :], in0=xqT[:, j, :], scalar=gn[:, G_XQ:G_XQ + 1],
                                       in1=mixT[:, 4 + j, :], op0=ALU.mult, op1=ALU.mult).then_inc(S("xq"), 1)
            pairs = [(t, u) for t in range(4) for u in range(2)]
            for n in range(len(pairs) + 1):
                if n < len(pairs):
                    o = full(dve, ("cs", *pairs[n]))
                    V.tensor_reduce(stat[:, 2 * n:2 * n + 2], o[:, :].rearrange("p (e c) -> p e c", e=2), AX.X, ALU.max,
                                    negate=True).then_inc(S("cmax"), 1)
                if n >= 1:
                    m = n - 1
                    dve.wait_ge(S("pcx_raw"), 2 * m + 2)
                    link(V.reciprocal(stat[:, 32 + 2 * m:34 + 2 * m], stat[:, 16 + 2 * m:18 + 2 * m]))
                    V.tensor_tensor(pcx[:, m % 2, :, :], pcx[:, m % 2, :, :],
                                    spread(stat[:, 32 + 2 * m:34 + 2 * m], 2, NM), ALU.mult).then_inc(S("pcx"), 1)
            o = full(dve, "css")
            for m in range(2):
                ins = V.tensor_copy(scs[:, m, :], o[:, m * 256:(m + 1) * 256])
            link(ins)
            dve.nop().then_inc(bank_free[PLAN["css"][0]], 1)
            V.tensor_tensor(mxc, scs[:, 0, :], scs[:, 1, :], ALU.max).then_inc(S("mxc"), 1)
            o = full(dve, "cmt")
            link(V.tensor_reduce(stat[:, 50:52], o[:, 0:256].rearrange("p (e c) -> p e c", e=2), AX.X, ALU.max, negate=True))
            dve.nop().then_inc(bank_free[PLAN["cmt"][0]], 1)
            for e in range(2):
                V.tensor_scalar(dgc[:, e, :], ident, stat[:, 50 + e:51 + e], None, ALU.mult).then_inc(S("dgc"), 1)
            o = full(dve, "cmb")
            for m in range(2):
                V.tensor_tensor(scs[:, m, :], scs[:, m, :], o[:, 0:256], ALU.add).then_inc(S("scs_raw"), 1)
            dve.wait_ge(S("scs_raw"), 2)
            dve.nop().then_inc(bank_free[PLAN["cmb"][0]], 1)
            o = full(dve, "cl")
            link(V.reciprocal(lrc, o[:, 0:256]))
            dve.nop().then_inc(bank_free[PLAN["cl"][0]], 1)
            o = full(dve, "cos")
            V.tensor_tensor(xoT[:, :, TP:NT].rearrange("p h (b t) -> p b h t", b=NB),
                            o[:, 0:256].rearrange("p (b h t) -> p b h t", b=NB, h=XH),
                            lrc.rearrange("p (b h t) -> p b h t", b=NB, h=XH), ALU.mult).then_inc(S("xoT_s"), 1)
            dve.wait_ge(S("xoT_s"), 1)
            dve.nop().then_inc(bank_free[PLAN["cos"][0]], 1)
            add_to_x("xo", "x_cross")
            scaled("ff", xT, hTk, G_FF, KD)
            meet(dve, 6)

            with dve.Fori(0, KF // 8) as i:
                for j in range(8):
                    for c in range(2):
                        b, n = at(("f1", j, c), i, 2)
                        dve.wait_ge(bank_free[b], n)
                        u = uT[:, bass.ds(i * 8 + j, 1), c * HALF:(c + 1) * HALF].rearrange("p a c -> p (a c)")
                        V.tensor_tensor(u, u, u, ALU.mult).then_inc(S("uT"), 1)
            with dve.Fori(0, KD // 2) as i:
                for j in range(2):
                    for c in range(2):
                        o = full(dve, ("f2", j, c), i, 1)
                        r = xT[:, bass.ds(i * 2 + j, 1), c * HALF:(c + 1) * HALF].rearrange("p a c -> p (a c)")
                        V.tensor_tensor(r, r, o[:, 0:HALF], ALU.add).then_inc(S("y_T"), 1)
                        dve.wait_ge(S("y_T"), i * 4 + (2 * j + c + 1))
                        dve.nop().then_inc(bank_free[PLAN[("f2", j, c)][0]], 1)
            for t in range(TILES):
                m = cols(t)[1]
                o = full(dve, ("y", t, 1))
                if t >= 2:
                    dve.wait_ge(S(f"y_out{t % 2}"), 16 * (t // 2))
                V.tensor_copy(ytok[0:m, t % 2, 512:1024], o[0:m, :]).then_inc(S("ytok_right"), 1)
                dve.wait_ge(S("ytok_right"), t + 1)
                dve.nop().then_inc(bank_free[PLAN[("y", t, 1)][0]], 1)

        @block.gpsimd
        def _(pool):
            G = nc.gpsimd
            link = Chain(pool, "pool_step")
            pool.wait_ge(S("km"), 1)
            pool.dma_start(mk_p.rearrange("l a (t p) h d -> p (l a t) (h d)", p=P), km_p).then_inc(S("mk_out"), 16)
            pool.wait_ge(S("vm"), 2)
            pool.dma_start(mv_p.rearrange("l a (t p) h d -> p (l a t) (h d)", p=P), vm_p[:, :, :]).then_inc(S("mv_out"), 16)
            meet(pool, 1)
            G.memset(qz, 0.0).then_inc(S("pads2"), 1)
            G.memset(qi, 0.0).then_inc(S("pads2"), 1)
            pool.wait_ge(S("e_l"), 1)
            G.tensor_tensor(kl, zT[:, 2:4, :], dl, ALU.mult).then_inc(S("kl"), 1)
            pool.wait_ge(S("e_k"), 1)
            G.tensor_tensor(ek, zT[:, 2:4, :], ek, ALU.mult).then_inc(S("kd"), 1)
            pool.wait_ge(S("sig_r"), 1)
            G.tensor_tensor(rs, rs, zT[:, 4:8, :], ALU.mult).then_inc(S("rs"), 1)
            pool.wait_ge(S("gla_state"), 16)
            pool.dma_start(gla_p[0, 0].rearrange("(q h) k v -> (h k) q v", q=2), st).then_inc(S("gla_out"), 16)
            pool.wait_ge(S("gla_state_s"), 4 * NB)
            pool.dma_start(gla_s[0].rearrange("b (q h) k v -> (h k) b q v", q=2), st_s).then_inc(S("gla_out"), 16)
            pool.wait_ge(S("gla_out"), 32)
            meet(pool, 2)
            for n, v in enumerate((qf[64:P, 4, :], kv[64:P, 4, :], stat[:, 192:232], qpd, kpnT, cknT)):
                G.memset(v, 0.0).then_inc(S("pads"), 1)
                pool.wait_ge(S("pads"), n + 1)
            pool.wait_ge(S("ckv"), 1)
            link(G.memset(ckn[0:NS, KR:KR + 1], 1.0))
            link(G.tensor_copy(ckn[0:NS, 0:KR], kv[0:NS, 4, 0:KR]))
            for dst, c0, c1 in ((ckv_p, 0, KR), (kpe_p, KR, KR + ROPE)):
                pool.dma_start(dst.rearrange("l a (t p) c -> p (l a t) c", p=P), kv[:, 0:4, c0:c1]).then_inc(S("ckv_out"), 16)
            for dst, c0, c1 in ((ckv_s, 0, KR), (kpe_s, KR, KR + ROPE)):
                pool.dma_start(dst.rearrange("l b t c -> (l b t) c"), kv[0:NS, 4, c0:c1]).then_inc(S("ckv_out"), 16)
            full(pool, ("qf", 4, 1))
            G.tensor_copy(kfull.rearrange("p t (h c) -> p t h c", h=MH)[:, :, :, MV:MQ],
                          spread(kv[:, 0:4, KR:KR + ROPE], 2, MH)).then_inc(S("kfull"), 1)
            pool.wait_ge(S("ckv_out"), 64)
            meet(pool, 3)
            meet(pool, 4)
            for v in cpg:
                G.memset(v[:, :, KR:KR + 1], 1.0).then_inc(S("page_one"), 1)
            meet(pool, 5)
            meet(pool, 6)
            for t in range(TILES):
                pool.wait_ge(S("ytok_left"), t + 1)
                pool.wait_ge(S("ytok_right"), t + 1)
                m = cols(t)[1]
                dst = y_p[0, t * P:(t + 1) * P, :] if t < 4 else y_s.rearrange("b t d -> (b t) d")
                pool.dma_start(dst, ytok[0:m, t % 2, :]).then_inc(S(f"y_out{t % 2}"), 16)
            pool.wait_ge(S("y_out0"), 48)
            pool.wait_ge(S("y_out1"), 32)
            pool.wait_ge(S("mk_out"), 16)
            pool.wait_ge(S("mv_out"), 16)


def shape_constants():
    c = np.zeros((P, C_END), np.float32)
    i = np.arange(P)
    c[:, C_ID:C_ID + P] = np.eye(P)
    c[:, C_ONE:C_ONE + P] = 1.0
    c[:, C_TRI:C_TRI + P] = i[None, :] >= i[:, None]
    c[:, C_CAUS:C_CAUS + P] = np.where(i[None, :] <= i[:, None], 0.0, NEG)
    s = np.arange(NS)
    same = (s[None, :] // TS == s[:, None] // TS) & (s[None, :] >= s[:, None])
    c[:NS, C_SMASK:C_SMASK + NS] = same
    c[:NS, C_SNEG:C_SNEG + NS] = np.where(same, 0.0, NEG)
    c[:NS, C_SEQ:C_SEQ + NB] = s[:, None] // TS == np.arange(NB)[None, :]
    scan = np.ones(NT, np.float32)
    scan[0:TP:P] = 0.0
    scan[TP:NT:TS] = 0.0
    c[:, C_SCAN:C_SCAN + NT] = scan
    half = ROPE // 2
    inv = (10000.0 ** (-np.arange(half, dtype=np.float32) / half)).astype(np.float32)
    pos = np.zeros((P, TILES), np.float32)
    for t in range(4):
        pos[:, t] = t * P + i
    pos[:NS, 4] = PAST + s % TS
    ang = (pos[:, :, None] * inv[None, None, :]).astype(np.float32).astype(np.float64)
    c[:, C_ROPE:C_ROPE + 80] = np.cos(ang).reshape(P, 80)
    c[:, C_ROPE + 80:C_ROPE + 160] = np.sin(ang).reshape(P, 80)
    c[:, C_EPS] = EPS
    c[:, C_LNX] = -0.5 * np.log(XD)
    return c


def ring_layout(w_in, w_out, w_xq, w_xk, w_xv, w_xo, w_ff1, w_ff2):
    def tiles(w):
        k, n = w.shape
        return w.reshape(k // P, P, n // P, P).transpose(2, 1, 0, 3)

    out = np.zeros((W_END, P, KD, P), np.float32)
    out[W_XK:W_XK + 4] = tiles(w_xk)
    out[W_XV:W_XV + 4] = tiles(w_xv)
    out[W_QK:W_QK + 4] = tiles(w_in[:, 0:512])
    out[W_V:W_V + 4] = tiles(w_in[:, 512:1024])
    out[W_R:W_R + 4] = tiles(w_in[:, 1024:1536])
    out[W_KVA:W_KVA + 2] = tiles(w_in[:, 1936:2192])
    out[W_AKPE, :, :, 0:16] = w_in[:, 1536:1552].reshape(KD, P, 16).transpose(1, 0, 2)
    out[W_AKPE, :, :, 16:48] = w_in[:, 2192:2224].reshape(KD, P, 32).transpose(1, 0, 2)
    out[W_QA:W_QA + 3] = tiles(w_in[:, 1552:1936])
    out[W_OUT:W_OUT + KD] = tiles(w_out)
    out[W_XQ:W_XQ + 4] = tiles(w_xq)
    xo = tiles(w_xo)
    for j in range(KD):
        out[W_XO + j // 2, :, (j % 2) * 4:(j % 2) * 4 + 4, :] = xo[j]
    out[W_F1:W_F1 + KF] = tiles(w_ff1)
    f2 = tiles(w_ff2)
    for j in range(KD):
        for q in range(4):
            out[W_F2 + 4 * j + q] = f2[j][:, q * 8:q * 8 + 8, :]
    return out.reshape(W_END, P, KD * P)


_OUTS = [(1, TP, D), (NB, TS, D), (1, 1, TP, KR), (1, 1, TP, ROPE), (1, 1, NM, XH, XD), (1, 1, NM, XH, XD),
         (1, 1, GH, DK, DV), (1, NB, TS, KR), (1, NB, TS, ROPE), (1, NB, GH, DK, DV)]


def kernel(x_prompt, x_sample, mem_prompt, cache_ckv, cache_kpe, cache_mem_k, cache_mem_v,
           state_gla, page_table, g_mix, w_in, w_gla_a2, b_gla_a, g_gla_o, g_mla_qa, w_mla_qb,
           g_mla_kva, w_mla_kvb, g_q_nope, g_k_nope, g_q_rope, g_k_rope, w_out, g_x, g_mem,
           w_xq, w_xk, w_xv, g_xq, g_xk, w_xo, g_ff, w_ff1, w_ff2):
    import concourse.bacc as bacc
    from concourse.bass_utils import run_bass_kernel_spmd

    def a(v):
        return np.ascontiguousarray(v)

    def by_partition(g):
        return a(g)[0].reshape(-1, P).T

    gains = np.concatenate([by_partition(g) for g in (g_mix, g_x, g_ff, g_mem, g_mla_qa, g_gla_o, g_xq, b_gla_a)],
                           axis=1)
    rows = np.concatenate([a(g) for g in (g_mla_kva, g_q_nope, g_k_nope, g_q_rope, g_k_rope, g_xk)], axis=1)
    ring = ring_layout(*(a(w)[0] for w in (w_in, w_out, w_xq, w_xk, w_xv, w_xo, w_ff1, w_ff2)))
    ins = {
        "x": a(x_prompt), "xs": a(x_sample), "mem": a(mem_prompt), "consts": shape_constants(), "gains": a(gains),
        "rows": a(rows), "ring_w": ring, "w_kvb": a(w_mla_kvb), "w_qb": a(w_mla_qb), "w_a2": a(w_gla_a2),
        "cache_ckv": a(cache_ckv), "cache_kpe": a(cache_kpe), "cache_mk": a(cache_mem_k), "cache_mv": a(cache_mem_v),
        "state": a(state_gla), "pages": a(page_table),
    }
    nc = bacc.Bacc("TRN2", target_bir_lowering=False, num_devices=1)
    args = [nc.dram_tensor(f"in_{n}_dram", v.shape, mybir.dt.from_np(v.dtype), kind="ExternalInput").ap()
            for n, v in ins.items()]
    args += [nc.dram_tensor(f"out_{i}_dram", s, F32, kind="ExternalOutput").ap() for i, s in enumerate(_OUTS)]
    build(nc, *args)
    r = run_bass_kernel_spmd(nc, [{f"in_{n}_dram": v for n, v in ins.items()}], core_ids=[0])
    return tuple(r.results[0][f"out_{i}_dram"] for i in range(len(_OUTS)))
```

```python
from contextlib import ExitStack

import numpy as np
import concourse.bass as bass
from concourse import mybir

F32 = mybir.dt.float32
F32R = mybir.dt.float32r
I32 = mybir.dt.int32
ALU = mybir.AluOpType
ACT = mybir.ActivationFunctionType
AX = mybir.AxisListType

P = 128
D = 1024
KD = D // P
TP = 512
NB = 8
TS = 8
NS = NB * TS
NT = TP + NS
HALF = NT // 2
TILES = 5
PAST = 2048
PAGE = 128
NPG = PAST // PAGE
GH, DK, DV = 4, 64, 128
MH, MV, ROPE = 8, 64, 32
MQ = MV + ROPE
QR, KR = 384, 256
KQ, KC = QR // P, KR // P
MLA_SCALE = float(MQ) ** -0.5
XH, XD = 4, 128
NM = 256
FF = 4 * D
KF = FF // P
EPS = 1e-6
NEG = -1.0e30
CLAMP = 80.0 * 16.0
TAU = 16.0

W_XK, W_XV, W_QK, W_QA, W_AKPE, W_V, W_KVA, W_R, W_OUT, W_XQ, W_XO, W_F1, W_END = (
    0, 4, 8, 12, 15, 16, 20, 22, 26, 34, 38, 42, 106)
SLOTS = 8
SPLITS = 2
MLP_TILES = 32
MLP_FILLS = 2 * (KF // 16) + 2

C_ID, C_ONE, C_TRI, C_CAUS, C_SMASK, C_SNEG, C_SEQ, C_SCAN, C_ROPE, C_EPS, C_POW, C_EPSK, C_END = (
    0, 128, 256, 384, 512, 576, 640, 648, 1224, 1384, 1385, 1386, 1387)
G_MIX, G_X, G_FF, G_MEM, G_QA, G_GLA, G_XQ, G_BA, G_END = 0, 8, 16, 24, 32, 35, 36, 37, 39
R_KVA, R_QN, R_KN, R_QR, R_KR, R_XK, R_END = 0, 256, 320, 384, 416, 448, 576


def make_plan():
    used = [0] * 8
    fills = {}

    def fill(key, bank):
        used[bank] += 1
        fills[key] = (bank, used[bank])

    rot = [0]

    def turn(key):
        fill(key, rot[0] % 8)
        rot[0] += 1

    for j in range(4):
        turn(("memT", j))
    turn("ms_mem")
    for t in range(2):
        turn(("xk", t))
    for t in range(2):
        turn(("xv", t))
    for k in range(KD):
        turn(("xT", k))
    turn("xTs")
    for h in range(2):
        turn(("ms_mix", h))
    for n in range(2):
        turn(("kmT", n))
    for j in (0, 1, 2, 3, 11, 8):
        for h in range(2):
            turn(("z", j, h))
    for p in range(2):
        for h in range(2):
            turn(("gate", p, h))
    for j in (9, 10):
        for h in range(2):
            turn(("z", j, h))
    for t in range(TILES):
        turn(("v", t))
    for t in range(TILES):
        turn(("kva", t))
    for j in range(4, 8):
        for h in range(2):
            turn(("z", j, h))
    for p in range(2):
        turn(("klt", p))
    turn("klts")
    for t in range(4):
        turn(("att", t))
    turn("atts")
    for c in range(2):
        turn(("ms_qa", c))
    for t in range(4):
        turn(("go", t))
        turn(("st", t))
    turn("gos")
    for b in range(NB):
        turn(("sst", b))
    for h in range(GH):
        for c in range(2):
            turn(("ms_gla", h, c))
    for n in range(4):
        turn(("wkT", n))
    for t in range(TILES):
        for c in range(2):
            turn(("qf", t, c))
    for k in range(KC):
        turn(("ckT", k))
    turn("ckTs")
    for t in range(TILES):
        turn(("krp", t))
    for t in range(4):
        turn(("vp", t))
    for h in range(MH):
        turn(("qT", h))
    turn("qTs")
    for k in range(KC):
        turn(("qabs", k))
    turn("qpd")
    for h in range(MH):
        turn(("kT", h))
    for t in range(4):
        for h in range(MH):
            n = t * MH + h
            fill(("s", t, h), n % 3)
            fill(("pT", t, h), (3, 6)[n % 2])
        fill(("po", t), 4 + t % 2)
        fill(("poT", t), 7)
    base = list(used)
    for n in range(8):
        fills[("ct", n)] = (n % 2, base[n % 2] + n // 2 + 1)
    for j in range(NPG):
        fills[("kr", j)] = (2 + j % 2, base[2 + j % 2] + j // 2 + 1)
    for g in range(4):
        fills[("sc", g)] = (4 + g % 2, base[4 + g % 2] + g // 2 + 1)
    fills["scn"] = (6, base[6] + 1)
    fills["pv"] = (6, base[6] + 2)
    fills["kpt"] = (7, base[7] - 2)
    fills["kpt0"] = (7, base[7] + 1)
    fills["mt"] = (7, base[7] + 3)
    fills["mb"] = (7, base[7] + 4)
    fills["pct"] = (7, base[7] + 5)
    for name in ("mt", "mb", "pct"):
        fills[name + "_last"] = (7, fills[name][1] - 1)
    stride = [4, 4, 8, 8, 2, 2, 2, 4]
    for b in range(8):
        used[b] += NB * stride[b]
    for j in range(4):
        fill(("wo", j, 0), j)
    rot[0] = 4
    turn("oms")
    for j in range(KD):
        for c in range(2):
            if j >= 4 or c == 1:
                turn(("wo", j, c))
    for c in range(2):
        turn(("ms_x", c))
    for j in range(XH + 1):
        for c in range(2):
            if j < XH:
                turn(("xq", j, c))
        for c in range(2):
            if j:
                turn(("ms_xq", j - 1, c))
    pairs = [(t, u) for u in range(2) for t in range(4)]
    for n in range(len(pairs) + 2):
        if n < len(pairs):
            turn(("cs", *pairs[n]))
        if n >= 2:
            turn(("cp", *pairs[n - 2]))
    for h in range(XH):
        turn(("co", h))
    rot[0] = 0
    for b in range(NB):
        for n in range(2):
            fill(("ck", b, n), (b * 2 + n) % 4)
    for u in range(NB // 2):
        fill(("css", u), 4 + u)
        fill(("cpT", u), u)
    for g in range(2):
        fill(("cv", g), 4 + g)
    for g in range(2):
        fill(("cvT", g), 6 + g)
    for j in range(KD):
        for c in range(2):
            turn(("xo", j, c))
    for c in range(2):
        turn(("ms_ff", c))
    base = list(used)
    for j in range(8):
        for c in range(2):
            n = 2 * j + c
            fills[("f1", j, c)] = (n % 8, base[n % 8] + n // 8 + 1)
    for j in range(4):
        for c in range(2):
            fills[("f2", j, c)] = (2 * j + c, base[2 * j + c] + 2 * (KF // 16) + 1)
    for b in range(8):
        used[b] += 2 * MLP_FILLS
    fills["end"] = (0, used[0])
    return fills, stride


PLAN, SEQ_STRIDE = make_plan()


def build(nc, x, xs, mem, consts, gains, rows, ring_w, w_kvb_d, w_qb_d, w_a2_d, cache_ckv, cache_kpe,
          cache_mk, cache_mv, state, pages, y_p, y_s, ckv_p, kpe_p, mk_p, mv_p, gla_p, ckv_s, kpe_s,
          gla_s):
    with ExitStack() as ctx:
        def sb(name, shape, dt=F32, extent=ctx):
            return extent.enter_context(nc.sbuf_tensor(name, shape, dt))

        sems = {}

        def S(name):
            if name not in sems:
                sems[name] = ctx.enter_context(nc.semaphore(name))
            return sems[name]

        cst = sb("cst", [P, C_END])
        gn = sb("gn", [P, G_END])
        row = sb("row", [P, R_END])
        xT = sb("xT", [P, KD, NT])
        with ExitStack() as whole:
            hT = sb("hT", [P, KD * NT], extent=whole)
        with ExitStack() as parts:
            sb("hT_begin", [P, 2560], extent=parts)
            c_parts = sb("c_parts", [P, 2, 2, 2, KC, P], F32R, extent=parts)
        sb("hT_extent", [P, KD * NT])
        ring = sb("ring", [P, SLOTS, KD, P])
        rstd = sb("rstd", [P, NT])
        ARENA = 23440
        with ExitStack() as before_mlp:
            w_kvb = sb("w_kvb", [P, KC, 2 * MH * MV], extent=before_mlp)
            w_a2 = sb("w_a2", [16, GH * DK], extent=before_mlp)
            vm_p = sb("vm_p", [P, 2, XH * XD], extent=before_mlp)
            kmT = sb("kmT", [P, 2, XH, P], extent=before_mlp)
            stat = sb("stat", [P, 640], extent=before_mlp)
            page_sb = sb("page_sb", [1, NB * NPG], I32, extent=before_mlp)
            mixT = sb("mixT", [P, KD, NT], extent=before_mlp)
            with ExitStack() as whole:
                arena = sb("arena", [P, ARENA], extent=whole)
            sb("arena_begin", [P, 9360], extent=before_mlp)
            wk_high = sb("wk_high", [P, KC, MH * MV], F32R, extent=before_mlp)
            sb("arena_middle", [P, 13984 - 9360 - KC * MH * MV], extent=before_mlp)
            wk_low = sb("wk_low", [P, KC, MH * MV], F32R, extent=before_mlp)
        hr = sb("hr", [P, 2, KD, NT], F32R)
        ur = sb("ur", [P, 2, KF // 2, NT], F32R)
        wr = sb("wr", [P, SPLITS, 2, KD * P], F32R)
        bank = [ctx.enter_context(nc.psum_tensor(f"bank{b}", [P, 512], F32)) for b in range(8)]

        def view(base, at, *shape):
            n = int(np.prod(shape))
            assert at + n <= base.shape[1], (at, shape)
            v = base[:, at:at + n]
            if len(shape) > 1:
                names = "abcd"[:len(shape)]
                v = v.rearrange(f"p ({' '.join(names)}) -> p {' '.join(names)}", **dict(zip(names, shape)))
            return v

        def spread(ap, axis, n):
            v = ap.unsqueeze(axis)
            return v.broadcast_to([*v.shape[:axis], n, *v.shape[axis + 1:]])

        ident = cst[:, C_ID:C_ID + P]
        ones = cst[:, C_ONE:C_ONE + P]
        tri = cst[:, C_TRI:C_TRI + P]
        causal = cst[:, C_CAUS:C_CAUS + P]
        smask = cst[0:NS, C_SMASK:C_SMASK + NS]
        sneg = cst[0:NS, C_SNEG:C_SNEG + NS]
        seqm = cst[0:NS, C_SEQ:C_SEQ + NB]
        scanm = cst[:, C_SCAN:C_SCAN + NT]
        cosn = view(cst, C_ROPE, TILES, ROPE // 2)
        sinn = view(cst, C_ROPE + 80, TILES, ROPE // 2)
        epsc = cst[:, C_EPS:C_EPS + 1]
        epsk = cst[:, C_EPSK:C_EPSK + 1]
        power = cst[:, C_POW:C_POW + 1]
        gxq = stat[:, 600:601]
        hTk = view(hT, 0, KD, NT)
        mix_flat = mixT[:, :, :].rearrange("p a b -> p (a b)")

        zT = view(arena, 0, 12, NT)
        vtok = view(arena, 6912, TILES, GH * DV)
        kv = view(arena, 9472, TILES, KR + ROPE)
        sq1 = view(arena, 10912, KD, NT)
        memx = view(arena, 15520, 2, D)
        memT = view(arena, 17568, KD, NM)
        hmT = view(arena, 19616, KD, NM)
        xin_s = view(arena, 21664, D)
        xin = mix_flat[:, 0:4 * D].rearrange("p (t d) -> p t d", t=4)
        km_p = view(hT, 0, 2, XH * XD)
        gb = view(arena, 10912, 2, NT)
        eb = view(arena, 12064, 2, NT)
        ek = view(arena, 13216, 2, NT)
        qz = view(arena, 14368, 2, 2, NT)
        qi = view(arena, 16672, 2, 2, NT)
        klt = view(arena, 18976, TILES, 2, P)
        st = view(arena, 20256, 2, DV)
        st_s = view(arena, 20512, NB, 2, DV)
        att = view(hT, 0, 4, GH, P)
        atts = view(hT, 2048, GH, NS)
        klm = view(hT, 2304, 2, 2, P)
        kl, eq = mixT[:, 2:4, :], mixT[:, 0:2, :]
        dq, dl = mixT[:, 0:2, :], mixT[:, 2:4, :]
        sqg = view(arena, 14368, GH, NT)
        rs = view(arena, 16672, GH, NT)
        qf = view(arena, 0, TILES, MH * MQ)
        qT = view(arena, 4608, MH, TP)
        qTs = view(arena, 8704, MH, NS)
        qabs = view(arena, 10912, KC, NB, MH * TS)
        qpd = view(arena, 11936, NB, 4, MH * TS)
        ckT = view(arena, 13984, KC, NT)
        cknT = view(arena, 22500, KC, P)
        kpnT = view(arena, 22760, P)
        ckn = view(arena, 15136, KR + 1)
        sqf = view(arena, 15396, TILES, MH * MQ)
        sqkv = view(arena, 18976, TILES, KR + ROPE)
        w_qb = view(mix_flat, 4 * NT, KQ, MH * MQ)
        sqa = view(hT, 2880, KQ, NT)
        qp4 = view(hT, 0, MH, P)
        w_kT = view(hT, 1728, MH, KR)
        sqk = view(hT, 3776, 512)
        kfull = view(arena, 19236, 4, MH * MQ)
        kT = view(arena, 0, MH, TP)
        vp = view(arena, 15396, 4, MH * MV)
        gq2 = view(arena, 22900, MV)
        gqr = view(arena, 22964, ROPE)
        pr = view(hT, 0, 3, 512)
        prT = view(hT, 1536, 2, 512)
        ot = view(hT, 2560, 2, 512)
        cpg = [view(arena, 17444, NPG, KR + 1), view(arena, 0, NPG, KR + 1)]
        kpg = [view(arena, 21556, NPG * ROPE), view(arena, 4112, NPG * ROPE)]
        sc = [view(arena, 4624, NPG + 1, MH * TS), view(arena, 8272, NPG + 1, MH * TS)]
        pb = view(arena, 5712, NPG + 1, MH * TS)
        pcs = view(arena, 6800, KR)
        pcT = view(arena, 7056, KC, MH, NS)
        mx = view(arena, 8080, P)
        dg = view(arena, 8208, 64)
        cT = view(hT, 0, 2, 2, KC, P)
        sqs = view(hT, 1024, 2, 512)
        kpT = view(hT, 2048, 4, P)
        vmc = view(arena, 0, NB, 2, XH * XD)
        kmc = view(arena, 8192, 2, 2, XH * XD)
        kmcT = view(arena, 10240, 2, 2, XH, P)
        xqT = view(arena, 12288, XH, NT)
        xoT = view(arena, 14592, XH, NT)
        pcx = view(arena, 16896, 2, 2, NM)
        pcxT = view(arena, 17920, XH, 2, TP)
        psx = view(arena, 17920, NB, NM)
        scs = view(arena, 22016, 2, NB * XH * TS)
        cv = view(arena, 16896, 2, XH * XD)
        relu = view(hT, 0, NT)
        usq = view(hT, NT, 2, NT)
        ytok = view(hT, 0, 4, D)

        bank_full = [S(f"bank_full{b}") for b in range(8)]
        bank_free = [S(f"bank_free{b}") for b in range(8)]

        def at(key, turn=0, stride=0):
            b, n = PLAN[key]
            return b, (n if isinstance(turn, int) and turn == 0 else turn * stride + n)

        def full(eng, key, turn=0, stride=0):
            b, n = at(key, turn, stride)
            eng.wait_ge(bank_full[b], n)
            return bank[b]

        def freed(ins, key):
            return ins.then_inc(bank_free[PLAN[key][0]], 1)

        def reopen(pe, key, turn=0, stride=0):
            b, n = at(key, turn, stride)
            if not (isinstance(n, int) and n == 1):
                pe.wait_ge(bank_free[b], n - 1)
            return bank[b]

        def filled(ins, key):
            return ins.then_inc(bank_full[PLAN[key][0]], 1)

        MET = (0, 3, 7, 11, 15)

        def meet(eng, n):
            eng.drain().then_inc(S("phase_end"), 1)
            eng.wait_ge(S("phase_end"), MET[n])

        def cols(t):
            return (t * P, P) if t < 4 else (TP, NS)

        def w_k(k):
            return w_kvb[:, k, :].rearrange("p (h c) -> p h c", h=MH)[:, :, 0:MV]

        def w_v(k):
            return w_kvb[:, k, :].rearrange("p (h c) -> p h c", h=MH)[:, :, MV:2 * MV]

        class Chain:

            def __init__(self, eng, name):
                self.eng, self.sem, self.n = eng, S(name), 0

            def __call__(self, ins):
                self.n += 1
                ins.then_inc(self.sem, 1)
                self.eng.wait_ge(self.sem, self.n)

        def wait_prT_free(eng, n, steps):
            if n >= 2:
                t, h = steps[n - 2]
                if h < MH - 1:
                    eng.wait_ge(S("prT_used"), (n - 2) - t)
                else:
                    full(eng, ("po", t))

        last_read = {}
        for j in range(4):
            last_read[W_XK + j], last_read[W_XV + j] = ("xk", 1), ("xv", 1)
            last_read[W_QK + j], last_read[W_R + j] = ("z", j, 1), ("z", 4 + j, 1)
            last_read[W_V + j], last_read[W_XQ + j] = ("v", 4), ("xq", j, 1)
            last_read[W_XO + j] = ("xo", 2 * j + 1, 1)
        for j in range(2):
            last_read[W_KVA + j] = ("kva", 4)
        last_read[W_AKPE] = ("kva", 4)
        for j in range(3):
            last_read[W_QA + j] = ("z", 8 + j, 1)
        for j in range(KD):
            last_read[W_OUT + j] = ("wo", j, 1)

        slot_in = [S(f"slot_in{s}") for s in range(SLOTS)]

        def slot(pe, tile):
            pe.wait_ge(slot_in[tile % SLOTS], 16 * (tile // SLOTS + 1))
            return tile % SLOTS

        squares = {"mem": 0, "mix": KD, "x": 2 * KD, "ff": 3 * KD}
        roots = {"mem": 0, "mix": 1, "qa": 3, "gla": 5, "x": 13, "xq": 15, "ff": 23}
        normed = {"mem": 0, "mix": KD, "qa": 2 * KD, "x": 2 * KD + KQ, "ff": 3 * KD + KQ}

        def rotated(E, link, v, c, s, tmp):
            a, b = v[..., 0:16], v[..., 16:32]
            link(E.tensor_tensor(tmp[0], a, c, ALU.mult))
            link(E.tensor_tensor(tmp[1], b, s, ALU.mult))
            link(E.tensor_tensor(tmp[2], b, c, ALU.mult))
            link(E.tensor_tensor(tmp[3], a, s, ALU.mult))
            link(E.tensor_tensor(a, tmp[0], tmp[1], ALU.subtract))
            return E.tensor_tensor(b, tmp[2], tmp[3], ALU.add)

        mlp_free = [PLAN[("f1", b // 2, b % 2)][1] - 1 + 2 * MLP_FILLS for b in range(8)]

        block = ctx.enter_context(nc.Block())

        @block.sync
        def _(sp):
            def load_tile(n):
                if n >= SLOTS:
                    b, c = PLAN[last_read[n - SLOTS]]
                    sp.wait_ge(bank_full[b], c)
                sp.dma_start(ring[:, n % SLOTS, :, :].rearrange("p a b -> p (a b)"), ring_w[n]).then_inc(
                    slot_in[n % SLOTS], 16)

            sp.dma_start(cst[:, :], consts).then_inc(S("const_in"), 16)
            sp.dma_start(memx, mem.rearrange("a (t p) d -> p (a t) d", p=P)).then_inc(S("mem_in"), 16)
            sp.dma_start(gn[:, :], gains).then_inc(S("const_in"), 16)
            sp.dma_start(row[:, :], rows.broadcast_to([P, R_END])).then_inc(S("const_in"), 16)
            for n in range(W_XK, W_XV):
                load_tile(n)
            sp.dma_start(xin, x.rearrange("a (t p) d -> p (a t) d", p=P)).then_inc(S("x_in"), 16)
            sp.dma_start(xin_s[0:NS, :], xs.rearrange("b t d -> (b t) d")).then_inc(S("x_in"), 16)
            for n in range(W_XV, W_QK):
                load_tile(n)
            sp.dma_start(page_sb[:, :], pages.rearrange("(o b) n -> o (b n)", o=1)).then_inc(S("page_in"), 16)
            sp.dma_start(w_a2[:, :], w_a2_d[0]).then_inc(S("wa2_in"), 16)
            sp.dma_start(w_kvb[:, :, :], w_kvb_d[0].rearrange("(k p) n -> p k n", p=P)).then_inc(S("wkvb_in"), 16)
            for n in range(W_QK, W_V):
                load_tile(n)
            sp.wait_ge(S("normed"), normed["mix"] + KD)
            sp.dma_start(st_s, state[0].rearrange("b (q h) k v -> (h k) b q v", q=2)).then_inc(S("state_in"), 16)
            sp.dma_start(w_qb, w_qb_d[0].rearrange("(k p) n -> p k n", p=P)).then_inc(S("wqb_in"), 16)
            for n in range(W_V, W_OUT):
                load_tile(n)
            for n in range(W_OUT, W_XQ):
                if last_read[n - SLOTS][0] in ("z", "kva", "v"):
                    load_tile(n)
            sp.wait_ge(S("page_in"), 16)

            def page_number(b, j):
                where = page_sb[0:1, bass.ds(b * NPG + j, 1)]
                return sp.value_load(where, min_val=0, max_val=cache_ckv.shape[1] - 1)

            def load_keys(b, par, anew=False):
                for j in range(NPG):
                    page = page_number(b, j)
                    if anew and j == 0:
                        sp.wait_ge(S("kpT"), b - 1)
                    sp.dma_start(kpg[par][:, j * ROPE:(j + 1) * ROPE], cache_kpe[0, bass.ds(page, 1), :, :].rearrange(
                        "a p c -> p (a c)")).then_inc(S(f"page_k{par}"), 16)

            def load_latents(b, par, anew=False):
                for j in range(NPG):
                    page = page_number(b, j)
                    if anew and j == 0:
                        sp.wait_ge(S("pv_out"), b - 1)
                    sp.dma_start(cpg[par][:, j, 0:KR], cache_ckv[0, bass.ds(page, 1), :, :].rearrange(
                        "a p c -> p (a c)")).then_inc(S(f"page_c{par}_{j // 4}"), 16)

            sp.wait_ge(S("phase_end"), MET[2])
            load_latents(0, 0)
            load_keys(0, 0)
            sp.wait_ge(S("phase_end"), MET[3])
            load_keys(1, 1)
            load_latents(1, 1)
            with sp.Fori(0, (NB - 2) // 2) as i:
                for par in range(2):
                    b = i * 2 + (2 + par)
                    load_keys(b, par, anew=True)
                    load_latents(b, par, anew=True)
            sp.wait_ge(S("phase_end"), MET[4])
            mk = cache_mk[0].rearrange("b (n p) h d -> b p n (h d)", p=P)
            mv = cache_mv[0].rearrange("b (n p) h d -> b p n (h d)", p=P)
            for b in range(2):
                sp.dma_start(kmc[:, b, :, :], mk[b]).then_inc(S(f"kmc_in{b}"), 16)
            for b in range(NB):
                sp.dma_start(vmc[:, b, :, :], mv[b]).then_inc(S("vmc_in"), 16)
            for n in range(W_XQ, W_F1):
                load_tile(n)
            for n in range(W_F1, W_F1 + SLOTS - 4):
                load_tile(n)
            for b in range(2, NB):
                bk, c = PLAN[("ck", b - 2, 1)]
                sp.wait_ge(bank_full[bk], c)
                sp.dma_start(kmc[:, b % 2, :, :], mk[b]).then_inc(S(f"kmc_in{b % 2}"), 16)
            for n in range(W_F1 + SLOTS - 4, W_F1 + SLOTS):
                load_tile(n)
            with sp.Fori(0, 2 * MLP_TILES // SLOTS - 1) as i:
                for j in range(SLOTS):
                    sp.wait_ge(S("w_split"), i * SLOTS + (j + 1))
                    sp.dma_start(ring[:, (W_F1 + j) % SLOTS, :, :].rearrange("p a b -> p (a b)"),
                                 ring_w[bass.ds(i * SLOTS + (W_F1 + SLOTS + j), 1)].rearrange("a p c -> p (a c)")
                                 ).then_inc(slot_in[(W_F1 + j) % SLOTS], 16)
            for t in range(TILES):
                sp.wait_ge(S("ytok_left"), t + 1)
                sp.wait_ge(S("ytok_right"), t + 1)
                m = cols(t)[1]
                dst = y_p[0, t * P:(t + 1) * P, :] if t < 4 else y_s.rearrange("b t d -> (b t) d")
                sp.dma_start(dst, ytok[0:m, t % 4, :]).then_inc(S(f"y_out{t % 2}"), 16)

        @block.tensor
        def _(pe):
            mm, tr = nc.tensor.matmul, nc.tensor.transpose

            def sums(name, keys, sq, n_k, width=HALF):
                outs = [reopen(pe, key) for key in keys]
                for k in range(n_k):
                    if name in squares:
                        pe.wait_ge(S("squares"), squares[name] + k + 1)
                    for c, key in enumerate(keys):
                        ins = mm(outs[c][:, 0:width], ones, sq[:, k, c * width:(c + 1) * width],
                                 start=(k == 0), stop=(k == n_k - 1))
                        if k == n_k - 1:
                            filled(ins, key)

            def project(key, lhsT, src, n_k, m=P, name=None):
                outs = [reopen(pe, (*key, c)) for c in range(2)]
                for k in range(n_k):
                    if name:
                        pe.wait_ge(S("normed"), normed[name] + k + 1)
                    for c in range(2):
                        ins = mm(outs[c][0:m, 0:HALF], lhsT(k), src[:, k, c * HALF:(c + 1) * HALF],
                                 start=(k == 0), stop=(k == n_k - 1))
                        if k == n_k - 1:
                            filled(ins, (*key, c))

            pe.wait_ge(S("const_in"), 48)
            pe.wait_ge(S("mem_in"), 16)
            for j in range(4):
                o = reopen(pe, ("memT", j))
                for kk in range(2):
                    for t in range(2):
                        ins = tr(o[:, (kk * 2 + t) * P:(kk * 2 + t + 1) * P],
                                 memx[:, t, (2 * j + kk) * P:(2 * j + kk + 1) * P], ident)
                filled(ins, ("memT", j))
            sums("mem", ["ms_mem"], sq1, KD, width=NM)
            for name, w0 in (("xk", W_XK), ("xv", W_XV)):
                for j in range(4):
                    slot(pe, w0 + j)
                for t in range(2):
                    o = reopen(pe, (name, t))
                    for k in range(KD):
                        pe.wait_ge(S("normed"), normed["mem"] + k + 1)
                        ins = mm(o[:, :], hmT[:, k, t * P:(t + 1) * P], ring[:, w0 % SLOTS:w0 % SLOTS + 4, k, :],
                                 start=(k == 0), stop=(k == KD - 1))
                    filled(ins, (name, t))
            pe.wait_ge(S("x_in"), 32)
            for k in range(KD):
                o = reopen(pe, ("xT", k))
                for t in range(4):
                    ins = tr(o[:, t * P:(t + 1) * P], xin[:, t, k * P:(k + 1) * P], ident)
                filled(ins, ("xT", k))
            o = reopen(pe, "xTs")
            for k in range(KD):
                ins = tr(o[:, k * NS:(k + 1) * NS], xin_s[0:NS, k * P:(k + 1) * P], ident[0:NS, 0:NS])
            filled(ins, "xTs")
            sums("mix", [("ms_mix", 0), ("ms_mix", 1)], sq1, KD)
            pe.wait_ge(S("km"), 1)
            for n in range(2):
                o = reopen(pe, ("kmT", n))
                for h in range(XH):
                    ins = tr(o[:, h * P:(h + 1) * P], km_p[:, n, h * XD:(h + 1) * XD], ident)
                filled(ins, ("kmT", n))
            def tile_z(j):
                if j == 11:
                    s = slot(pe, W_AKPE)
                    project(("z", j), lambda k: ring[:, s, k, 0:16], hTk, KD, m=16)
                else:
                    s = slot(pe, W_QK + j if j < 4 else W_R + j - 4 if j < 8 else W_QA + j - 8)
                    project(("z", j), lambda k: ring[:, s, k, :], hTk, KD, name=None if j else "mix")

            for j in (0, 1, 2, 3, 11, 8):
                tile_z(j)
            pe.wait_ge(S("wa2_in"), 16)
            for c in range(2):
                b, n = PLAN[("z", 11, c)]
                pe.wait_ge(bank_free[b], n)
            for p in range(2):
                for c in range(2):
                    o = reopen(pe, ("gate", p, c))
                    filled(mm(o[:, 0:HALF], w_a2[:, p * P:(p + 1) * P], zT[0:16, 11, c * HALF:(c + 1) * HALF],
                              start=True, stop=True), ("gate", p, c))
            tile_z(9)
            tile_z(10)
            for name, w0, n_w in (("v", W_V, 4), ("kva", W_KVA, 2)):
                for j in range(n_w):
                    slot(pe, w0 + j)
                for t in range(TILES):
                    c0, m = cols(t)
                    o = reopen(pe, (name, t))
                    s0 = w0 % SLOTS
                    n_out = GH * DV if name == "v" else KR
                    for k in range(KD):
                        ins = mm(o[0:m, 0:n_out], hTk[:, k, c0:c0 + m], ring[:, s0:s0 + n_out // P, k, :],
                                 start=(k == 0), stop=(k == KD - 1))
                    if name == "kva":
                        for k in range(KD):
                            ins = mm(o[0:m, KR:KR + ROPE], hTk[:, k, c0:c0 + m],
                                     ring[:, W_AKPE % SLOTS, k, 16:16 + ROPE], start=(k == 0), stop=(k == KD - 1))
                    filled(ins, (name, t))
            for j in range(4, 8):
                tile_z(j)

            pe.wait_ge(S("kl"), 1)
            for p in range(2):
                o = reopen(pe, ("klt", p))
                for t in range(4):
                    ins = tr(o[:, t * P:(t + 1) * P], kl[:, p, t * P:(t + 1) * P], ident)
                filled(ins, ("klt", p))
            o = reopen(pe, "klts")
            for p in range(2):
                ins = tr(o[0:NS, p * P:(p + 1) * P], kl[:, p, TP:NT], ident)
            filled(ins, "klts")
            pe.wait_ge(S("kd"), 1)
            pe.wait_ge(S("qz"), 8)
            for t in range(4):
                o = reopen(pe, ("att", t))
                for h in range(GH):
                    ins = mm(o[:, h * P:(h + 1) * P], ek[:, h // 2, t * P:(t + 1) * P],
                             qz[:, h // 2, h % 2, t * P:(t + 1) * P], start=True, stop=True)
                filled(ins, ("att", t))
            o = reopen(pe, "atts")
            for h in range(GH):
                ins = mm(o[0:NS, h * NS:(h + 1) * NS], ek[:, h // 2, TP:NT], qz[:, h // 2, h % 2, TP:NT],
                         start=True, stop=True)
            filled(ins, "atts")
            pe.wait_ge(S("sq_qa"), 1)
            sums("qa", [("ms_qa", 0), ("ms_qa", 1)], sqa, KQ)
            pe.wait_ge(S("klt"), 3)
            for t in range(4):
                o = reopen(pe, ("go", t))
                pe.wait_ge(S("att"), t + 1)
                if t:
                    pe.wait_ge(S("gla_state"), 4 * t)
                for h in range(GH):
                    ins = mm(o[:, h * P:(h + 1) * P], vtok[:, t, h * DV:(h + 1) * DV], att[:, t, h, :],
                             start=True, stop=(t == 0))
                    if t:
                        ins = mm(o[:, h * P:(h + 1) * P], st[:, h // 2, :], qi[:, h // 2, h % 2, t * P:(t + 1) * P],
                                 start=False, stop=True)
                filled(ins, ("go", t))
                o = reopen(pe, ("st", t))
                for p in range(2):
                    ins = mm(o[:, p * 256:(p + 1) * 256], klt[:, t, p, :], vtok[:, t, p * 256:(p + 1) * 256],
                             start=True, stop=True)
                filled(ins, ("st", t))
            pe.wait_ge(S("att"), 5)
            pe.wait_ge(S("state_in"), 16)
            o = reopen(pe, "gos")
            for h in range(GH):
                mm(o[:, h * NS:(h + 1) * NS], vtok[0:NS, 4, h * DV:(h + 1) * DV], atts[0:NS, h, :],
                   start=True, stop=False, skip_group_check=True)
                for b in range(NB):
                    ins = mm(o[:, h * NS + b * TS:h * NS + (b + 1) * TS], st_s[:, b, h // 2, :],
                             qi[:, h // 2, h % 2, TP + b * TS:TP + (b + 1) * TS], start=False, stop=True,
                             skip_group_check=True)
            filled(ins, "gos")
            for b in range(NB):
                o = reopen(pe, ("sst", b))
                pe.wait_ge(S("klm"), b + 1)
                for p in range(2):
                    ins = mm(o[:, p * 256:(p + 1) * 256], klm[0:NS, b % 2, p, :],
                             vtok[0:NS, 4, p * 256:(p + 1) * 256], start=True, stop=True)
                filled(ins, ("sst", b))
            pe.wait_ge(S("sq_gla"), 1)
            for h in range(GH):
                for c in range(2):
                    o = reopen(pe, ("ms_gla", h, c))
                    filled(mm(o[:, 0:HALF], ones, sqg[:, h, c * HALF:(c + 1) * HALF], start=True, stop=True),
                           ("ms_gla", h, c))

            pe.wait_ge(S("wkvb_in"), 16)
            for n in range(4):
                o = reopen(pe, ("wkT", n))
                for e in range(2):
                    for k in range(KC):
                        h = 2 * n + e
                        ins = tr(o[0:MV, (e * 2 + k) * P:(e * 2 + k + 1) * P],
                                 w_kvb[:, k, h * P:h * P + MV], ident)
                filled(ins, ("wkT", n))
            pe.wait_ge(S("wqb_in"), 16)
            pe.wait_ge(S("normed"), normed["qa"] + KQ)
            for t in range(TILES):
                c0, m = cols(t)
                for c in range(2):
                    o = reopen(pe, ("qf", t, c))
                    for k in range(KQ):
                        ins = mm(o[0:m, 0:384], zT[:, 8 + k, c0:c0 + m], w_qb[:, k, c * 384:(c + 1) * 384],
                                 start=(k == 0), stop=(k == KQ - 1))
                    filled(ins, ("qf", t, c))
            pe.wait_ge(S("ckv"), 1)
            for k in range(KC):
                o = reopen(pe, ("ckT", k))
                for t in range(4):
                    ins = tr(o[:, t * P:(t + 1) * P], kv[:, t, k * P:(k + 1) * P], ident)
                filled(ins, ("ckT", k))
            o = reopen(pe, "ckTs")
            for k in range(KC):
                tr(o[:, k * NS:(k + 1) * NS], kv[0:NS, 4, k * P:(k + 1) * P], ident[0:NS, 0:NS])
            filled(tr(o[0:ROPE, P:P + NS], kv[0:NS, 4, KR:KR + ROPE], ident[0:NS, 0:NS]), "ckTs")
            pe.wait_ge(S("ckT"), 3)
            for t in range(TILES):
                c0, m = cols(t)
                o = reopen(pe, ("krp", t))
                for k in range(KC):
                    ins = mm(o[0:m, :], ckT[:, k, c0:c0 + m], w_k(k), start=(k == 0), stop=(k == KC - 1))
                filled(ins, ("krp", t))
            for t in range(4):
                o = reopen(pe, ("vp", t))
                for k in range(KC):
                    ins = mm(o[:, :], ckT[:, k, t * P:(t + 1) * P], w_v(k), start=(k == 0), stop=(k == KC - 1))
                filled(ins, ("vp", t))
            pe.wait_ge(S("q_ready"), 1)
            for h in range(MH):
                o = reopen(pe, ("qT", h))
                for t in range(4):
                    ins = tr(o[0:MQ, t * P:(t + 1) * P], qf[:, t, h * MQ:(h + 1) * MQ], ident)
                filled(ins, ("qT", h))
            o = reopen(pe, "qTs")
            for h in range(MH):
                ins = tr(o[0:MQ, h * NS:(h + 1) * NS], qf[0:NS, 4, h * MQ:(h + 1) * MQ], ident[0:NS, 0:NS])
            filled(ins, "qTs")
            pe.wait_ge(S("qTs"), 1)
            pe.wait_ge(S("w_kT"), 4)
            for k in range(KC):
                o = reopen(pe, ("qabs", k))
                for h in range(MH):
                    ins = mm(o[:, h * NS:(h + 1) * NS], w_kT[0:MV, h, k * P:(k + 1) * P], qTs[0:MV, h, :],
                             start=True, stop=True)
                filled(ins, ("qabs", k))
            pe.wait_ge(S("qp4"), 1)
            o = reopen(pe, "qpd")
            for h in range(MH):
                ins = tr(o[:, h * NS:(h + 1) * NS], qp4[0:NS, h, :], ident[0:NS, 0:NS])
            filled(ins, "qpd")
            pe.wait_ge(S("kfull"), 2)
            for h in range(MH):
                o = reopen(pe, ("kT", h))
                for t in range(4):
                    ins = tr(o[0:MQ, t * P:(t + 1) * P], kfull[:, t, h * MQ:(h + 1) * MQ], ident)
                filled(ins, ("kT", h))
            meet(pe, 2)

            steps = [(t, h) for t in range(4) for h in range(MH)]

            def out_rows(t):
                pe.wait_ge(S("ot"), t + 1)
                o = reopen(pe, ("poT", t))
                for j in range(4):
                    ins = tr(o[:, j * P:(j + 1) * P], ot[:, t % 2, j * P:(j + 1) * P], ident)
                filled(ins, ("poT", t))

            for n in range(len(steps) + 5):
                if n < len(steps):
                    t, h = steps[n]
                    o = reopen(pe, ("s", t, h))
                    filled(mm(o[:, 0:(t + 1) * P], qT[0:MQ, h, t * P:(t + 1) * P], kT[0:MQ, h, 0:(t + 1) * P],
                              start=True, stop=True), ("s", t, h))
                if 2 <= n < len(steps) + 2:
                    t, h = steps[n - 2]
                    pe.wait_ge(S("pr"), n - 1)
                    o = reopen(pe, ("pT", t, h))
                    for s in range(t + 1):
                        ins = tr(o[:, s * P:(s + 1) * P], pr[:, (n - 2) % 3, s * P:(s + 1) * P], ident)
                    filled(ins, ("pT", t, h))
                if 3 <= n < len(steps) + 3:
                    t, h = steps[n - 3]
                    pe.wait_ge(S(f"prT{(n - 3) % 2}"), (n - 3) // 2 + 1)
                    if h == 0:
                        reopen(pe, ("po", t))
                    o = bank[PLAN[("po", t)][0]]
                    for s in range(t + 1):
                        ins = mm(o[:, h * MV:(h + 1) * MV], prT[:, (n - 3) % 2, s * P:(s + 1) * P],
                                 vp[:, s, h * MV:(h + 1) * MV], start=(s == 0), stop=(s == t))
                    if h < MH - 1:
                        ins.then_inc(S("prT_used"), 1)
                    else:
                        filled(ins, ("po", t))
                if n >= 5 and steps[n - 5][1] == MH - 1:
                    out_rows(steps[n - 5][0])
            meet(pe, 3)

            def uses(b):
                return b // 2 + 1 if isinstance(b, int) else b[0] + (b[1] + 1)

            def transposed_pages(par, n, b):
                if n % 2 == 0:
                    pe.wait_ge(S(f"page_c{par}_{n // 2}"), (uses(b)) * 64)
                bb = b if isinstance(b, int) else b[2]
                o = reopen(pe, ("ct", n), bb, 4)
                for e in range(2):
                    for k in range(KC):
                        ins = tr(o[:, (e * KC + k) * P:(e * KC + k + 1) * P],
                                 cpg[par][:, 2 * n + e, k * P:(k + 1) * P], ident)
                filled(ins, ("ct", n))

            def softmax_max(b, last=""):
                pe.wait_ge(S("mx"), b + 1)
                o = reopen(pe, "mt" + last, b, 4)
                filled(tr(o[:, 0:P], mx, ident), "mt")

            def softmax_spread(b, last=""):
                pe.wait_ge(S("dg"), b + 1)
                o = reopen(pe, "mb" + last, b, 4)
                filled(mm(o[:, 0:64], ones[0:64, :], dg[0:64, :], start=True, stop=True), "mb")

            def weighted(b, par):
                pe.wait_ge(S("pb"), b + 1)
                o = reopen(pe, "pv", b, 2)
                for j in range(NPG):
                    mm(o[0:64, 0:KR + 1], pb[:, j, :], cpg[par][:, j, :], start=(j == 0), stop=False)
                filled(mm(o[0:64, 0:KR + 1], pb[0:NS, NPG, :], ckn[0:NS, :], start=False, stop=True), "pv")

            def weighted_T(b, last=""):
                pe.wait_ge(S("pcs"), b + 1)
                o = reopen(pe, "pct" + last, b, 4)
                for k in range(KC):
                    ins = tr(o[:, k * P:(k + 1) * P], pcs[:, k * P:(k + 1) * P], ident)
                filled(ins, "pct")

            def new_tokens(b):
                o = reopen(pe, "scn", b, 2)
                for k in range(KC):
                    mm(o[:, 0:64], cknT[:, k, :], qabs[:, k, bass.ds(b, 1), :].rearrange("p a c -> p (a c)"),
                       start=(k == 0), stop=(k == KC - 1))
                filled(mm(o[:, 64:128], kpnT,
                          qpd[:, bass.ds(b, 1), 0, :].rearrange("p a c -> p (a c)"),
                          start=True, stop=True), "scn")

            def sequence(b, par, half, following, first=False):
                tb = b if isinstance(b, int) else (half[0], half[1], b)
                prev = None if first else b - 1
                if first:
                    transposed_pages(par, 0, tb)
                if prev is not None:
                    new_tokens(prev)
                pe.wait_ge(S(f"page_k{par}"), uses(tb) * (16 * NPG))
                o = reopen(pe, "kpt0") if first else reopen(pe, "kpt", b, 4)
                for g in range(4):
                    ins = tr(o[:, g * P:(g + 1) * P], kpg[par][:, g * P:(g + 1) * P], ident)
                filled(ins, "kpt")
                for n in range(8):
                    if n < 7:
                        transposed_pages(par, n + 1, tb)
                    pe.wait_ge(S("c_low"), b * 8 + (n + 1))
                    for e in range(2):
                        j = 2 * n + e
                        o = reopen(pe, ("kr", j), b, 8)
                        for k in range(KC):
                            mm(o[:, :], c_parts[:, n % 2, 0, e, k, :], wk_high[:, k, :], start=(k == 0), stop=False)
                            mm(o[:, :], c_parts[:, n % 2, 1, e, k, :], wk_high[:, k, :], start=False, stop=False)
                            ins = mm(o[:, :], c_parts[:, n % 2, 0, e, k, :], wk_low[:, k, :],
                                     start=False, stop=(k == KC - 1))
                        filled(ins, ("kr", j))
                        g, i = j // 4, j % 4
                        if i == 0:
                            reopen(pe, ("sc", g), b, 2)
                        o = bank[PLAN[("sc", g)][0]]
                        for k in range(KC):
                            ins = mm(o[:, i * 64:(i + 1) * 64], cT[:, n % 2, e, k, :],
                                     qabs[:, k, bass.ds(b, 1), :].rearrange("p a c -> p (a c)"),
                                     start=(k == 0), stop=(k == KC - 1))
                        if i < 3 and e == 1:
                            ins.then_inc(S("cT_used"), 1)
                        if i == 3:
                            if g == 0:
                                pe.wait_ge(S("kpT"), b + 1)
                            filled(mm(o[:, 256:512], kpT[:, g, :],
                                      qpd[:, bass.ds(b, 1), :, :].rearrange("p a q c -> p (a q c)"),
                                      start=True, stop=True), ("sc", g))
                        if j == 14 and following is not None:
                            transposed_pages(1 - par, 0, following)
                        if prev is not None:
                            if j == 5:
                                softmax_max(prev)
                            if j == 7:
                                softmax_spread(prev)
                            if j == 10:
                                weighted(prev, 1 - par)
                            if j == 12:
                                weighted_T(prev)

            def half_output(j, c=0):
                s = slot(pe, W_OUT + j)
                o = reopen(pe, ("wo", j, c))
                for k in range(KD):
                    ins = mm(o[:, 0:HALF], ring[:, s, k, :], mixT[:, k, c * HALF:(c + 1) * HALF],
                             start=(k == 0), stop=(k == KD - 1))
                filled(ins, ("wo", j, c))

            pe.wait_ge(S("page_one"), 2)
            pe.wait_ge(S("wk_parts"), 2)
            sequence(0, 0, None, 1, first=True)
            with pe.Fori(0, (NB - 2) // 2) as i:
                sequence(i * 2 + 1, 1, (i, 0), (i, 1, i * 2 + 2))
                sequence(i * 2 + 2, 0, (i, 1), (i, 1, i * 2 + 3))
            sequence(NB - 1, 1, None, None)
            new_tokens(NB - 1)
            half_output(0)
            half_output(1)
            softmax_max(NB - 1, "_last")
            softmax_spread(NB - 1, "_last")
            half_output(2)
            weighted(NB - 1, 1)
            half_output(3)
            weighted_T(NB - 1, "_last")
            pe.wait_ge(S("pcT"), NB)
            o = reopen(pe, "oms")
            for h in range(MH):
                for k in range(KC):
                    ins = mm(o[MV * (h % 2):MV * (h % 2 + 1), (h // 2) * NS:(h // 2 + 1) * NS],
                             w_kvb[:, k, h * P + MV:(h + 1) * P], pcT[:, k, h, :], start=(k == 0), stop=(k == KC - 1))
            filled(ins, "oms")
            meet(pe, 4)

            for j in range(4):
                half_output(j, 1)
            for j in range(4, KD):
                s = slot(pe, W_OUT + j)
                project(("wo", j), lambda k: ring[:, s, k, :], mixT, KD)
            sums("x", [("ms_x", 0), ("ms_x", 1)], mixT, KD)
            for j in range(XH + 1):
                if j < XH:
                    s = slot(pe, W_XQ + j)
                    project(("xq", j), lambda k: ring[:, s, k, :], hTk, KD, name=None if j else "x")
                if j:
                    pe.wait_ge(S("sq_xq"), j)
                    for c in range(2):
                        o = reopen(pe, ("ms_xq", j - 1, c))
                        filled(mm(o[:, 0:HALF], ones, mixT[:, j - 1, c * HALF:(c + 1) * HALF], start=True, stop=True),
                               ("ms_xq", j - 1, c))
            pairs = [(t, u) for u in range(2) for t in range(4)]
            for n in range(len(pairs) + 2):
                if n < len(pairs):
                    t, u = pairs[n]
                    pe.wait_ge(S("xq"), 2 * u + 2)
                    o = reopen(pe, ("cs", t, u))
                    for e in range(2):
                        h = 2 * u + e
                        ins = mm(o[:, e * NM:(e + 1) * NM], xqT[:, h, t * P:(t + 1) * P], kmT[:, :, h, :],
                                 start=True, stop=True)
                    filled(ins, ("cs", t, u))
                if n >= 2:
                    t, u = pairs[n - 2]
                    pe.wait_ge(S("pcx"), n - 1)
                    o = reopen(pe, ("cp", t, u))
                    for e in range(2):
                        for m in range(2):
                            ins = tr(o[:, (e * 2 + m) * P:(e * 2 + m + 1) * P],
                                     pcx[:, (n - 2) % 2, e, m * P:(m + 1) * P], ident)
                    filled(ins, ("cp", t, u))
            pe.wait_ge(S("pcxT"), 8)
            for h in range(XH):
                o = reopen(pe, ("co", h))
                for m in range(2):
                    ins = mm(o[:, :], vm_p[:, m, h * XD:(h + 1) * XD], pcxT[:, h, m, :], start=(m == 0), stop=(m == 1))
                filled(ins, ("co", h))
            for b in range(NB + 1):
                if b < NB:
                    pe.wait_ge(S(f"kmc_in{b % 2}"), 16 * (b // 2 + 1))
                    for m in range(2):
                        o = reopen(pe, ("ck", b, m))
                        for h in range(XH):
                            ins = tr(o[:, h * P:(h + 1) * P], kmc[:, b % 2, m, h * XD:(h + 1) * XD], ident)
                        filled(ins, ("ck", b, m))
                if b:
                    q = b - 1
                    pe.wait_ge(S("kmcT"), 2 * q + 2)
                    if q % 2 == 0:
                        o = reopen(pe, ("css", q // 2))
                    o = bank[PLAN[("css", q // 2)][0]]
                    c0 = TP + 32 * (q // 4)
                    for h in range(XH):
                        ins = mm(o[32 * h:32 * h + 32, (q % 2) * NM:(q % 2 + 1) * NM], xqT[:, h, c0:c0 + 32],
                                 kmcT[:, q % 2, :, h, :], start=True, stop=True)
                    if q % 2 == 0:
                        ins.then_inc(S("kmcT_used"), 1)
                    else:
                        filled(ins, ("css", q // 2))
            for u in range(NB // 2):
                pe.wait_ge(S("psx"), u + 1)
                o = reopen(pe, ("cpT", u))
                for e in range(2):
                    for m in range(2):
                        ins = tr(o[:, (e * 2 + m) * P:(e * 2 + m + 1) * P], psx[:, 2 * u + e, m * P:(m + 1) * P], ident)
                filled(ins, ("cpT", u))
            pe.wait_ge(S("vmc_in"), 16 * NB)
            for g in range(2):
                pe.wait_ge(S("scs"), 4 * g + 4)
                o = reopen(pe, ("cv", g))
                for e in range(4):
                    b = 4 * g + e
                    for m in range(2):
                        ins = mm(o[32 * e:32 * e + 32, :], scs[:, m, b * 32:(b + 1) * 32], vmc[:, b, m, :],
                                 start=(m == 0), stop=(m == 1))
                filled(ins, ("cv", g))
            for g in range(2):
                b, n = PLAN[("cv", g)]
                pe.wait_ge(bank_free[b], n)
                o = reopen(pe, ("cvT", g))
                for h in range(XH):
                    ins = tr(o[:, h * P:(h + 1) * P], cv[:, g, h * P:(h + 1) * P], ident)
                filled(ins, ("cvT", g))
            pe.wait_ge(S("xoT_p"), XH)
            pe.wait_ge(S("xoT_s"), 2 * XH)
            for j in range(KD):
                s = slot(pe, W_XO + j // 2)
                project(("xo", j), lambda k: ring[:, s, (j % 2) * 4 + k, :], xoT, XH)
            sums("ff", [("ms_ff", 0), ("ms_ff", 1)], mixT, KD)

            def split_tile(tile, j, outs, src, k0, n_k, start, stop, key=None):
                pe.wait_ge(S("w_split"), tile + 1)
                w = wr[:, j % SPLITS, :, :].rearrange("p e (k c) -> p e k c", k=KD)
                for k in range(n_k):
                    if key and key[0] == "f1" and j == 0:
                        if k < KD // 2:
                            pe.wait_ge(S("h_low_first"), k + 1)
                        else:
                            pe.wait_ge(S("h_low_last"), k + 1 - KD // 2)
                    for n, (ew, ex) in enumerate(((0, 0), (0, 1), (1, 0))):
                        for c in range(2):
                            ins = mm(outs[c][:, 0:HALF], w[:, ew, k, :],
                                     src[:, ex, k0 + k, c * HALF:(c + 1) * HALF],
                                     start=(start and k == 0 and n == 0), stop=(stop and k == n_k - 1 and n == 2))
                            if stop and k == n_k - 1 and n == 2 and c == 0:
                                filled(ins, key)
                ins.then_inc(S("tile_done"), 1)

            for half in range(2):
                with pe.Fori(0, KF // 16) as i:
                    for j in range(8):
                        outs = [reopen(pe, ("f1", j, c), i * 2 + half * MLP_FILLS, 1) for c in range(2)]
                        split_tile(i * 8 + (half * MLP_TILES + j), j, outs, hr, 0, KD, True, True, ("f1", j, 0))
                with pe.Fori(0, KD // 4) as i:
                    for j in range(4):
                        outs = [reopen(pe, ("f2", j, c), i + half * MLP_FILLS, 1) for c in range(2)]
                        for q in range(2):
                            pe.wait_ge(S("u_low"), half * (KF // 2) + (q + 1) * KD + 2)
                            split_tile(i * 8 + (half * MLP_TILES + KF // 2 + 2 * j + q), 2 * j + q, outs, ur, q * 8, 8,
                                       q == 0, q == 1, ("f2", j, 0))
            for b in range(8):
                pe.wait_ge(bank_free[b], mlp_free[b])
            for t in range(TILES):
                c0, m = cols(t)
                for c in range(2):
                    if t == 4:
                        pe.wait_ge(S(("ytok_left", "ytok_right")[c]), 1)
                    o = bank[(2 * t + c) % 8]
                    for k in range(4):
                        ins = tr(o[0:m, k * P:(k + 1) * P], xT[:, 4 * c + k, c0:c0 + m], ident)
                    ins.then_inc(S("y_turned"), 1)

        @block.scalar
        def _(act):
            link = Chain(act, "act_step")
            A = nc.scalar.activation

            def first_root(key, r, n, width=HALF):
                o = full(act, key)
                link(A(o[:, 0:width], o[:, 0:width], ACT.Identity, bias=epsc, scale=1.0 / n))
                link(A(r, o[:, 0:width], ACT.Ln))
                A(r, r, ACT.Exp, scale=-0.5).then_inc(S("root"), 1)

            nc.scalar.preload_act_table_set("natural_log_exp_and_others")
            act.wait_ge(S("const_in"), 48)
            for j in (0, 2):
                o = full(act, ("memT", j))
                freed(nc.scalar.copy(memT[:, 2 * j:2 * j + 2, :], o[:, :].rearrange("p (a b) -> p a b", a=2)), ("memT", j))
            for k in range(KD):
                b, n = PLAN[("memT", k // 2)]
                act.wait_ge(bank_free[b], n)
                A(sq1[:, k, 0:NM], memT[:, k, :], ACT.Square).then_inc(S("squares"), 1)
            first_root("ms_mem", rstd[:, 0:NM], D, width=NM)
            for t in range(2):
                o = full(act, ("xk", t))
                link(nc.scalar.copy(km_p[:, t, :], o[:, :]))
                freed(A(sq1[:, 4 + t, 0:512], o[:, :], ACT.Square), ("xk", t))
            for k in range(0, KD, 2):
                o = full(act, ("xT", k))
                freed(nc.scalar.copy(xT[:, k, 0:TP], o[:, :]), ("xT", k))
            o = full(act, "xTs")
            freed(nc.scalar.copy(xT[:, :, TP:NT], o[:, :].rearrange("p (k c) -> p k c", k=KD)), "xTs")
            b, n = PLAN["xTs"]
            act.wait_ge(bank_free[b], n)
            act.wait_ge(S("km"), 1)
            for k in range(KD):
                b, n = PLAN[("xT", k)]
                act.wait_ge(bank_free[b], n)
                A(sq1[:, k, :], xT[:, k, :], ACT.Square).then_inc(S("squares"), 1)
            for c in range(2):
                first_root(("ms_mix", c), rstd[:, c * HALF:(c + 1) * HALF], D)
            o = full(act, ("kmT", 0))
            freed(nc.scalar.copy(kmT[:, 0, :, :].rearrange("p a b -> p (a b)"), o[:, :]), ("kmT", 0))
            def left(j):
                m = P if j < 11 else 16
                o = full(act, ("z", j, 0))
                freed(nc.scalar.copy(zT[0:m, j, 0:HALF], o[0:m, 0:HALF]), ("z", j, 0))

            for j in (0, 1, 2, 3, 11, 8):
                left(j)
            for p in range(2):
                for c in range(2):
                    o = full(act, ("gate", p, c))
                    freed(A(eb[:, p, c * HALF:(c + 1) * HALF], o[:, 0:HALF], ACT.Identity,
                            bias=gn[:, G_BA + p:G_BA + p + 1]), ("gate", p, c))
            for p in range(2):
                for c in range(2):
                    b, n = PLAN[("gate", p, c)]
                    act.wait_ge(bank_free[b], n)
            link(A(ek, eb, ACT.Abs))
            link(A(ek, ek, ACT.Exp, scale=-1.0))
            A(ek, ek, ACT.Ln, bias=1.0).then_inc(S("softplus"), 1)
            left(9)
            left(10)
            act.wait_ge(S("dq"), 3)
            link(A(ek, dq, ACT.Exp, scale=-1.0 / TAU))
            A(eq, dq, ACT.Exp, scale=1.0 / TAU).then_inc(S("e_k"), 1)
            A(eb, gb, ACT.Exp, scale=1.0 / TAU).then_inc(S("e_b"), 1)
            act.wait_ge(S("dl"), 4)
            A(dl, dl, ACT.Exp, scale=1.0 / TAU).then_inc(S("e_l"), 1)
            for name, dst, w in (("v", vtok, GH * DV), ("kva", kv, KR + ROPE)):
                for t in (0, 2, 4):
                    m = cols(t)[1]
                    o = full(act, (name, t))
                    freed(nc.scalar.copy(dst[0:m, t, :], o[0:m, 0:w]), (name, t))
            for t in range(TILES):
                b, n = PLAN[("kva", t)]
                act.wait_ge(bank_free[b], n)
            act.wait_ge(S("kv_pad"), 1)
            A(sqkv, kv, ACT.Square).then_inc(S("sq_kv"), 1)
            for j in range(4, 8):
                left(j)

            full(act, ("z", 7, 1))
            for c in range(2):
                for j in (8, 9, 10):
                    b, n = PLAN[("z", j, c)]
                    act.wait_ge(bank_free[b], n)
            A(sqa, zT[:, 8:11, :], ACT.Square).then_inc(S("sq_qa"), 1)
            act.wait_ge(S("ss_kv"), 2)
            o = full(act, ("klt", 0))
            freed(nc.scalar.copy(klt[:, 0:4, 0, :], o[:, :].rearrange("p (t c) -> p t c", t=4)), ("klt", 0))
            b, n = PLAN[("klt", 0)]
            act.wait_ge(bank_free[b], n)
            o = full(act, "klts")
            link(nc.scalar.copy(klt[0:NS, 4, :, :], o[0:NS, 0:256].rearrange("p (q c) -> p q c", q=2)))
            act.nop().then_inc(bank_free[PLAN["klts"][0]], 1)
            act.nop().then_inc(S("klt"), 2)
            for c in range(2):
                first_root(("ms_qa", c), rstd[:, c * HALF:(c + 1) * HALF], QR)
            for t in range(4):
                o = full(act, ("go", t))
                freed(nc.scalar.copy(mixT[:, 0:GH, t * P:(t + 1) * P], o[:, :].rearrange("p (h c) -> p h c", h=GH)),
                      ("go", t))
            o = full(act, "gos")
            freed(nc.scalar.copy(mixT[:, 0:GH, TP:NT], o[:, 0:GH * NS].rearrange("p (h c) -> p h c", h=GH)), "gos")
            for key in [("go", t) for t in range(4)] + ["gos"]:
                b, n = PLAN[key]
                act.wait_ge(bank_free[b], n)
            A(sqg, mixT[:, 0:GH, :], ACT.Square).then_inc(S("sq_gla"), 1)
            A(rs, zT[:, 4:8, :], ACT.Sigmoid).then_inc(S("sig_r"), 1)
            nc.scalar.preload_act_table_set("natural_log_exp_and_others")
            for h in range(GH):
                for c in range(2):
                    first_root(("ms_gla", h, c), sqg[:, h, c * HALF:(c + 1) * HALF], DV)
            meet(act, 1)

            for n in (0, 2):
                o = full(act, ("wkT", n))
                freed(nc.scalar.copy(w_kT[0:MV, 2 * n:2 * n + 2, :].rearrange("p a b -> p (a b)"), o[0:MV, :]),
                      ("wkT", n))
                b, c = PLAN[("wkT", n)]
                act.wait_ge(bank_free[b], c)
                act.nop().then_inc(S("w_kT"), 1)
            for t in range(TILES + 1):
                if t < TILES:
                    m = cols(t)[1]
                    o = full(act, ("qf", t, 0))
                    freed(nc.scalar.copy(qf[0:m, t, 0:384], o[0:m, 0:384]), ("qf", t, 0))
                if t:
                    for c in range(2):
                        b, n = PLAN[("qf", t - 1, c)]
                        act.wait_ge(bank_free[b], n)
                    if t == TILES:
                        act.wait_ge(S("pads"), 1)
                    A(sqf[:, t - 1, :], qf[:, t - 1, :], ACT.Square).then_inc(S("sq_qf"), 1)
            o = full(act, ("ckT", 0))
            freed(nc.scalar.copy(ckT[:, 0, 0:TP], o[:, :]), ("ckT", 0))
            o = full(act, "ckTs")
            nc.scalar.copy(ckT[:, :, TP:NT], o[:, 0:P].rearrange("p (k c) -> p k c", k=KC))
            act.wait_ge(S("pads"), 5)
            nc.scalar.copy(cknT[:, :, 0:NS], o[:, 0:P].rearrange("p (k c) -> p k c", k=KC))
            link(nc.scalar.copy(kpnT[0:ROPE, 0:NS], o[0:ROPE, P:P + NS]))
            act.nop().then_inc(bank_free[PLAN["ckTs"][0]], 1)
            act.nop().then_inc(S("ckT"), 2)
            act.wait_ge(S("ms_q"), 1)
            link(A(stat[:, 112:192], stat[:, 32:112], ACT.Ln))
            A(stat[:, 112:192], stat[:, 112:192], ACT.Exp, scale=-0.5).then_inc(S("r_q"), 1)
            for t in range(TILES):
                m = cols(t)[1]
                o = full(act, ("krp", t))
                if t < 4:
                    link(nc.scalar.copy(kfull[:, t, :].rearrange("p (h c) -> p h c", h=MH)[:, :, 0:MV],
                                        o[:, :].rearrange("p (h c) -> p h c", h=MH)))
                if t:
                    act.wait_ge(S("ss_kr"), t)
                A(sqk[0:m, :], o[0:m, :], ACT.Square).then_inc(S("sq_kr"), 1)
                act.wait_ge(S("sq_kr"), t + 1)
                act.nop().then_inc(bank_free[PLAN[("krp", t)][0]], 1)
            act.wait_ge(S("ms_kr"), 1)
            link(A(stat[:, 232:272], stat[:, 192:232], ACT.Ln))
            A(stat[:, 232:272], stat[:, 232:272], ACT.Exp, scale=-0.5).then_inc(S("r_kr"), 1)
            for h in range(0, MH, 2):
                o = full(act, ("qT", h))
                freed(nc.scalar.copy(qT[0:MQ, h, :], o[0:MQ, :]), ("qT", h))
            o = full(act, "qTs")
            freed(nc.scalar.copy(qTs[0:MQ, :, :].rearrange("p h c -> p (h c)"), o[0:MQ, :]), "qTs")
            b, n = PLAN["qTs"]
            act.wait_ge(bank_free[b], n)
            act.nop().then_inc(S("qTs"), 1)
            for h in range(0, MH, 2):
                o = full(act, ("kT", h))
                freed(nc.scalar.copy(kT[0:MQ, h, :], o[0:MQ, :]), ("kT", h))
            meet(act, 2)

            steps = [(t, h) for t in range(4) for h in range(MH)]
            for n in range(len(steps) + 5):
                if n < len(steps):
                    t, h = steps[n]
                    o = bank[PLAN[("s", t, h)][0]]
                    act.wait_ge(S("row_max"), n + 1)
                    if n >= 3:
                        full(act, ("pT", *steps[n - 3]))
                    A(pr[:, n % 3, 0:(t + 1) * P], o[:, 0:(t + 1) * P], ACT.Exp, bias=stat[:, 32 + n:33 + n],
                      accum_out=stat[:, 64 + n:65 + n]).then_inc(S("pr"), 1)
                    act.wait_ge(S("pr"), n + 1)
                    act.nop().then_inc(bank_free[PLAN[("s", t, h)][0]], 1)
                if 2 <= n < len(steps) + 2 and n % 2 == 1:
                    t, h = steps[n - 2]
                    o = full(act, ("pT", t, h))
                    wait_prT_free(act, n - 2, steps)
                    nc.scalar.copy(prT[:, 1, 0:(t + 1) * P], o[:, 0:(t + 1) * P]).then_inc(S("prT1"), 1)
                    act.wait_ge(S("prT1"), (n - 2) // 2 + 1)
                    act.nop().then_inc(bank_free[PLAN[("pT", t, h)][0]], 1)
                if n >= 5 and steps[n - 5][1] == MH - 1:
                    t = steps[n - 5][0]
                    o = full(act, ("poT", t))
                    freed(nc.scalar.copy(mixT[:, 4:8, t * P:(t + 1) * P], o[:, :].rearrange("p (j c) -> p j c", j=4)),
                          ("poT", t))
            meet(act, 3)

            def page_square(b, j):
                o = full(act, ("kr", j), b, 8)
                if isinstance(b, int) and b == 0 and j < 2:
                    pass
                else:
                    act.wait_ge(S("ss_pg"), b * NPG + (j - 1))
                freed(A(sqs[:, j % 2, :], o[:, :], ACT.Square), ("kr", j))

            def high_parts(b, n):
                act.wait_ge(S("cT"), b * 8 + (n + 1))
                nc.scalar.copy(c_parts[:, n % 2, 0, :, :, :].rearrange("p e k c -> p (e k c)"),
                               cT[:, n % 2, :, :, :].rearrange("p a b c -> p (a b c)")).then_inc(S("c_high"), 1)

            def rope_keys(b, first):
                o = full(act, "kpt0") if first else full(act, "kpt", b, 4)
                nc.scalar.copy(kpT.rearrange("p a b -> p (a b)"), o[:, :]).then_inc(S("kpT"), 1)
                act.wait_ge(S("kpT"), b + 1)
                act.nop().then_inc(bank_free[7], 1)

            def exponentials(b):
                act.wait_ge(S("sc_minus_max"), b + 1)
                A(pb, pb, ACT.Exp).then_inc(S("pb"), 1)

            def sequence(b, first=False, last=False):
                if first:
                    high_parts(b, 0)
                rope_keys(b, first)
                for j in range(NPG):
                    if j % 2 == 0 and j < NPG - 2:
                        high_parts(b, j // 2 + 1)
                    if j == 9 and not first:
                        exponentials(b - 1)
                    if j == NPG - 1 and not last:
                        high_parts(b + 1, 0)
                    page_square(b, j)

            sequence(0, True)
            with act.Fori(0, (NB - 2) // 2) as i:
                sequence(i * 2 + 1)
                sequence(i * 2 + 2)
            sequence(NB - 1, last=True)
            exponentials(NB - 1)
            o = full(act, "oms")
            freed(nc.scalar.copy(mixT[:, 4:8, TP:NT], o[:, 0:256].rearrange("p (j c) -> p j c", j=4)), "oms")
            meet(act, 4)

            for k in range(KD):
                act.wait_ge(S("x_mix"), 5 + k if k < 4 else 2 * k + 2)
                if k == 0:
                    full(act, ("wo", KD - 1, 1))
                A(mixT[:, k, :], xT[:, k, :], ACT.Square).then_inc(S("squares"), 1)
            for c in range(2):
                first_root(("ms_x", c), rstd[:, c * HALF:(c + 1) * HALF], D)
            for j in range(XH + 1):
                if j < XH:
                    for c in range(2):
                        o = full(act, ("xq", j, c))
                        freed(nc.scalar.copy(xqT[:, j, c * HALF:(c + 1) * HALF], o[:, 0:HALF]), ("xq", j, c))
                    for c in range(2):
                        b, n = PLAN[("xq", j, c)]
                        act.wait_ge(bank_free[b], n)
                    A(mixT[:, j, :], xqT[:, j, :], ACT.Square).then_inc(S("sq_xq"), 1)
                if j:
                    for c in range(2):
                        first_root(("ms_xq", j - 1, c), mixT[:, 3 + j, c * HALF:(c + 1) * HALF], XD)
            pairs = [(t, u) for u in range(2) for t in range(4)]
            for n in range(len(pairs) + 2):
                if n < len(pairs):
                    t, u = pairs[n]
                    o = bank[PLAN[("cs", t, u)][0]]
                    act.wait_ge(S("cmax"), n + 1)
                    if n >= 2:
                        full(act, ("cp", *pairs[n - 2]))
                    for e in range(2):
                        A(pcx[:, n % 2, e, :], o[:, e * NM:(e + 1) * NM], ACT.Exp,
                          bias=stat[:, 2 * n + e:2 * n + e + 1],
                          accum_out=stat[:, 16 + 2 * n + e:17 + 2 * n + e]).then_inc(S("pcx_raw"), 1)
                    act.wait_ge(S("pcx_raw"), 2 * n + 2)
                    act.nop().then_inc(bank_free[PLAN[("cs", t, u)][0]], 1)
                if n >= 2:
                    t, u = pairs[n - 2]
                    o = full(act, ("cp", t, u))
                    nc.scalar.copy(pcxT[:, 2 * u:2 * u + 2, :, t * P:(t + 1) * P],
                                   o[:, :].rearrange("p (e m c) -> p e m c", e=2, m=2)).then_inc(S("pcxT"), 1)
                    act.wait_ge(S("pcxT"), n - 1)
                    act.nop().then_inc(bank_free[PLAN[("cp", t, u)][0]], 1)
            for h in range(XH):
                o = full(act, ("co", h))
                nc.scalar.copy(xoT[:, h, 0:TP], o[:, :]).then_inc(S("xoT_p"), 1)
                act.wait_ge(S("xoT_p"), h + 1)
                act.nop().then_inc(bank_free[PLAN[("co", h)][0]], 1)
            for b in range(NB):
                for m in range(2):
                    o = full(act, ("ck", b, m))
                    if b >= 2 and m == 0:
                        if b % 2 == 0:
                            act.wait_ge(S("kmcT_used"), b // 2)
                        else:
                            full(act, ("css", (b - 2) // 2))
                    nc.scalar.copy(kmcT[:, b % 2, m, :, :].rearrange("p a b -> p (a b)"), o[:, :]).then_inc(S("kmcT"), 1)
                    act.wait_ge(S("kmcT"), 2 * b + m + 1)
                    act.nop().then_inc(bank_free[PLAN[("ck", b, m)][0]], 1)
                for u in {3: [0], 5: [1], 7: [2, 3]}.get(b, []):
                    o = bank[PLAN[("css", u)][0]]
                    act.wait_ge(S("smax"), u + 1)
                    for e in range(2):
                        A(psx[:, 2 * u + e, :], o[:, e * NM:(e + 1) * NM], ACT.Exp,
                          bias=stat[:, 64 + 2 * u + e:65 + 2 * u + e],
                          accum_out=stat[:, 72 + 2 * u + e:73 + 2 * u + e]).then_inc(S("psx_raw"), 1)
                    act.wait_ge(S("psx_raw"), 2 * u + 2)
                    act.nop().then_inc(bank_free[PLAN[("css", u)][0]], 1)
            o = full(act, ("cv", 0))
            freed(nc.scalar.copy(cv[:, 0, :], o[:, :]), ("cv", 0))
            for k in range(KD):
                act.wait_ge(S("x_cross"), 2 * k + 2)
                A(mixT[:, k, :], xT[:, k, :], ACT.Square).then_inc(S("squares"), 1)
            for c in range(2):
                first_root(("ms_ff", c), rstd[:, c * HALF:(c + 1) * HALF], D)

            for k in range(KD):
                act.wait_ge(S("normed"), normed["ff"] + k + 1)
                nc.scalar.copy(hr[:, 0, k, :], hTk[:, k, :]).then_inc(S("h_high"), 1)
            for half in range(2):
                with act.Fori(0, KF // 16) as i:
                    for j in range(8):
                        n = i * 8 + (half * (KF // 2) + j)
                        tile = i * 8 + (half * MLP_TILES + j)
                        o = full(act, ("f1", j, 0), i * 2 + half * MLP_FILLS, 1)
                        freed(A(relu[:, 0:HALF], o[:, 0:HALF], ACT.Relu), ("f1", j, 0))
                        act.wait_ge(S("tile_done"), tile + 1)
                        o = bank[PLAN[("f1", j, 1)][0]]
                        freed(A(relu[:, HALF:NT], o[:, 0:HALF], ACT.Relu), ("f1", j, 1))
                        for c in range(2):
                            b, m = at(("f1", j, c), i * 2 + half * MLP_FILLS, 1)
                            act.wait_ge(bank_free[b], m)
                        act.wait_ge(S("u_low"), n + 1)
                        A(usq[:, j % 2, :], relu, ACT.Square).then_inc(S("u"), 1)
                        act.wait_ge(S("u"), n + 1)
                        nc.scalar.copy(ur[:, 0, bass.ds(i * 8 + j, 1), :].rearrange("p a c -> p (a c)"),
                                       usq[:, j % 2, :]).then_inc(S("u_high"), 1)
            for t in range(TILES):
                m = cols(t)[1]
                act.wait_ge(S("y_turned"), 2 * t + 1)
                if t == 4:
                    act.wait_ge(S("y_out0"), 32)
                nc.scalar.copy(ytok[0:m, t % 4, 0:512], bank[2 * t % 8][0:m, :]).then_inc(S("ytok_left"), 1)

        @block.vector
        def _(dve):
            link = Chain(dve, "dve_step")
            V = nc.vector

            def refine(key, r, n, width=HALF):
                o = bank[PLAN[key][0]]
                dve.wait_ge(S("root"), n)
                m = o[:, 0:width]
                link(V.scalar_tensor_tensor(out=m, in0=m, scalar=-0.5, in1=r, op0=ALU.mult, op1=ALU.mult))
                link(V.tensor_tensor(m, m, r, ALU.mult))
                link(V.scalar_tensor_tensor(out=r, in0=m, scalar=1.5, in1=r, op0=ALU.add, op1=ALU.mult))
                dve.nop().then_inc(bank_free[PLAN[key][0]], 1)

            def scaled(name, src, dst, g0, n_k, width=NT):
                if name == "mem":
                    refine("ms_mem", rstd[:, 0:NM], 1, width=NM)
                elif name != "qa":
                    for c in range(2):
                        refine((f"ms_{name}", c), rstd[:, c * HALF:(c + 1) * HALF], roots[name] + c + 1)
                for k in range(n_k):
                    V.scalar_tensor_tensor(out=dst[:, k, 0:width], in0=src[:, k, 0:width],
                                           scalar=gn[:, g0 + k:g0 + k + 1], in1=rstd[:, 0:width],
                                           op0=ALU.mult, op1=ALU.mult).then_inc(S("normed"), 1)

            dve.wait_ge(S("const_in"), 48)
            for j in (1, 3):
                o = full(dve, ("memT", j))
                freed(V.tensor_copy(memT[:, 2 * j:2 * j + 2, :], o[:, :].rearrange("p (a b) -> p a b", a=2)), ("memT", j))
            for j in range(4):
                b, n = PLAN[("memT", j)]
                dve.wait_ge(bank_free[b], n)
            scaled("mem", memT, hmT, G_MEM, KD, width=NM)
            b, n = PLAN[("xk", 1)]
            dve.wait_ge(bank_free[b], n)
            V.tensor_reduce(stat[:, 0:8].rearrange("p (t h) -> p t h", t=2),
                            sq1[:, 4:6, 0:512].rearrange("p t (h d) -> p t h d", h=XH), AX.X, ALU.add).then_inc(S("ss_km"), 1)
            for t in range(2):
                o = full(dve, ("xv", t))
                V.tensor_copy(vm_p[:, t, :], o[:, :]).then_inc(S("vm"), 1)
                dve.wait_ge(S("vm"), t + 1)
                dve.nop().then_inc(bank_free[PLAN[("xv", t)][0]], 1)
            dve.wait_ge(S("r_km"), 1)
            km8 = km_p.rearrange("p t (h d) -> p (t h) d", h=XH)
            link(V.tensor_tensor(km8, km8, spread(stat[:, 8:16], 2, XD), ALU.mult))
            V.tensor_tensor(km8, km8, spread(row[:, R_XK:R_XK + XD], 1, 8), ALU.mult).then_inc(S("km"), 1)
            for k in range(1, KD, 2):
                o = full(dve, ("xT", k))
                freed(V.tensor_copy(xT[:, k, 0:TP], o[:, :]), ("xT", k))
            for key in [("xT", k) for k in range(KD)] + ["xTs"]:
                b, n = PLAN[key]
                dve.wait_ge(bank_free[b], n)
            full(dve, ("kmT", 1))
            dve.wait_ge(S("mk_out"), 16)
            scaled("mix", xT, hTk, G_MIX, KD)
            o = full(dve, ("kmT", 1))
            freed(V.tensor_copy(kmT[:, 1, :, :].rearrange("p a b -> p (a b)"), o[:, :]), ("kmT", 1))
            def right(j):
                m = P if j < 11 else 16
                o = full(dve, ("z", j, 1))
                freed(V.tensor_copy(zT[0:m, j, HALF:NT], o[0:m, 0:HALF]), ("z", j, 1))

            for j in (0, 1, 2, 3, 11, 8):
                right(j)
            dve.wait_ge(S("softplus"), 1)
            link(V.scalar_tensor_tensor(out=ek, in0=eb, scalar=0.0, in1=ek, op0=ALU.min, op1=ALU.subtract))
            for p in range(2):
                link(V.tensor_tensor_scan(gb[:, p, :], scanm, ek[:, p, :], 0.0, ALU.mult, ALU.add))

            def chunks(ap, p, prompt=True):
                return (ap[:, p, 0:TP].rearrange("p (c t) -> p c t", c=4) if prompt
                        else ap[:, p, TP:NT].rearrange("p (c t) -> p c t", c=NB))

            for p in range(2):
                g = chunks(gb, p)
                V.tensor_tensor(chunks(dq, p), g, g[:, :, 63:64].broadcast_to([P, 4, P]), ALU.subtract).then_inc(S("dq"), 1)
            link(V.tensor_copy(dq[:, :, TP:NT], gb[:, :, TP:NT]))
            dve.wait_ge(S("dq"), 2)
            V.tensor_scalar(dq, dq, CLAMP, -CLAMP, ALU.min, ALU.max).then_inc(S("dq"), 1)
            for p in range(2):
                g, gs = chunks(gb, p), chunks(gb, p, False)
                V.tensor_tensor(chunks(dl, p), g[:, :, P - 1:P].broadcast_to([P, 4, P]), g, ALU.subtract).then_inc(S("dl"), 1)
                V.tensor_tensor(chunks(dl, p, False), gs[:, :, TS - 1:TS].broadcast_to([P, NB, TS]), gs,
                                ALU.subtract).then_inc(S("dl"), 1)
            right(9)
            right(10)
            for name, dst, w in (("v", vtok, GH * DV), ("kva", kv, KR + ROPE)):
                for t in (1, 3):
                    o = full(dve, (name, t))
                    freed(V.tensor_copy(dst[:, t, :], o[:, 0:w]), (name, t))
            dve.wait_ge(S("sq_kv"), 1)
            V.tensor_reduce(stat[:, 0:5], sqkv[:, :, 0:KR], AX.X, ALU.add).then_inc(S("ss_kv"), 1)
            V.tensor_reduce(stat[:, 5:10], sqkv[:, :, KR:KR + ROPE], AX.X, ALU.add).then_inc(S("ss_kv"), 1)
            dve.wait_ge(S("pads2"), 2)
            for dst, e, sem in ((qz, eq, "e_k"), (qi, eb, "e_b")):
                dve.wait_ge(S(sem), 1)
                for h in range(2):
                    for p in range(2):
                        r = slice(64 * h, 64 * h + 64)
                        V.scalar_tensor_tensor(out=dst[r, p, h, :], in0=zT[r, p, :], scalar=float(DK) ** -0.5,
                                               in1=e[r, p, :], op0=ALU.mult, op1=ALU.mult).then_inc(S("qz"), 1)
            for j in range(4, 8):
                right(j)

            o = full(dve, ("klt", 1))
            V.tensor_copy(klt[:, 0:4, 1, :], o[:, :].rearrange("p (t c) -> p t c", t=4)).then_inc(S("klt"), 1)
            dve.wait_ge(S("klt"), 3)
            dve.nop().then_inc(bank_free[PLAN[("klt", 1)][0]], 1)
            for t in range(4):
                o = full(dve, ("att", t))
                V.tensor_tensor(att[:, t, :, :], o[:, :].rearrange("p (h c) -> p h c", h=GH), spread(tri, 1, GH),
                                ALU.mult).then_inc(S("att"), 1)
                dve.wait_ge(S("att"), t + 1)
                dve.nop().then_inc(bank_free[PLAN[("att", t)][0]], 1)
            o = full(dve, "atts")
            V.tensor_tensor(atts[0:NS, :, :], o[0:NS, 0:256].rearrange("p (h c) -> p h c", h=GH),
                            spread(smask, 1, GH), ALU.mult).then_inc(S("att"), 1)
            dve.wait_ge(S("att"), 5)
            dve.nop().then_inc(bank_free[PLAN["atts"][0]], 1)
            for c in range(2):
                refine(("ms_qa", c), rstd[:, c * HALF:(c + 1) * HALF], roots["qa"] + c + 1)

            def masked_keys(b):
                V.tensor_scalar(klm[0:NS, b % 2, :, :], klt[0:NS, 4, :, :], seqm[:, b:b + 1], None,
                                ALU.mult).then_inc(S("klm"), 1)

            dve.wait_ge(S("qz"), 8)
            for t in range(4):
                o = full(dve, ("st", t))
                for h in range(2):
                    for p in range(2):
                        r = slice(64 * h, 64 * h + 64)
                        upd = o[r, p * 256 + h * P:p * 256 + (h + 1) * P]
                        if t == 0:
                            ins = V.tensor_copy(st[r, p, :], upd)
                        else:
                            ins = V.scalar_tensor_tensor(out=st[r, p, :], in0=st[r, p, :],
                                                         scalar=eb[r, p, t * P + P - 1:(t + 1) * P], in1=upd,
                                                         op0=ALU.mult, op1=ALU.add)
                        ins.then_inc(S("gla_state"), 1)
                dve.wait_ge(S("gla_state"), 4 * t + 4)
                dve.nop().then_inc(bank_free[PLAN[("st", t)][0]], 1)
            masked_keys(0)
            masked_keys(1)
            dve.wait_ge(S("state_in"), 16)
            for b in range(NB):
                o = full(dve, ("sst", b))
                for h in range(2):
                    for p in range(2):
                        r = slice(64 * h, 64 * h + 64)
                        c = TP + b * TS + TS - 1
                        V.scalar_tensor_tensor(out=st_s[r, b, p, :], in0=st_s[r, b, p, :], scalar=eb[r, p, c:c + 1],
                                               in1=o[r, p * 256 + h * P:p * 256 + (h + 1) * P],
                                               op0=ALU.mult, op1=ALU.add).then_inc(S("gla_state_s"), 1)
                dve.wait_ge(S("gla_state_s"), 4 * b + 4)
                dve.nop().then_inc(bank_free[PLAN[("sst", b)][0]], 1)
                if b + 2 < NB:
                    masked_keys(b + 2)
            scaled("qa", zT[:, 8:11, :], zT[:, 8:11, :], G_QA, KQ)
            for h in range(GH):
                for c in range(2):
                    refine(("ms_gla", h, c), sqg[:, h, c * HALF:(c + 1) * HALF], roots["gla"] + 2 * h + c + 1)
            link(V.scalar_tensor_tensor(out=mixT[:, 0:GH, :], in0=mixT[:, 0:GH, :], scalar=gn[:, G_GLA:G_GLA + 1],
                                        in1=sqg, op0=ALU.mult, op1=ALU.mult))
            dve.wait_ge(S("rs"), 1)
            V.tensor_tensor(mixT[:, 0:GH, :], mixT[:, 0:GH, :], rs, ALU.mult)
            meet(dve, 1)

            def rotate(v, c, s, tmp):
                return rotated(V, link, v, c, s, tmp)

            link(V.tensor_scalar(gq2, row[:, R_QN:R_QN + MV], MLA_SCALE * MV ** 0.5, None, ALU.mult))
            link(V.tensor_tensor(gq2, gq2, row[:, R_KN:R_KN + MV], ALU.mult))
            link(V.tensor_scalar(gqr, row[:, R_QR:R_QR + ROPE], MLA_SCALE, None, ALU.mult))
            for n in (1, 3):
                o = full(dve, ("wkT", n))
                link(V.tensor_copy(w_kT[0:MV, 2 * n:2 * n + 2, :].rearrange("p a b -> p (a b)"), o[0:MV, :]))
                dve.nop().then_inc(S("w_kT"), 1)
                dve.nop().then_inc(bank_free[PLAN[("wkT", n)][0]], 1)
            s4 = sqf.rearrange("p t (h c) -> p t h c", h=MH)
            for t in range(TILES + 1):
                if t < TILES:
                    m = cols(t)[1]
                    o = full(dve, ("qf", t, 1))
                    freed(V.tensor_copy(qf[0:m, t, 384:768], o[0:m, 0:384]), ("qf", t, 1))
                if t:
                    dve.wait_ge(S("sq_qf"), t)
                    link(V.tensor_reduce(stat[:, 24 + 8 * t:32 + 8 * t], s4[:, t - 1, :, 0:MV], AX.X, ALU.add))
                    link(V.tensor_reduce(stat[:, 64 + 8 * t:72 + 8 * t], s4[:, t - 1, :, MV:MQ], AX.X, ALU.add))
            link(V.tensor_scalar(stat[:, 32:72], stat[:, 32:72], 1.0 / MV, EPS, ALU.mult, ALU.add))
            V.tensor_scalar(stat[:, 72:112], stat[:, 72:112], 1.0 / ROPE, EPS, ALU.mult, ALU.add).then_inc(S("ms_q"), 1)
            o = full(dve, ("ckT", 1))
            V.tensor_copy(ckT[:, 1, 0:TP], o[:, :]).then_inc(S("ckT"), 1)
            dve.drain()
            dve.nop().then_inc(bank_free[PLAN[("ckT", 1)][0]], 1)
            q8 = qf.rearrange("p t (h c) -> p (t h) c", h=MH)

            def key_sums(t):
                m = cols(t)[1]
                dve.wait_ge(S("sq_kr"), t + 1)
                V.tensor_reduce(stat[0:m, 192 + 8 * t:200 + 8 * t], sqk[0:m, :].rearrange("p (h c) -> p h c", h=MH),
                                AX.X, ALU.add).then_inc(S("ss_kr"), 1)

            def newton(m, r):
                link(V.scalar_tensor_tensor(out=m, in0=m, scalar=-0.5, in1=r, op0=ALU.mult, op1=ALU.mult))
                link(V.tensor_tensor(m, m, r, ALU.mult))
                link(V.scalar_tensor_tensor(out=r, in0=m, scalar=1.5, in1=r, op0=ALU.add, op1=ALU.mult))

            dve.wait_ge(S("r_q"), 1)
            newton(stat[:, 32:112], stat[:, 112:192])
            link(V.tensor_tensor(q8[:, :, 0:MV], q8[:, :, 0:MV], spread(stat[:, 112:152], 2, MV), ALU.mult))
            link(V.tensor_tensor(q8[:, :, 0:MV], q8[:, :, 0:MV], spread(gq2, 1, 40), ALU.mult))
            link(V.tensor_tensor(q8[:, :, MV:MQ], q8[:, :, MV:MQ], spread(stat[:, 152:192], 2, ROPE), ALU.mult))
            link(V.tensor_tensor(q8[:, :, MV:MQ], q8[:, :, MV:MQ], spread(gqr, 1, 40), ALU.mult))
            qr = qf.rearrange("p t (h c) -> p t h c", h=MH)[:, :, :, MV:MQ]
            qtmp = [view(arena, 15396 + 640 * n, TILES, MH, 16) for n in range(4)]
            rotate(qr, spread(cosn, 2, MH), spread(sinn, 2, MH), qtmp).then_inc(S("q_ready"), 1)
            dve.wait_ge(S("q_ready"), 1)
            full(dve, ("ms_qa", 1))
            V.tensor_copy(qp4[0:NS, :, :].rearrange("p h (q c) -> p h q c", q=4),
                          spread(qf[0:NS, 4, :].rearrange("p (h c) -> p h c", h=MH)[:, :, MV:MQ], 2, 4)
                          ).then_inc(S("qp4"), 1)
            for t in range(TILES):
                key_sums(t)
            dve.wait_ge(S("ss_kr"), TILES)
            V.tensor_scalar(stat[:, 192:232], stat[:, 192:232], 1.0, MV * EPS, ALU.mult, ALU.add).then_inc(S("ms_kr"), 1)
            for t in range(4):
                o = full(dve, ("vp", t))
                freed(V.tensor_copy(vp[:, t, :], o[:, :]), ("vp", t))
            dve.wait_ge(S("r_kr"), 1)
            newton(stat[:, 192:232], stat[:, 232:272])
            k8 = kfull.rearrange("p t (h c) -> p (t h) c", h=MH)
            V.tensor_tensor(k8[:, :, 0:MV], k8[:, :, 0:MV], spread(stat[:, 232:264], 2, MV), ALU.mult).then_inc(
                S("kfull"), 1)
            for h in range(1, MH, 2):
                o = full(dve, ("qT", h))
                freed(V.tensor_copy(qT[0:MQ, h, :], o[0:MQ, :]), ("qT", h))
            for k in range(KC):
                o = full(dve, ("qabs", k))
                freed(V.tensor_copy(qabs[:, k, :, :].rearrange("p b (h t) -> p h b t", h=MH),
                                    o[:, :].rearrange("p (h b t) -> p h b t", h=MH, b=NB)), ("qabs", k))
            dve.wait_ge(S("pads"), 5)
            o = full(dve, "qpd")
            for q in range(4):
                r = slice(32 * q, 32 * q + 32)
                ins = V.tensor_copy(qpd[r, :, q, :].rearrange("p b (h t) -> p h b t", h=MH),
                                    o[r, :].rearrange("p (h b t) -> p h b t", h=MH, b=NB))
            link(ins)
            dve.nop().then_inc(bank_free[PLAN["qpd"][0]], 1)
            for h in range(1, MH, 2):
                o = full(dve, ("kT", h))
                freed(V.tensor_copy(kT[0:MQ, h, :], o[0:MQ, :]), ("kT", h))
            V.tensor_copy(stat[0:NS, 264 + 16:264 + 24], stat[0:NS, 264:272])
            meet(dve, 2)

            steps = [(t, h) for t in range(4) for h in range(MH)]
            for n in range(len(steps) + 5):
                if n < len(steps):
                    t, h = steps[n]
                    o = full(dve, ("s", t, h))
                    link(V.tensor_tensor(o[:, t * P:(t + 1) * P], o[:, t * P:(t + 1) * P], causal, ALU.add))
                    V.tensor_reduce(stat[:, 32 + n:33 + n], o[:, 0:(t + 1) * P], AX.X, ALU.max, negate=True).then_inc(
                        S("row_max"), 1)
                if 2 <= n < len(steps) + 2 and n % 2 == 0:
                    t, h = steps[n - 2]
                    o = full(dve, ("pT", t, h))
                    wait_prT_free(dve, n - 2, steps)
                    V.tensor_copy(prT[:, 0, 0:(t + 1) * P], o[:, 0:(t + 1) * P]).then_inc(S("prT0"), 1)
                    dve.wait_ge(S("prT0"), (n - 2) // 2 + 1)
                    dve.nop().then_inc(bank_free[PLAN[("pT", t, h)][0]], 1)
                if 4 <= n < len(steps) + 4 and steps[n - 4][1] == MH - 1:
                    t = steps[n - 4][0]
                    o = full(dve, ("po", t))
                    dve.wait_ge(S("pr"), 8 * t + 8)
                    link(V.reciprocal(stat[:, 0:8], stat[:, 64 + 8 * t:72 + 8 * t]))
                    if t >= 2:
                        full(dve, ("poT", t - 2))
                    V.tensor_tensor(ot[:, t % 2, :].rearrange("p (h c) -> p h c", h=MH),
                                    o[:, :].rearrange("p (h c) -> p h c", h=MH), spread(stat[:, 0:8], 2, MV),
                                    ALU.mult).then_inc(S("ot"), 1)
                    dve.wait_ge(S("ot"), t + 1)
                    dve.nop().then_inc(bank_free[PLAN[("po", t)][0]], 1)
            meet(dve, 3)

            V.memset(mx, 0.0)
            V.memset(pcs, 0.0)
            for v in sc:
                link(V.memset(v[:, NPG, :], NEG))
            for _ in range(2):
                dve.nop().then_inc(S("sc_room"), 1)

            def turned(b, n):
                o = full(dve, ("ct", n), b, 4)
                if not (isinstance(b, int) and b == 0 and n < 2):
                    m = n - 2 if n >= 2 else n + 6
                    bb = b if n >= 2 else b - 1
                    if m % 2 == 0:
                        dve.wait_ge(S("cT_used"), bb * 4 + (m // 2 + 1))
                    else:
                        full(dve, ("sc", m // 2), bb, 2)
                rows_T = cT[:, n % 2, :, :, :].rearrange("p a b c -> p (a b c)")
                V.tensor_copy(rows_T, o[:, :]).then_inc(S("cT"), 1)
                dve.wait_ge(S("cT"), b * 8 + (n + 1))
                dve.nop().then_inc(bank_free[n % 2], 1)
                dve.wait_ge(S("c_high"), b * 8 + (n + 1))
                V.tensor_tensor(c_parts[:, n % 2, 1, :, :, :].rearrange("p e k c -> p (e k c)"), rows_T,
                                c_parts[:, n % 2, 0, :, :, :].rearrange("p e k c -> p (e k c)"),
                                ALU.subtract).then_inc(S("c_low"), 1)

            def page_sums(b, j):
                o = bank_free[2 + j % 2]
                dve.wait_ge(o, b * 8 + (PLAN[("kr", j)][1]))
                g = (j // 4) % 2
                V.tensor_reduce(stat[:, 64 + 32 * g + 8 * (j % 4):72 + 32 * g + 8 * (j % 4)],
                                sqs[:, j % 2, :].rearrange("p (h c) -> p h c", h=MH), AX.X, ALU.add).then_inc(
                    S("ss_pg"), 1)

            def group_scores(b, g, par):
                o = full(dve, ("sc", g), b, 2)
                dve.wait_ge(S("r_pg"), b * 4 + (g + 1))
                s4 = sc[par][:, 4 * g:4 * g + 4, :]
                r = stat[:, 128 + 32 * (g % 2):160 + 32 * (g % 2)]
                V.tensor_tensor(s4.rearrange("p j (h t) -> p (j h) t", h=MH),
                                o[:, 0:256].rearrange("p (j t) -> p j t", t=TS), spread(r, 2, TS), ALU.mult).then_inc(
                    S("sc_done"), 1)
                dve.wait_ge(S("sc_done"), b * 4 + (g + 1))
                dve.nop().then_inc(S("sc_room"), 1)
                V.tensor_tensor(s4.rearrange("p j c -> p (j c)"), s4.rearrange("p j c -> p (j c)"), o[:, 256:512],
                                ALU.add).then_inc(S("sc_sum"), 1)
                dve.wait_ge(S("sc_sum"), b * 4 + (g + 1))
                dve.nop().then_inc(bank_free[4 + g % 2], 1)

            def new_scores(b, par):
                o = full(dve, "scn", b, 2)
                sn = sc[par][0:NS, NPG, :]
                V.tensor_tensor(sn.rearrange("p (h t) -> p h t", h=MH), o[0:NS, 0:64].rearrange("p (h t) -> p h t", h=MH),
                                spread(stat[0:NS, 280:288], 2, TS), ALU.mult).then_inc(S("scn_step"), 1)
                dve.wait_ge(S("scn_step"), b * 3 + 1)
                V.tensor_tensor(sn, sn, o[0:NS, 64:128], ALU.add).then_inc(S("scn_step"), 1)
                dve.wait_ge(S("scn_step"), b * 3 + 2)
                dve.nop().then_inc(bank_free[6], 1)
                V.tensor_tensor(sn.rearrange("p (h t) -> p h t", h=MH), sn.rearrange("p (h t) -> p h t", h=MH),
                                spread(sneg[:, bass.ds(b * TS, TS)], 1, MH), ALU.add).then_inc(S("scn_step"), 1)
                dve.wait_ge(S("scn_step"), b * 3 + 3)
                dve.wait_ge(S("sc_sum"), b * 4 + 4)
                V.tensor_reduce(mx[:, 0:64], sc[par].rearrange("p j c -> p c j"), AX.X, ALU.max).then_inc(S("mx"), 1)

            def row_max(b, last=""):
                o = full(dve, "mt" + last, b, 4)
                V.tensor_reduce(stat[0:64, 200:201], o[0:64, 0:P], AX.X, ALU.max, negate=True).then_inc(S("nmx"), 1)
                dve.wait_ge(S("nmx"), b + 1)
                dve.nop().then_inc(bank_free[7], 1)
                V.tensor_scalar(dg[0:64, :], ident[0:64, 0:64], stat[0:64, 200:201], None, ALU.mult).then_inc(S("dg"), 1)

            def minus_max(b, par, last=""):
                o = full(dve, "mb" + last, b, 4)
                if not (isinstance(b, int) and b == 0):
                    dve.wait_ge(S("pv_out"), b)
                V.tensor_tensor(pb, sc[par], spread(o[:, 0:64], 1, NPG + 1), ALU.add).then_inc(S("sc_minus_max"), 1)
                dve.wait_ge(S("sc_minus_max"), b + 1)
                dve.nop().then_inc(bank_free[7], 1)

            def divide(b):
                o = full(dve, "pv", b, 2)
                V.reciprocal(stat[0:64, 201:202], o[0:64, KR:KR + 1]).then_inc(S("pv_r"), 1)
                dve.wait_ge(S("pv_r"), b + 1)
                if not (isinstance(b, int) and b == 0):
                    dve.wait_ge(S("pcT"), b)
                V.tensor_scalar(pcs[0:64, :], o[0:64, 0:KR], stat[0:64, 201:202], None, ALU.mult).then_inc(S("pcs"), 1)
                dve.wait_ge(S("pcs"), b + 1)
                dve.nop().then_inc(bank_free[6], 1)
                dve.nop().then_inc(S("pv_out"), 1)

            def keep(b, last=""):
                o = full(dve, "pct" + last, b, 4)
                V.tensor_copy(pcT[:, :, :, bass.ds(b * TS, TS)],
                              o[:, 0:KC * P].rearrange("p (k h t) -> p k h t", k=KC, h=2 * MH)[:, :, 0:MH, :]).then_inc(S("pcT"), 1)
                dve.wait_ge(S("pcT"), b + 1)
                dve.nop().then_inc(bank_free[7], 1)

            def sequence(b, par, first=False, last=False):
                if first:
                    turned(b, 0)
                for n in range(8):
                    if n < 7:
                        turned(b, n + 1)
                    if not first and n == 3:
                        row_max(b - 1)
                    if not first and n == 4:
                        minus_max(b - 1, 1 - par)
                    page_sums(b, 2 * n)
                    if not first and n == 1:
                        group_scores(b - 1, 3, 1 - par)
                        new_scores(b - 1, 1 - par)
                    if n in (3, 5, 7):
                        group_scores(b, n // 2 - 1, par)
                    if not first and n == 5:
                        divide(b - 1)
                    if not first and n == 6:
                        keep(b - 1)
                    if n == 7 and not last:
                        turned(b + 1, 0)
                    page_sums(b, 2 * n + 1)

            sequence(0, 0, True)
            with dve.Fori(0, (NB - 2) // 2) as i:
                sequence(i * 2 + 1, 1)
                sequence(i * 2 + 2, 0)
            sequence(NB - 1, 1, last=True)
            group_scores(NB - 1, 3, 1)
            new_scores(NB - 1, 1)
            row_max(NB - 1, "_last")
            minus_max(NB - 1, 1, "_last")
            divide(NB - 1)
            keep(NB - 1, "_last")
            meet(dve, 4)

            def add_to_x(name, sem, order):
                for n, (j, c) in enumerate(order):
                    o = full(dve, (name, j, c))
                    r = xT[:, j, c * HALF:(c + 1) * HALF]
                    V.tensor_tensor(r, r, o[:, 0:HALF], ALU.add).then_inc(S(sem), 1)
                    dve.wait_ge(S(sem), n + 1)
                    dve.nop().then_inc(bank_free[PLAN[(name, j, c)][0]], 1)

            in_turn = [(j, c) for j in range(KD) for c in range(2)]

            link(V.tensor_scalar(gxq, gn[:, G_XQ:G_XQ + 1], float(XD) ** -0.5, None, ALU.mult))
            add_to_x("wo", "x_mix", [(j, 0) for j in range(4)] + [(j, 1) for j in range(4)] + in_turn[8:])
            scaled("x", xT, hTk, G_X, KD)
            def query_head(j):
                for c in range(2):
                    refine(("ms_xq", j, c), mixT[:, 4 + j, c * HALF:(c + 1) * HALF], roots["xq"] + 2 * j + c + 1)
                V.scalar_tensor_tensor(out=xqT[:, j, :], in0=xqT[:, j, :], scalar=gxq,
                                       in1=mixT[:, 4 + j, :], op0=ALU.mult, op1=ALU.mult).then_inc(S("xq"), 1)
            for j in range(XH - 1):
                query_head(j)
            pairs = [(t, u) for u in range(2) for t in range(4)]
            for n in range(len(pairs) + 1):
                if n < len(pairs):
                    if n == 2:
                        query_head(XH - 1)
                    o = full(dve, ("cs", *pairs[n]))
                    V.tensor_reduce(stat[:, 2 * n:2 * n + 2], o[:, :].rearrange("p (e c) -> p e c", e=2), AX.X, ALU.max,
                                    negate=True).then_inc(S("cmax"), 1)
                if n >= 1:
                    m = n - 1
                    dve.wait_ge(S("pcx_raw"), 2 * m + 2)
                    link(V.reciprocal(stat[:, 32 + 2 * m:34 + 2 * m], stat[:, 16 + 2 * m:18 + 2 * m]))
                    V.tensor_tensor(pcx[:, m % 2, :, :], pcx[:, m % 2, :, :],
                                    spread(stat[:, 32 + 2 * m:34 + 2 * m], 2, NM), ALU.mult).then_inc(S("pcx"), 1)
            for u in range(NB // 2 + 1):
                if u < NB // 2:
                    o = full(dve, ("css", u))
                    V.tensor_reduce(stat[:, 64 + 2 * u:66 + 2 * u], o[:, :].rearrange("p (e c) -> p e c", e=2), AX.X,
                                    ALU.max, negate=True).then_inc(S("smax"), 1)
                if u:
                    v = u - 1
                    dve.wait_ge(S("psx_raw"), 2 * v + 2)
                    link(V.reciprocal(stat[:, 80 + 2 * v:82 + 2 * v], stat[:, 72 + 2 * v:74 + 2 * v]))
                    V.tensor_tensor(psx[:, 2 * v:2 * v + 2, :], psx[:, 2 * v:2 * v + 2, :],
                                    spread(stat[:, 80 + 2 * v:82 + 2 * v], 2, NM), ALU.mult).then_inc(S("psx"), 1)
            for b in range(NB):
                o = full(dve, ("cpT", b // 2))
                V.tensor_copy(scs[:, :, b * 32:(b + 1) * 32].rearrange("p m (h t) -> p m h t", h=XH),
                              o[:, :].rearrange("p (e m h b t) -> p e m h b t", e=2, m=2, h=XH, b=4)[:, b % 2, :, :, b % 4, :]
                              ).then_inc(S("scs"), 1)
                dve.wait_ge(S("scs"), b + 1)
                if b % 2:
                    dve.nop().then_inc(bank_free[PLAN[("cpT", b // 2)][0]], 1)
            o = full(dve, ("cv", 1))
            freed(V.tensor_copy(cv[:, 1, :], o[:, :]), ("cv", 1))
            for g in range(2):
                o = full(dve, ("cvT", g))
                oo = o[:, :].rearrange("p (h b g t) -> p h b g t", h=XH, b=4, g=XH)
                for h in range(XH):
                    V.tensor_copy(xoT[:, h, TP + 32 * g:TP + 32 * g + 32].rearrange("p (b t) -> p b t", b=4),
                                  oo[:, h, :, h, :]).then_inc(S("xoT_s"), 1)
                dve.wait_ge(S("xoT_s"), 4 * g + 4)
                dve.nop().then_inc(bank_free[PLAN[("cvT", g)][0]], 1)
            add_to_x("xo", "x_cross", in_turn)

            def split(tile, j):
                n = W_F1 + j % SLOTS
                count = tile // SLOTS + n // SLOTS + 1 if isinstance(tile, int) else tile[0] + (tile[1] // SLOTS + n // SLOTS + 1)
                number = tile if isinstance(tile, int) else tile[0] * SLOTS + tile[1]
                dve.wait_ge(slot_in[n % SLOTS], count * 16)
                if not (isinstance(number, int) and number < SPLITS):
                    dve.wait_ge(S("tile_done"), number - (SPLITS - 1))
                src = ring[:, n % SLOTS, :, :].rearrange("p k c -> p (k c)")
                V.tensor_copy(wr[:, j % SPLITS, 0, :], src).then_inc(S("w_high"), 1)
                dve.wait_ge(S("w_high"), number + 1)
                V.tensor_tensor(wr[:, j % SPLITS, 1, :], src, wr[:, j % SPLITS, 0, :], ALU.subtract).then_inc(
                    S("w_split"), 1)

            def hidden(half, i):
                for j in range(8):
                    split((i, half * MLP_TILES + j + 2) if not isinstance(i, int) else i * 8 + half * MLP_TILES + j + 2,
                          j + 2)
                    n = i * 8 + (half * (KF // 2) + j)
                    dve.wait_ge(S("u_high"), n + 1)
                    V.tensor_tensor(ur[:, 1, bass.ds(i * 8 + j, 1), :].rearrange("p a c -> p (a c)"), usq[:, j % 2, :],
                                    ur[:, 0, bass.ds(i * 8 + j, 1), :].rearrange("p a c -> p (a c)"),
                                    ALU.subtract).then_inc(S("u_low"), 1)

            def outputs(half, i, last=False):
                for j in range(4):
                    tile = half * MLP_TILES + KF // 2 + 2 * j + 2
                    if not (last and j == 3):
                        for e in range(2):
                            split((i, tile + e) if not isinstance(i, int) else i * 8 + tile + e, 2 * j + 2 + e)
                    for c in range(2):
                        if c == 0:
                            o = full(dve, ("f2", j, 0), i + half * MLP_FILLS, 1)
                        else:
                            dve.wait_ge(S("tile_done"), i * 8 + tile)
                            o = bank[PLAN[("f2", j, 1)][0]]
                        at_i = bass.ds(i * 4 + j, 1) if not isinstance(i, int) else slice(i * 4 + j, i * 4 + j + 1)
                        r = xT[:, at_i, c * HALF:(c + 1) * HALF].rearrange("p a c -> p (a c)")
                        freed(V.tensor_tensor(r, r, o[:, 0:HALF], ALU.add), ("f2", j, c))

            for _ in range(2):
                dve.nop().then_inc(S("u_low"), 1)
            split(0, 0)
            split(1, 1)
            scaled("ff", xT, hTk, G_FF, KD)
            for k in range(KD // 2, KD):
                dve.wait_ge(S("h_high"), k + 1)
                V.tensor_tensor(hr[:, 1, k, :], hTk[:, k, :], hr[:, 0, k, :], ALU.subtract).then_inc(S("h_low_last"), 1)
            for half in range(2):
                with dve.Fori(0, KF // 16) as i:
                    hidden(half, i)
                if half == 0:
                    with dve.Fori(0, KD // 4) as i:
                        outputs(half, i)
                else:
                    outputs(half, 0)
                    outputs(half, 1, last=True)
            for t in range(TILES):
                m = cols(t)[1]
                dve.wait_ge(S("y_turned"), 2 * t + 2)
                if t == 4:
                    dve.wait_ge(S("y_out0"), 32)
                V.tensor_copy(ytok[0:m, t % 4, 512:1024], bank[(2 * t + 1) % 8][0:m, :]).then_inc(S("ytok_right"), 1)

        @block.gpsimd
        def _(pool):
            G = nc.gpsimd
            link = Chain(pool, "pool_step")
            def rsqrt(out, v=None, scale=None, eps=EPS):
                if v is not None:
                    link(G.tensor_scalar(out, v, scale, eps, ALU.mult, ALU.add))
                shape = [out.shape[0], *out.shape[1:]]
                p = power
                while len(p.shape) < len(shape):
                    p = p.unsqueeze(1)
                return G.tensor_tensor(out, out, p.broadcast_to(shape), ALU.pow)

            pool.wait_ge(S("const_in"), 48)
            pool.wait_ge(S("ss_km"), 1)
            rsqrt(stat[:, 8:16], stat[:, 0:8], 1.0 / XD).then_inc(S("r_km"), 1)
            pool.wait_ge(S("km"), 1)
            pool.dma_start(mk_p.rearrange("l a (t p) h d -> p (l a t) (h d)", p=P), km_p).then_inc(S("mk_out"), 16)
            pool.wait_ge(S("vm"), 2)
            pool.dma_start(mv_p.rearrange("l a (t p) h d -> p (l a t) (h d)", p=P), vm_p[:, :, :]).then_inc(S("mv_out"), 16)
            G.memset(kv[64:P, 4, :], 0.0).then_inc(S("kv_pad"), 1)
            pool.wait_ge(S("kv_pad"), 1)
            pool.wait_ge(S("normed"), normed["mix"] + KD)
            G.memset(qz, 0.0).then_inc(S("pads2"), 1)
            G.memset(qi, 0.0).then_inc(S("pads2"), 1)
            pool.wait_ge(S("e_l"), 1)
            G.tensor_tensor(kl, zT[:, 2:4, :], dl, ALU.mult).then_inc(S("kl"), 1)
            pool.wait_ge(S("e_k"), 1)
            G.tensor_tensor(ek, zT[:, 2:4, :], ek, ALU.mult).then_inc(S("kd"), 1)
            pool.wait_ge(S("ss_kv"), 2)
            link(rsqrt(stat[:, 16:21], stat[:, 0:5], 1.0 / KR))
            link(rsqrt(stat[:, 21:26], stat[:, 5:10], 1.0 / ROPE))
            lat, kpe = kv[:, :, 0:KR], kv[:, :, KR:KR + ROPE]
            link(G.tensor_tensor(lat, lat, spread(stat[:, 16:21], 2, KR), ALU.mult))
            link(G.tensor_tensor(lat, lat, spread(row[:, R_KVA:R_KVA + KR], 1, TILES), ALU.mult))
            link(G.tensor_tensor(kpe, kpe, spread(stat[:, 21:26], 2, ROPE), ALU.mult))
            link(G.tensor_tensor(kpe, kpe, spread(row[:, R_KR:R_KR + ROPE], 1, TILES), ALU.mult))
            ktmp = [view(stat, 272 + 80 * n, TILES, 16) for n in range(4)]
            rotated(G, link, kpe, cosn, sinn, ktmp).then_inc(S("ckv"), 1)
            pool.wait_ge(S("sig_r"), 1)
            G.tensor_tensor(rs, rs, zT[:, 4:8, :], ALU.mult).then_inc(S("rs"), 1)
            pool.wait_ge(S("gla_state"), 16)
            pool.dma_start(gla_p[0, 0].rearrange("(q h) k v -> (h k) q v", q=2), st).then_inc(S("gla_out"), 16)
            pool.wait_ge(S("gla_state_s"), 4 * NB)
            pool.dma_start(gla_s[0].rearrange("b (q h) k v -> (h k) b q v", q=2), st_s).then_inc(S("gla_out"), 16)
            meet(pool, 1)
            for n, v in enumerate((qf[64:P, 4, :], stat[:, 192:232], qpd, kpnT, cknT)):
                if n == 4:
                    pool.wait_ge(S("gla_out"), 32)
                G.memset(v, 0.0).then_inc(S("pads"), 1)
                pool.wait_ge(S("pads"), n + 1)
            pool.wait_ge(S("ckv"), 1)
            link(G.memset(ckn[0:NS, KR:KR + 1], 1.0))
            link(G.tensor_copy(ckn[0:NS, 0:KR], kv[0:NS, 4, 0:KR]))
            for dst, c0, c1 in ((ckv_p, 0, KR), (kpe_p, KR, KR + ROPE)):
                pool.dma_start(dst.rearrange("l a (t p) c -> p (l a t) c", p=P), kv[:, 0:4, c0:c1]).then_inc(S("ckv_out"), 16)
            for dst, c0, c1 in ((ckv_s, 0, KR), (kpe_s, KR, KR + ROPE)):
                pool.dma_start(dst.rearrange("l b t c -> (l b t) c"), kv[0:NS, 4, c0:c1]).then_inc(S("ckv_out"), 16)
            G.tensor_copy(kfull.rearrange("p t (h c) -> p t h c", h=MH)[:, :, :, MV:MQ],
                          spread(kv[:, 0:4, KR:KR + ROPE], 2, MH)).then_inc(S("kfull"), 1)
            pool.wait_ge(S("ckv_out"), 64)
            meet(pool, 2)
            pool.wait_ge(S("wkvb_in"), 16)
            for k in range(KC):
                link(G.tensor_copy(wk_high[:, k, :].rearrange("p (h c) -> p h c", h=MH), w_k(k)))
                G.tensor_tensor(wk_low[:, k, :].rearrange("p (h c) -> p h c", h=MH), w_k(k),
                                wk_high[:, k, :].rearrange("p (h c) -> p h c", h=MH),
                                ALU.subtract).then_inc(S("wk_parts"), 1)
            meet(pool, 3)
            for v in cpg:
                G.memset(v[:, :, KR:KR + 1], 1.0).then_inc(S("page_one"), 1)

            def inverse_norms(b, g):
                pool.wait_ge(S("ss_pg"), b * NPG + (4 * g + 4))
                r = stat[:, 128 + 32 * (g % 2):160 + 32 * (g % 2)]
                s = stat[:, 64 + 32 * (g % 2):96 + 32 * (g % 2)]
                pool.wait_ge(S("sc_room"), b * 4 + (g + 1))
                G.tensor_tensor(r, s, epsk.broadcast_to([P, 32]), ALU.add).then_inc(S("ms_pg"), 1)
                pool.wait_ge(S("ms_pg"), b * 4 + (g + 1))
                G.tensor_tensor(r, r, power.broadcast_to([P, 32]), ALU.pow).then_inc(S("r_pg"), 1)

            with pool.Fori(0, NB) as b:
                for g in range(4):
                    inverse_norms(b, g)
            meet(pool, 4)
            for k in range(KD // 2):
                pool.wait_ge(S("h_high"), k + 1)
                G.tensor_tensor(hr[:, 1, k, :], hTk[:, k, :], hr[:, 0, k, :], ALU.subtract).then_inc(S("h_low_first"), 1)
            pool.wait_ge(S("y_out0"), 48)
            pool.wait_ge(S("y_out1"), 32)
            pool.wait_ge(S("mk_out"), 16)
            pool.wait_ge(S("mv_out"), 16)


def shape_constants():
    c = np.zeros((P, C_END), np.float32)
    i = np.arange(P)
    c[:, C_ID:C_ID + P] = np.eye(P)
    c[:, C_ONE:C_ONE + P] = 1.0
    c[:, C_TRI:C_TRI + P] = i[None, :] >= i[:, None]
    c[:, C_CAUS:C_CAUS + P] = np.where(i[None, :] <= i[:, None], 0.0, NEG)
    s = np.arange(NS)
    same = (s[None, :] // TS == s[:, None] // TS) & (s[None, :] >= s[:, None])
    c[:NS, C_SMASK:C_SMASK + NS] = same
    c[:NS, C_SNEG:C_SNEG + NS] = np.where(same, 0.0, NEG)
    c[:NS, C_SEQ:C_SEQ + NB] = s[:, None] // TS == np.arange(NB)[None, :]
    scan = np.ones(NT, np.float32)
    scan[0:TP:P] = 0.0
    scan[TP:NT:TS] = 0.0
    c[:, C_SCAN:C_SCAN + NT] = scan
    half = ROPE // 2
    inv = (10000.0 ** (-np.arange(half, dtype=np.float32) / half)).astype(np.float32)
    pos = np.zeros((P, TILES), np.float32)
    for t in range(4):
        pos[:, t] = t * P + i
    pos[:NS, 4] = PAST + s % TS
    ang = (pos[:, :, None] * inv[None, None, :]).astype(np.float32).astype(np.float64)
    c[:, C_ROPE:C_ROPE + 80] = np.cos(ang).reshape(P, 80)
    c[:, C_ROPE + 80:C_ROPE + 160] = np.sin(ang).reshape(P, 80)
    c[:, C_EPS] = EPS
    c[:, C_POW] = -0.5
    c[:, C_EPSK] = MV * EPS
    return c


def ring_layout(w_in, w_out, w_xq, w_xk, w_xv, w_xo, w_ff1, w_ff2):
    def tiles(w):
        k, n = w.shape
        return w.reshape(k // P, P, n // P, P).transpose(2, 1, 0, 3)

    out = np.zeros((W_END, P, KD, P), np.float32)
    out[W_XK:W_XK + 4] = tiles(w_xk)
    out[W_XV:W_XV + 4] = tiles(w_xv)
    out[W_QK:W_QK + 4] = tiles(w_in[:, 0:512])
    out[W_V:W_V + 4] = tiles(w_in[:, 512:1024])
    out[W_R:W_R + 4] = tiles(w_in[:, 1024:1536])
    out[W_KVA:W_KVA + 2] = tiles(w_in[:, 1936:2192])
    out[W_AKPE, :, :, 0:16] = w_in[:, 1536:1552].reshape(KD, P, 16).transpose(1, 0, 2)
    out[W_AKPE, :, :, 16:48] = w_in[:, 2192:2224].reshape(KD, P, 32).transpose(1, 0, 2)
    out[W_QA:W_QA + 3] = tiles(w_in[:, 1552:1936])
    out[W_OUT:W_OUT + KD] = tiles(w_out)
    out[W_XQ:W_XQ + 4] = tiles(w_xq)
    xo = tiles(w_xo)
    for j in range(KD):
        out[W_XO + j // 2, :, (j % 2) * 4:(j % 2) * 4 + 4, :] = xo[j]
    f1, f2 = tiles(w_ff1), tiles(w_ff2)
    for half in range(2):
        n = W_F1 + half * MLP_TILES
        out[n:n + KF // 2] = f1[half * (KF // 2):(half + 1) * (KF // 2)]
        for j in range(KD):
            for q in range(2):
                k0 = half * (KF // 2) + q * KD
                out[n + KF // 2 + 2 * j + q] = f2[j][:, k0:k0 + KD, :]
    return out.reshape(W_END, P, KD * P)


_OUTS = [(1, TP, D), (NB, TS, D), (1, 1, TP, KR), (1, 1, TP, ROPE), (1, 1, NM, XH, XD), (1, 1, NM, XH, XD),
         (1, 1, GH, DK, DV), (1, NB, TS, KR), (1, NB, TS, ROPE), (1, NB, GH, DK, DV)]


def kernel(x_prompt, x_sample, mem_prompt, cache_ckv, cache_kpe, cache_mem_k, cache_mem_v,
           state_gla, page_table, g_mix, w_in, w_gla_a2, b_gla_a, g_gla_o, g_mla_qa, w_mla_qb,
           g_mla_kva, w_mla_kvb, g_q_nope, g_k_nope, g_q_rope, g_k_rope, w_out, g_x, g_mem,
           w_xq, w_xk, w_xv, g_xq, g_xk, w_xo, g_ff, w_ff1, w_ff2):
    import concourse.bacc as bacc
    from concourse.bass_utils import run_bass_kernel_spmd

    def a(v):
        return np.ascontiguousarray(v)

    def by_partition(g):
        return a(g)[0].reshape(-1, P).T

    gains = np.concatenate([by_partition(g) for g in (g_mix, g_x, g_ff, g_mem, g_mla_qa, g_gla_o, g_xq, b_gla_a)],
                           axis=1)
    rows = np.concatenate([a(g) for g in (g_mla_kva, g_q_nope, g_k_nope, g_q_rope, g_k_rope, g_xk)], axis=1)
    ring = ring_layout(*(a(w)[0] for w in (w_in, w_out, w_xq, w_xk, w_xv, w_xo, w_ff1, w_ff2)))
    ins = {
        "x": a(x_prompt), "xs": a(x_sample), "mem": a(mem_prompt), "consts": shape_constants(), "gains": a(gains),
        "rows": a(rows), "ring_w": ring, "w_kvb": a(w_mla_kvb), "w_qb": a(w_mla_qb), "w_a2": a(w_gla_a2),
        "cache_ckv": a(cache_ckv), "cache_kpe": a(cache_kpe), "cache_mk": a(cache_mem_k), "cache_mv": a(cache_mem_v),
        "state": a(state_gla), "pages": a(page_table),
    }
    nc = bacc.Bacc("TRN2", target_bir_lowering=False, num_devices=1)
    args = [nc.dram_tensor(f"in_{n}_dram", v.shape, mybir.dt.from_np(v.dtype), kind="ExternalInput").ap()
            for n, v in ins.items()]
    args += [nc.dram_tensor(f"out_{i}_dram", s, F32, kind="ExternalOutput").ap() for i, s in enumerate(_OUTS)]
    build(nc, *args)
    r = run_bass_kernel_spmd(nc, [{f"in_{n}_dram": v for n, v in ins.items()}], core_ids=[0])
    return tuple(r.results[0][f"out_{i}_dram"] for i in range(len(_OUTS)))
```
